# Optimizing a Trainium2 kernel written in Bass

```python
import math
import jax, jax.numpy as jnp
from jax import lax
import numpy as np

'''Hybrid YOCO-style decoder trunk: mLSTM matrix-memory layers followed by
differential-attention layers that all read one shared K/V.

Inputs:
  x          (BATCH, SEQ, D_MODEL) float32 residual stream
  positions  (BATCH, SEQ) int32 token positions (rotary angles)
  parameters (stacked per layer type, see setup_inputs)
Output:
  (BATCH, SEQ, D_MODEL) float32

Per layer (sandwich norm):  x += post_norm(mixer(pre_norm(x)));
                            x += post_norm(sqrelu_mlp(pre_norm(x)))
Layers [0, N_A) use the mLSTM mixer; at the start of layer N_A one shared
rotary K (two key maps per head) and V are projected from rmsnorm(x); every
later layer uses a differential-attention mixer with its own queries.
'''

D_MODEL = 1024
BATCH = 1
SEQ = 512
DEPTH = 2

N_A_LAYERS = DEPTH // 2
N_B_LAYERS = DEPTH - N_A_LAYERS
D_FF = 4 * D_MODEL
NORM_EPS = 1e-6

M_HEADS = 4
M_V_DIM = D_MODEL // M_HEADS
M_QK_DIM = M_V_DIM // 2
M_CHUNK = 64
GATE_SOFTCAP = 15.0
M_QK_COLS = M_HEADS * M_QK_DIM
M_PROJ = 2 * M_QK_COLS + 2 * D_MODEL + 2 * M_HEADS

A_HEADS = 8
A_HEAD_DIM = D_MODEL // (2 * A_HEADS)
A_V_DIM = 2 * A_HEAD_DIM
Q_BLOCK = 128
ROPE_THETA = 10000.0

kernel_name = 'yoco_mlstm_diffattn_hybrid'

def rmsnorm(x, g):
    xf = x.astype(jnp.float32)
    y = xf * lax.rsqrt(jnp.mean(xf * xf, axis=-1, keepdims=True) + NORM_EPS)
    return (y * g.astype(jnp.float32)).astype(x.dtype)

def softcap(x, cap):
    return cap * jnp.tanh(x / cap)

def rope_tables(positions, dim):
    inv = 1.0 / (ROPE_THETA ** (jnp.arange(0, dim, 2, dtype=jnp.float32) / dim))
    ang = positions.astype(jnp.float32)[..., None] * inv
    return jnp.cos(ang), jnp.sin(ang)

def apply_rope(t, cos, sin):
    t1, t2 = jnp.split(t.astype(jnp.float32), 2, axis=-1)
    c = cos[:, :, None, :]
    s = sin[:, :, None, :]
    return jnp.concatenate([t1 * c - t2 * s, t2 * c + t1 * s], axis=-1).astype(t.dtype)

def sqrelu_mlp(h, w_up, w_down):
    u = jax.nn.relu(h @ w_up)
    return (u * u) @ w_down

def mlstm_mixer(h, w_in, b_gates, g_head, w_out):
    B, S, _ = h.shape
    L = M_CHUNK
    nc = S // L
    proj = h @ w_in
    cuts = [M_QK_COLS, 2 * M_QK_COLS, 2 * M_QK_COLS + D_MODEL, 2 * M_QK_COLS + 2 * D_MODEL]
    q, k, v, o, gts = jnp.split(proj, cuts, axis=-1)
    gts = softcap((gts + b_gates).astype(jnp.float32), GATE_SOFTCAP)
    log_i = gts[..., :M_HEADS]
    log_f = jax.nn.log_sigmoid(gts[..., M_HEADS:])

    def to_chunks(t, dh):
        return t.astype(jnp.float32).reshape(B, nc, L, M_HEADS, dh).transpose(1, 0, 3, 2, 4)

    def gate_chunks(t):
        return t.reshape(B, nc, L, M_HEADS).transpose(1, 0, 3, 2)

    qc = to_chunks(q, M_QK_DIM)
    kc = to_chunks(k, M_QK_DIM) * (M_QK_DIM ** -0.5)
    vc = to_chunks(v, M_V_DIM)
    ic = gate_chunks(log_i)
    fc = gate_chunks(log_f)
    causal = jnp.tril(jnp.ones((L, L), dtype=bool))

    def step(carry, xs):
        C, n, m = carry
        q_, k_, v_, li, lf = xs
        b = jnp.cumsum(lf, axis=-1)
        dmat = b[..., :, None] - b[..., None, :] + li[..., None, :]
        dmat = jnp.where(causal, dmat, -jnp.inf)
        inter = b + m[..., None]
        m_row = jnp.maximum(inter, jnp.max(dmat, axis=-1))
        w_intra = jnp.exp(dmat - m_row[..., None])
        s_inter = jnp.exp(inter - m_row)
        s_qk = jnp.einsum('bhjd,bhsd->bhjs', q_, k_) * w_intra
        num = (s_inter[..., None] * jnp.einsum('bhjd,bhde->bhje', q_, C)
               + jnp.einsum('bhjs,bhse->bhje', s_qk, v_))
        den = s_inter * jnp.einsum('bhjd,bhd->bhj', q_, n) + jnp.sum(s_qk, axis=-1)
        h_out = num / jnp.maximum(jnp.abs(den), jnp.exp(-m_row))[..., None]
        b_last = b[..., -1]
        g_s = b_last[..., None] - b + li
        m_new = jnp.maximum(b_last + m, jnp.max(g_s, axis=-1))
        decay = jnp.exp(b_last + m - m_new)
        w_s = jnp.exp(g_s - m_new[..., None])
        C_new = decay[..., None, None] * C + jnp.einsum('bhs,bhsd,bhse->bhde', w_s, k_, v_)
        n_new = decay[..., None] * n + jnp.einsum('bhs,bhsd->bhd', w_s, k_)
        return (C_new, n_new, m_new), h_out

    init = (jnp.zeros((B, M_HEADS, M_QK_DIM, M_V_DIM), jnp.float32),
            jnp.zeros((B, M_HEADS, M_QK_DIM), jnp.float32),
            jnp.zeros((B, M_HEADS), jnp.float32))
    _, hs = lax.scan(step, init, (qc, kc, vc, ic, fc))
    hs = hs.transpose(1, 0, 3, 2, 4).reshape(B, S, M_HEADS, M_V_DIM)
    hs = rmsnorm(hs, g_head.reshape(M_HEADS, M_V_DIM))
    og = jax.nn.sigmoid(o.astype(jnp.float32)).reshape(B, S, M_HEADS, M_V_DIM)
    y = (og * hs).reshape(B, S, D_MODEL).astype(h.dtype)
    return y @ w_out

def shared_kv(x, kv_norm_g, w_kv, cos, sin):
    B, S, _ = x.shape
    kv = rmsnorm(x, kv_norm_g) @ w_kv
    k = kv[..., :D_MODEL].reshape(B, S, 2 * A_HEADS, A_HEAD_DIM)
    k = apply_rope(k, cos, sin).reshape(B, S, A_HEADS, 2, A_HEAD_DIM)
    v = kv[..., D_MODEL:].reshape(B, S, A_HEADS, A_V_DIM)
    return k, v

def diff_attention(h, w_q, lam, g_head, w_out, k_sh, v_sh, cos, sin, lam_init):
    B, S, _ = h.shape
    nb = S // Q_BLOCK
    q = (h @ w_q).reshape(B, S, 2 * A_HEADS, A_HEAD_DIM)
    q = apply_rope(q, cos, sin) * (A_HEAD_DIM ** -0.5)
    q = q.reshape(B, nb, Q_BLOCK, A_HEADS, 2, A_HEAD_DIM).transpose(1, 0, 2, 3, 4, 5)
    lamf = lam.astype(jnp.float32)
    lam_full = (jnp.exp(jnp.sum(lamf[0] * lamf[1])) - jnp.exp(jnp.sum(lamf[2] * lamf[3]))
                + lam_init)
    k_idx = jnp.arange(S)

    def block(args):
        qi, bi = args
        scores = jnp.einsum('bqhcd,bkhcd->bhcqk', qi, k_sh).astype(jnp.float32)
        q_idx = bi * Q_BLOCK + jnp.arange(Q_BLOCK)
        mask = k_idx[None, :] <= q_idx[:, None]
        scores = jnp.where(mask, scores, -jnp.inf)
        p = jax.nn.softmax(scores, axis=-1)
        pd = p[:, :, 0] - lam_full * p[:, :, 1]
        return jnp.einsum('bhqk,bkhe->bqhe', pd.astype(v_sh.dtype), v_sh)

    o = lax.map(block, (q, jnp.arange(nb)))
    o = o.transpose(1, 0, 2, 3, 4).reshape(B, S, A_HEADS, A_V_DIM)
    o = rmsnorm(o, g_head.reshape(A_HEADS, A_V_DIM)) * (1.0 - lam_init)
    return o.reshape(B, S, D_MODEL) @ w_out

def setup_inputs(seed: int = 0) -> dict:
    key = jax.random.key(seed)
    ks = jax.random.split(key, 16)
    f32 = jnp.float32
    nrm = jax.random.normal
    x = nrm(ks[0], (BATCH, SEQ, D_MODEL), f32)
    positions = jnp.broadcast_to(jnp.arange(SEQ, dtype=jnp.int32)[None, :], (BATCH, SEQ))
    norm_g = 1.0 + 0.02 * nrm(ks[1], (DEPTH, 4, D_MODEL), f32)
    a_w_in = nrm(ks[2], (N_A_LAYERS, D_MODEL, M_PROJ), f32) * D_MODEL ** -0.5
    ig_b = 0.1 * nrm(ks[3], (N_A_LAYERS, M_HEADS), f32)
    fg_b = jnp.linspace(3.0, 6.0, M_HEADS, dtype=f32)[None, :] + 0.1 * nrm(ks[4], (N_A_LAYERS, M_HEADS), f32)
    a_b_gates = jnp.concatenate([ig_b, fg_b], axis=-1)
    a_g_head = 1.0 + 0.02 * nrm(ks[5], (N_A_LAYERS, D_MODEL), f32)
    a_w_out = nrm(ks[6], (N_A_LAYERS, D_MODEL, D_MODEL), f32) * D_MODEL ** -0.5
    kv_norm_g = 1.0 + 0.02 * nrm(ks[7], (D_MODEL,), f32)
    w_kv = nrm(ks[8], (D_MODEL, 2 * D_MODEL), f32) * D_MODEL ** -0.5
    b_w_q = nrm(ks[9], (N_B_LAYERS, D_MODEL, D_MODEL), f32) * D_MODEL ** -0.5
    b_lam = 0.1 * nrm(ks[10], (N_B_LAYERS, 4, A_HEAD_DIM), f32)
    b_g_head = 1.0 + 0.02 * nrm(ks[11], (N_B_LAYERS, D_MODEL), f32)
    b_w_out = nrm(ks[12], (N_B_LAYERS, D_MODEL, D_MODEL), f32) * D_MODEL ** -0.5
    mlp_w_up = nrm(ks[13], (DEPTH, D_MODEL, D_FF), f32) * D_MODEL ** -0.5
    mlp_w_down = nrm(ks[14], (DEPTH, D_FF, D_MODEL), f32) * D_FF ** -0.5
    return {'x': x, 'positions': positions, 'norm_g': norm_g,
            'a_w_in': a_w_in, 'a_b_gates': a_b_gates, 'a_g_head': a_g_head, 'a_w_out': a_w_out,
            'kv_norm_g': kv_norm_g, 'w_kv': w_kv,
            'b_w_q': b_w_q, 'b_lam': b_lam, 'b_g_head': b_g_head, 'b_w_out': b_w_out,
            'mlp_w_up': mlp_w_up, 'mlp_w_down': mlp_w_down}

def reference(x, positions, norm_g, a_w_in, a_b_gates, a_g_head, a_w_out,
              kv_norm_g, w_kv, b_w_q, b_lam, b_g_head, b_w_out, mlp_w_up, mlp_w_down):
    cos, sin = rope_tables(positions, A_HEAD_DIM)
    k_sh = None
    v_sh = None
    for layer in range(DEPTH):
        g = norm_g[layer]
        if layer < N_A_LAYERS:
            y = mlstm_mixer(rmsnorm(x, g[0]), a_w_in[layer], a_b_gates[layer],
                            a_g_head[layer], a_w_out[layer])
        else:
            j = layer - N_A_LAYERS
            if j == 0:
                k_sh, v_sh = shared_kv(x, kv_norm_g, w_kv, cos, sin)
            lam_init = 0.8 - 0.6 * math.exp(-0.3 * layer)
            y = diff_attention(rmsnorm(x, g[0]), b_w_q[j], b_lam[j], b_g_head[j], b_w_out[j],
                               k_sh, v_sh, cos, sin, lam_init)
        x = x + rmsnorm(y, g[1])
        x = x + rmsnorm(sqrelu_mlp(rmsnorm(x, g[2]), mlp_w_up[layer], mlp_w_down[layer]), g[3])
    return x


_drawn_inputs = setup_inputs


def setup_inputs(seed=0):
    import zlib

    import numpy as np

    out = dict(_drawn_inputs(seed))
    spreads = {}
    factors = {'a_g_head': 3.498, 'kv_norm_g': 4.651, 'b_g_head': 5.397}
    for name, (base, spread) in spreads.items():
        noise = np.random.default_rng([zlib.crc32(name.encode()), seed]).standard_normal(out[name].shape)
        drawn = base * np.exp(spread * noise) if base else spread * noise
        out[name] = __import__('jax').numpy.asarray(drawn.astype(out[name].dtype))
    for name, factor in factors.items():
        out[name] = (out[name] * factor).astype(out[name].dtype)
    return out
```

```python
import math
from contextlib import ExitStack

import numpy as np

import concourse.bass as bass
from concourse import mybir

F32 = mybir.dt.float32
F32R = mybir.dt.float32r
I32 = mybir.dt.int32
ALU = mybir.AluOpType
ACT = mybir.ActivationFunctionType
AX = mybir.AxisListType

P = 128
SEQ, D_MODEL, D_FF = 512, 1024, 4096
T = SEQ // P
C = D_MODEL // P
COLS = 512
UC = 4
EPS = 1e-6
MASKED = -1e30

M_HEADS, M_V, M_QK = 4, 256, 128
CAP = 15.0
VW = M_V + 2
BLK = T * (T + 1) // 2
A_HEADS, A_DIM = 8, 64
HALF = A_DIM // 2
LAM_INIT = 0.8 - 0.6 * math.exp(-0.3)

U_QK, U_V, U_O, U_OUT, U_UP, U_DOWN = 0, 4, 8, 12, 16, 32
U_Q2, U_K2, U_V2, U_OUT2, U_UP2, U_DOWN2, UNITS = 48, 52, 56, 60, 64, 80, 96
G_QK, G_V, G_O, G_OUT, G_UP, G_DOWN = 0, 2, 4, 6, 8, 16
G_Q2, G_K2, G_V2, G_OUT2, G_UP2, G_DOWN2 = 18, 20, 22, 24, 26, 34
UPG = D_FF // COLS
DU = 16
KU = D_FF // (UC * P)
TURN_X0, TURN_YM, TURN_X1, TURN_X2, TURN_YA, TURN_X3 = range(6)
SET_X0, SET_YM, SET_X1, SET_Q, SET_KV, SET_YA, SET_X3 = range(7)
GC_AHEAD, GC_KV, GC_BHEAD = 64, 72, 80
GROWS = 88
KSTART = (0, 512, 1024, 896)
TWO_PI = (6.28125, 0.0019340515136718750, 1.2554228305816650390625e-06, 2.1219957914e-11)


def trunk(nc, x, positions, norm_g, a_w_in, a_b_gates, a_g_head, a_w_out, kv_norm_g, w_kv, b_w_q,
          b_lam, b_g_head, b_w_out, mlp_w_up, mlp_w_down, inv_freq, out):
    def chunks(w):
        return w.rearrange("(c p) n -> p c n", p=P)

    w_in, w_out = chunks(a_w_in[0]), chunks(a_w_out[0])
    w_q2, w_kv2, w_out2 = chunks(b_w_q[0]), chunks(w_kv), chunks(b_w_out[0])
    w_up = [chunks(mlp_w_up[n]) for n in range(2)]
    w_down = [chunks(mlp_w_down[n]) for n in range(2)]
    x_rows = x[0].rearrange("(t p) d -> t p d", p=P)
    out_rows = out[0].rearrange("(t p) d -> t p d", p=P)

    with ExitStack() as ctx:
        base = nc.sbuf_base
        at = [(base + 63) // 64 * 64]

        def place(name, shape, dtype, offset=None):
            size = int(np.prod(shape[1:])) * 4
            if offset is None:
                offset = at[0]
                at[0] += (size + 31) // 32 * 32
            return nc.alloc_sbuf_tensor_at(name, shape, dtype, offset=offset)

        def sem(name):
            return ctx.enter_context(nc.semaphore(name))

        x_sb = place("x_sb", [P, T, D_MODEL], F32)
        wraw = place("wraw", [P, 2, UC, COLS], F32)
        whi = place("whi", [P, 2, UC, COLS], F32R)
        wlo = place("wlo", [P, 2, UC, COLS], F32R)
        KB = 1024
        ra = at[0]
        at[0] += 32 * KB
        act_hi = place("act_hi", [P, C, SEQ], F32R, ra)
        act_lo = place("act_lo", [P, C, SEQ], F32R, ra + 16 * KB)
        decay = place("decay", [P, 2, BLK * P], F32, ra)
        p_hi = place("p_hi", [P, 2, BLK * P], F32R, ra + 10 * KB)
        p_lo = place("p_lo", [P, 2, BLK * P], F32R, ra + 20 * KB)
        o_nat = place("o_nat", [P, T, D_MODEL], F32, ra)
        probs = place("probs", [P, 2, 2, SEQ], F32, ra + 16 * KB)
        pt_hi = place("pt_hi", [P, 2, SEQ], F32R, ra + 24 * KB)
        pt_lo = place("pt_lo", [P, 2, SEQ], F32R, ra + 28 * KB)
        ru = at[0]
        at[0] += 65 * KB
        u_sq = place("u_sq", [P, D_FF // P, SEQ], F32, ru)
        mq_hi = place("mq_hi", [P, M_HEADS, SEQ], F32R, ru)
        mq_lo = place("mq_lo", [P, M_HEADS, SEQ], F32R, ru + 8 * KB)
        mk_hi = place("mk_hi", [P, M_HEADS, SEQ], F32R, ru + 16 * KB)
        mk_lo = place("mk_lo", [P, M_HEADS, SEQ], F32R, ru + 24 * KB)
        mv_hi = place("mv_hi", [P, T, M_HEADS, VW], F32R, ru + 32 * KB)
        mv_lo_at = ru + 32 * KB + T * M_HEADS * VW * 4
        mv_end = mv_lo_at + T * M_HEADS * VW * 4
        mv_lo = place("mv_lo", [P, T, M_HEADS, VW], F32R, mv_lo_at)
        q_hi = place("q_hi", [P, A_HEADS, SEQ], F32R, ru)
        q_lo = place("q_lo", [P, A_HEADS, SEQ], F32R, ru + 16 * KB)
        k_hi = place("k_hi", [P, A_HEADS, SEQ], F32R, ru + 32 * KB)
        k_lo = place("k_lo", [P, A_HEADS, SEQ], F32R, ru + 48 * KB)
        xq_hi = place("xq_hi", [P, C, SEQ], F32R, ru + 32 * KB)
        xq_lo = place("xq_lo", [P, C, SEQ], F32R, ru + 48 * KB)
        re = at[0]
        at[0] += 32 * KB
        y_nat = place("y_nat", [P, T, D_MODEL], F32, re)
        rg = re + 16 * KB
        g_raw = place("g_raw", [2 * M_HEADS, SEQ], F32, rg)
        f_raw = place("f_raw", [M_HEADS, SEQ], F32, rg + 2 * KB)
        sp_row = place("sp_row", [M_HEADS, SEQ], F32, rg + 4 * KB)
        b_row = place("b_row", [M_HEADS, SEQ], F32, rg + 6 * KB)
        m_row = place("m_row", [M_HEADS, SEQ], F32, rg + 8 * KB)
        a_row = place("a_row", [M_HEADS, SEQ], F32, rg + 10 * KB)
        e_row = place("e_row", [M_HEADS, SEQ], F32, rg + 12 * KB)
        junk_m = place("junk_m", [P, M_V], F32, rg + 10 * KB)
        r_row = place("r_row", [M_HEADS, BLK * P], F32, re)
        r_hi = place("r_hi", [M_HEADS, BLK * P], F32R, rg)
        r_lo = place("r_lo", [M_HEADS, BLK * P], F32R, rg + 5 * KB)
        sel = place("sel", [M_HEADS, M_HEADS, P], F32, rg + 14 * KB)
        v_hi = place("v_hi", [P, T, D_MODEL], F32R, re)
        v_lo = place("v_lo", [P, T, D_MODEL], F32R, re + 16 * KB)
        roped = place("roped", [P, T, COLS], F32, re)
        relu_t = place("relu_t", [P, 2, COLS], F32, re)
        tmp = place("tmp", [P, 2, D_MODEL], F32, re + 4 * KB)
        gpost = place("gpost", [P, D_MODEL], F32)
        rs = at[0]
        at[0] += 4 * KB
        scr_a = place("scr_a", [P, COLS], F32, rs)
        scr_b = place("scr_b", [P, COLS], F32, rs + 2 * KB)
        pdiff = place("pdiff", [P, 2, SEQ], F32, rs)
        lam_in = place("lam_in", [P, 4, A_DIM], F32, rs)
        lam_pr = place("lam_pr", [P, 2, A_DIM], F32, rs + 1 * KB)
        ang = place("ang", [P, 2, T, HALF], F32, rs + 2 * KB)
        turns = place("turns", [P, 2, T, HALF], F32, rs + 3 * KB)
        rj = at[0]
        junk = place("junk", [P, COLS], F32)
        sel_r = place("sel_r", [M_HEADS, M_HEADS, P], F32R, rj)
        ident = place("ident", [P, P], F32)
        ident_r = place("ident_r", [P, P], F32R)
        mask_st = place("mask_st", [P, P], F32R)
        mask_ts = place("mask_ts", [P, P], F32R)
        grows = place("grows", [GROWS, P], F32, mv_end)
        gcols = place("gcols", [P, GROWS], F32)
        wg_raw = place("wg_raw", [P, C, 8], F32, mv_lo_at)
        wg_hi = place("wg_hi", [P, C, 8], F32R, mv_lo_at + 256)
        wg_lo = place("wg_lo", [P, C, 8], F32R, mv_lo_at + 512)
        gate_b = place("gate_b", [8, 1], F32, mv_lo_at + 768)
        gate_b15 = place("gate_b15", [8, 1], F32, mv_lo_at + 800)
        pos_i = place("pos_i", [P, T], I32)
        pos_f = place("pos_f", [P, T], F32)
        inv = place("inv", [P, HALF], F32)
        trig = place("trig", [P, 2, T, HALF], F32)
        lam_s = place("lam_s", [P, 2], F32)
        lam_e = place("lam_e", [P, 2], F32)
        lam2 = place("lam2", [P, 2], F32)
        ssq = place("ssq", [P, T, 2], F32)
        bias0 = place("bias0", [P, T], F32)
        rms = place("rms", [P, T], F32)
        fac = place("fac", [P, T], F32)
        ssx = place("ssx", [P, T], F32)
        rmsx = place("rmsx", [P, T], F32)
        rx = place("rx", [P, T], F32)
        rx2 = place("rx2", [P, T], F32)
        rx4 = place("rx4", [P, T], F32)
        dcum = place("dcum", [M_HEADS, T, T], F32)
        carry = place("carry", [M_HEADS, T], F32)
        acol = place("acol", [P, 2 * T, M_HEADS], F32)
        den = place("den", [P, T, M_HEADS], F32)
        den2 = place("den2", [P, T, M_HEADS], F32)
        mss = place("mss", [P, T, M_HEADS], F32)
        mfac = place("mfac", [P, T, M_HEADS], F32)
        smax = place("smax", [P, 2, 2], F32)
        nmax = place("nmax", [P, 2, 2], F32)
        lsum = place("lsum", [P, 2, 2], F32)
        linv = place("linv", [P, 2, 2], F32)
        oss = place("oss", [P, T, A_HEADS], F32)
        orms = place("orms", [P, T, A_HEADS], F32)
        epsc = place("epsc", [P, 1], F32)
        assert at[0] <= nc.sbuf_usable_end, at[0]

        ps = ctx.enter_context(nc.psum_tensor("ps", [P, 8, COLS], F32))

        x_in = [sem(f"x_in{t}") for t in range(T)]
        grows_in, gate_in, pos_in, lam_in_s = (sem(n) for n in ("grows_in", "gate_in", "pos_in", "lam_in"))
        gpost_in = sem("gpost_in")
        raw_loaded = [sem(f"raw_loaded{s}") for s in range(2)]
        whi_ready, weights_ready, unit_used = sem("whi_ready"), sem("weights_ready"), sem("unit_used")
        bank_done = sem("bank_done")
        consts_ready, gcols_turned, gcols_ready = sem("consts_ready"), sem("gcols_turned"), sem("gcols_ready")
        consts_r_ready = sem("consts_r_ready")
        nat_ready, turned = sem("nat_ready"), sem("turned")
        acts_hi, acts_ready = sem("acts_hi"), sem("acts_ready")
        act_self, dve_self = sem("act_self"), sem("dve_self")
        sq0, rms_ready, gpost_used = sem("sq0"), sem("rms_ready"), sem("gpost_used")
        bias0_ready = sem("bias0_ready")
        rmsx_ready, rx_ready = sem("rmsx_ready"), sem("rx_ready")
        gw_hi, gw_ready, gates_done = sem("gw_hi"), sem("gw_ready"), sem("gates_done")
        tanh_ready, f_rows_in = sem("tanh_ready"), sem("f_rows_in")
        sp_ready, mneg_ready, e_ready = sem("sp_ready"), sem("mneg_ready"), sem("e_ready")
        rows_ready, r_hi_ready = sem("rows_ready"), sem("r_hi_ready")
        acol_turned, acol_ready = sem("acol_turned"), sem("acol_ready")
        m_hi, m_evac = sem("m_hi"), sem("m_evac")
        ones_ready = sem("ones_ready")
        sig_ready = sem("sig_ready")
        bcast_done, decay_ready, s_done = sem("bcast_done"), sem("decay_ready"), sem("s_done")
        p_ready, p_hi_ready, p_lo_ready = sem("p_ready"), sem("p_hi_ready"), sem("p_lo_ready")
        av_done, av_sq, av_evac = sem("av_done"), sem("av_sq"), sem("av_evac")
        mvar_ready, mstd_ready = sem("mvar_ready"), sem("mstd_ready")
        relu_ready, up_evac = sem("relu_ready"), sem("up_evac")
        down_hi, down_ready = sem("down_hi"), sem("down_ready")
        ang_ready, trig_ready = sem("ang_ready"), sem("trig_ready")
        lams_ready, lame_ready = sem("lams_ready"), sem("lame_ready")
        rope_ready, rope_turned, qk_hi, qk_ready = sem("rope_ready"), sem("rope_turned"), sem("qk_hi"), sem("qk_ready")
        v_hi_s, v_ready = sem("v_hi_s"), sem("v_ready")
        scores_done, max_ready, exp_ready = sem("scores_done"), sem("max_ready"), sem("exp_ready")
        diff_ready, pt_done, pt_hi_s, pt_ready = sem("diff_ready"), sem("pt_done"), sem("pt_hi_s"), sem("pt_ready")
        o_done, o_copied, ovar_ready, ostd_ready = sem("o_done"), sem("o_copied"), sem("ovar_ready"), sem("ostd_ready")
        o_squared = sem("o_squared")
        stored = sem("stored")

        def wait_bank(eng, G, b):
            if b < 3:
                eng.wait_ge(bank_done, 3 * G + b + 1)
            elif G < G_DOWN:
                eng.wait_ge(unit_used, 2 * G + 2)
            elif G < G_Q2:
                eng.wait_ge(unit_used, U_DOWN + KU * (G - G_DOWN + 1))
            elif G < G_DOWN2:
                eng.wait_ge(unit_used, U_Q2 + 2 * (G - G_Q2) + 2)
            else:
                eng.wait_ge(unit_used, U_DOWN2 + KU * (G - G_DOWN2 + 1))

        block = ctx.enter_context(nc.Block())

        @block.sync
        def _(sp):
            def load(u, s, src):
                if not (isinstance(u, int) and u < 2):
                    sp.wait_ge(weights_ready, u - 1)
                sp.dma_start(wraw[:, s], src).then_inc(raw_loaded[s], 16)

            def short_stage(u0, w, col0, groups):
                for g in range(groups):
                    for s in range(2):
                        load(u0 + 2 * g + s, s, w[:, UC * s:UC * s + UC, col0 + g * COLS:col0 + (g + 1) * COLS])

            def mlp(u_up, u_down, w1, w2):
                with sp.Fori(0, UPG) as g:
                    for s in range(2):
                        load(g * 2 + (u_up + s), s, w1[:, UC * s:UC * s + UC, bass.ds(g * COLS, COLS)])
                for n in range(2):
                    with sp.Fori(0, KU // 2) as j:
                        for s in range(2):
                            load(j * 2 + (u_down + KU * n + s), s,
                                 w2[:, bass.ds(j * (2 * UC) + UC * s, UC), n * COLS:(n + 1) * COLS])

            def load_gpost(n, layer, i):
                if n:
                    sp.wait_ge(gpost_used, n * T)
                sp.dma_start(gpost[:], norm_g[layer, i:i + 1, :].to_broadcast([P, D_MODEL])).then_inc(gpost_in, 16)

            for t in range(T):
                sp.dma_start(x_sb[:, t], x_rows[t]).then_inc(x_in[t], 16)
            sp.dma_start(grows[0:64, :], norm_g.rearrange("l i (c p) -> (l i c) p", p=P)).then_inc(grows_in, 16)
            sp.dma_start(grows[64:72, :], a_g_head.rearrange("l (c p) -> (l c) p", p=P)).then_inc(grows_in, 16)
            sp.dma_start(grows[72:80, :], kv_norm_g.rearrange("(c p) -> c p", p=P)).then_inc(grows_in, 16)
            sp.dma_start(grows[80:88, :], b_g_head.rearrange("l (c p) -> (l c) p", p=P)).then_inc(grows_in, 16)
            short_stage(U_QK, w_in, 0, 1)
            sp.dma_start(wg_raw[:], w_in[:, :, 3 * D_MODEL:3 * D_MODEL + 8]).then_inc(gate_in, 16)
            sp.dma_start(gate_b[:], a_b_gates.rearrange("l g -> g l")).then_inc(gate_in, 16)
            load_gpost(0, 0, 1)
            sp.dma_start(pos_i[:], positions[0].rearrange("(t p) -> p t", p=P), allow_slow_non_contiguous=True).then_inc(pos_in, 16)
            sp.dma_start(inv[:], inv_freq.to_broadcast([P, HALF])).then_inc(pos_in, 16)
            short_stage(U_QK + 2, w_in, COLS, 1)
            sp.wait_ge(tanh_ready, 1)
            sp.dma_start(f_raw[:], g_raw[M_HEADS:2 * M_HEADS, :]).then_inc(f_rows_in, 16)
            short_stage(U_V, w_in, D_MODEL, 4)
            short_stage(U_OUT, w_out, 0, 2)
            mlp(U_UP, U_DOWN, w_up[0], w_down[0])
            load_gpost(1, 0, 3)
            sp.dma_start(lam_in[:], b_lam.rearrange("l a d -> l (a d)").to_broadcast([P, 4 * A_DIM])).then_inc(lam_in_s, 16)
            short_stage(U_Q2, w_q2, 0, 2)
            load_gpost(2, 1, 1)
            short_stage(U_K2, w_kv2, 0, 4)
            short_stage(U_OUT2, w_out2, 0, 2)
            mlp(U_UP2, U_DOWN2, w_up[1], w_down[1])
            load_gpost(3, 1, 3)
            for t in range(T):
                sp.wait_ge(nat_ready, 6 * T + t + 1)
                sp.dma_start(out_rows[t], x_sb[:, t]).then_inc(stored, 16)
            sp.wait_ge(stored, 16 * T)

        @block.gpsimd
        def _(pool):
            g = nc.gpsimd
            g.memset(ident[:], 0.0).then_inc(consts_ready, 1)
            pool.wait_ge(consts_ready, 1)
            g.affine_select(out=ident[:], in_=ident[:], compare_op=ALU.not_equal, fill=1.0, base=0,
                            pattern=[[-1, P]], channel_multiplier=1).then_inc(consts_ready, 1)
            g.memset(sel[:], 0.0).then_inc(consts_ready, 1)
            pool.wait_ge(consts_ready, 3)
            g.affine_select(out=sel[:], in_=sel[:], compare_op=ALU.not_equal, fill=1.0, base=0,
                            pattern=[[-1, M_HEADS], [0, P]], channel_multiplier=1).then_inc(consts_ready, 1)
            g.memset(scr_a[:, 0:2 * P], 0.0).then_inc(consts_ready, 1)
            pool.wait_ge(consts_ready, 5)
            g.affine_select(out=scr_a[:, 0:P], in_=scr_a[:, 0:P], compare_op=ALU.is_ge, fill=MASKED, base=0,
                            pattern=[[1, P]], channel_multiplier=-1).then_inc(consts_ready, 1)
            g.affine_select(out=scr_a[:, P:2 * P], in_=scr_a[:, P:2 * P], compare_op=ALU.is_ge, fill=MASKED, base=0,
                            pattern=[[-1, P]], channel_multiplier=1).then_inc(consts_ready, 1)

            def lo_part(u, s):
                pool.wait_ge(whi_ready, u + 1)
                g.tensor_tensor(wlo[:, s], wraw[:, s], whi[:, s].bitcast(F32), ALU.subtract).then_inc(weights_ready, 1)

            with pool.Fori(0, UNITS // 2) as j:
                for s in range(2):
                    lo_part(j * 2 + s, s)

        @block.scalar
        def _(act):
            a = nc.scalar
            own = [0]

            def done(ins):
                own[0] += 1
                ins.then_inc(act_self, 1)
                act.wait_ge(act_self, own[0])

            def w_hi(u, s):
                if isinstance(u, int):
                    if u >= UNITS:
                        return
                    act.wait_ge(raw_loaded[s], 16 * (u // 2 + 1))
                    if u >= 2:
                        act.wait_ge(unit_used, u - 1)
                a.activation(whi[:, s], wraw[:, s], ACT.Copy).then_inc(whi_ready, 1)

            def w_hi_at(j, u0, s):
                act.wait_ge(raw_loaded[s], j * 16 + 16 * (u0 // 2 + 1))
                act.wait_ge(unit_used, j * 2 + (u0 + s - 1))
                a.activation(whi[:, s], wraw[:, s], ACT.Copy).then_inc(whi_ready, 1)

            def turned_chunk(c):
                return ps[:, T * (c % 2):T * (c % 2) + T, P * (c // 2):P * (c // 2) + P]

            def acts_out(turn, n, c, gc, dst):
                if c == 0:
                    act.wait_ge(turned, T * turn + T)
                if c >= 2 or gc == GC_KV or (gc == 8 * 4 and c):
                    act.wait_ge(acts_ready, n - 1)
                a.activation(dst[:, c].rearrange("p (t k) -> p t k", t=T), turned_chunk(c), ACT.Copy,
                             scale=gcols[:, gc + c:gc + c + 1]).then_inc(acts_hi, 1)

            def x_squares(t, first):
                if first:
                    act.wait_ge(x_in[t], 16)
                done(a.activation(y_nat[:, t] if first else tmp[:, 0], x_sb[:, t], ACT.Square, accum_out=ssx[:, t:t + 1]))
                a.activation(rmsx[:, t:t + 1], ssx[:, t:t + 1], ACT.Sqrt, scale=1.0 / D_MODEL,
                             bias=epsc[:, 0:1]).then_inc(rmsx_ready, 1)

            def post_norm(n, G, mlp):
                for t in range(T):
                    wait_bank(act, G + 1, t)
                    done(a.activation(junk[:], ps[:, 4 + t], ACT.Square, accum_out=ssq[:, t, 1:2]))
                    act.wait_ge(bias0_ready, T * n + t + 1)
                    a.activation(rms[:, t:t + 1], ssq[:, t, 1:2], ACT.Sqrt,
                                 scale=rx4[:, t:t + 1] if mlp else 1.0 / D_MODEL,
                                 bias=bias0[:, t:t + 1]).then_inc(rms_ready, 1)

            def first_squares(n, G):
                for t in range(T):
                    wait_bank(act, G, t)
                    own[0] += 1
                    a.activation(junk[:], ps[:, t], ACT.Square, accum_out=ssq[:, t, 0:1]).then_inc(act_self, 1)
                    act.wait_ge(act_self, own[0])
                    a.copy(ssq[:, t, 1:2], ssq[:, t, 0:1]).then_inc(sq0, 1)

            def x_stats(turn):
                for t in range(T):
                    act.wait_ge(nat_ready, T * turn + t + 1)
                    x_squares(t, False)

            act.wait_ge(gcols_ready, 1)
            for t in range(T):
                x_squares(t, True)
            w_hi(0, 0)
            act.wait_ge(consts_ready, 7)
            a.activation(ident_r[:], ident[:], ACT.Copy).then_inc(consts_r_ready, 1)
            a.activation(sel_r[:], sel[:], ACT.Copy).then_inc(consts_r_ready, 1)
            a.activation(mask_st[:], scr_a[:, 0:P], ACT.Copy).then_inc(consts_r_ready, 1)
            a.activation(mask_ts[:], scr_a[:, P:2 * P], ACT.Copy).then_inc(consts_r_ready, 1)
            act.wait_ge(gate_in, 32)
            a.activation(wg_hi[:], wg_raw[:], ACT.Copy).then_inc(gw_hi, 1)
            for c in range(C):
                acts_out(TURN_X0, C * SET_X0 + c, c, 0, act_hi)
            w_hi(1, 1)
            w_hi(2, 0)
            w_hi(3, 1)
            for h in range(M_HEADS):
                wait_bank(act, G_QK, h)
                a.activation(mq_hi[:, h], ps[:, h], ACT.Copy).then_inc(m_hi, 1)
            act.wait_ge(gates_done, 1)
            act.wait_ge(gw_ready, 2)
            a.activation(g_raw[:], ps[0:8, 4], ACT.Tanh, scale=1.0 / CAP, bias=gate_b15[:, 0:1]).then_inc(tanh_ready, 1)
            act.wait_ge(f_rows_in, 16)
            done(a.activation(e_row[:], f_raw[:], ACT.Exp, scale=-CAP))
            a.activation(sp_row[:], e_row[:], ACT.Ln, bias=1.0).then_inc(sp_ready, 1)
            w_hi(4, 0)
            act.wait_ge(mneg_ready, 1)
            a.activation(e_row[:], b_row[:], ACT.Exp).then_inc(e_ready, 1)
            act.wait_ge(rows_ready, 1)
            a.activation(r_hi[:], r_row[:], ACT.Copy).then_inc(r_hi_ready, 1)
            w_hi(5, 1)
            for h in range(M_HEADS):
                wait_bank(act, G_QK + 1, h)
                a.activation(mk_hi[:, h], ps[:, 4 + h], ACT.Copy, scale=M_QK ** -0.5).then_inc(m_hi, 1)
            for g in range(2):
                w_hi(U_V + 2 * g + 2, 0)
                w_hi(U_V + 2 * g + 3, 1)
                for t in range(T):
                    wait_bank(act, G_V + g, t)
                    a.activation(mv_hi[:, t, 2 * g:2 * g + 2, 0:M_V],
                                 ps[:, 4 * g + t].rearrange("p (h e) -> p h e", h=2), ACT.Copy).then_inc(m_hi, 1)
            for g in range(2):
                w_hi(U_O + 2 * g + 2, 0)
                w_hi(U_O + 2 * g + 3, 1)
                for t in range(T):
                    wait_bank(act, G_O + g, t)
                    a.activation(y_nat[:, t, g * COLS:(g + 1) * COLS], ps[:, 4 * g + t], ACT.Sigmoid).then_inc(sig_ready, 1)
            act.wait_ge(acol_ready, 1)

            def head_weights(h):
                for k in range(T):
                    w = P * (T - k)
                    act.wait_ge(bcast_done, T * h + T)
                    if h >= 2:
                        act.wait_ge(p_lo_ready, T * (h - 2) + k + 1)
                    b, o = divmod(KSTART[k], COLS)
                    a.activation(decay[:, h % 2, KSTART[k]:KSTART[k] + w], ps[:, b, o:o + w], ACT.Exp,
                                 bias=acol[:, k, h:h + 1]).then_inc(decay_ready, 1)
                for k in range(T):
                    w = P * (T - k)
                    act.wait_ge(p_ready, T * h + k + 1)
                    if h >= 2:
                        act.wait_ge(av_done, T * (h - 1))
                    sl = slice(KSTART[k], KSTART[k] + w)
                    a.activation(p_hi[:, h % 2, sl], decay[:, h % 2, sl], ACT.Copy).then_inc(p_hi_ready, 1)

            def head_squares(h):
                for J in range(T):
                    act.wait_ge(av_done, T * h + J + 1)
                    done(a.activation(junk_m[:], ps[:, 6 + J % 2, 0:M_V], ACT.Square, accum_out=mss[:, J, h:h + 1]))
                    a.copy(den[:, J, h:h + 1], ps[:, 6 + J % 2, M_V:M_V + 1]).then_inc(av_sq, 1)

            head_weights(0)
            for h in range(1, M_HEADS):
                head_weights(h)
                head_squares(h - 1)
            head_squares(M_HEADS - 1)
            act.wait_ge(mvar_ready, 1)
            a.activation(mfac[:], mss[:], ACT.Sqrt, scale=1.0 / M_V, bias=epsc[:, 0:1]).then_inc(mstd_ready, 1)
            for c in range(C):
                acts_out(TURN_YM, C * SET_YM + c, c, GC_AHEAD, act_hi)
            w_hi(U_OUT + 2, 0)
            w_hi(U_OUT + 3, 1)
            first_squares(0, G_OUT)
            w_hi(U_OUT + 4, 0)
            post_norm(0, G_OUT, False)

            def mlp(layer, u_up, u_down, G_up, G_down, turn, aset, aset_gc, n_post):
                for c in range(C):
                    acts_out(turn, C * aset + c, c, aset_gc, act_hi)
                w_hi(u_up + 1, 1)
                x_stats(turn)

                def relus(i, g2):
                    for b in range(4):
                        n = i * 8 + (4 * g2 + b)
                        if b < 3:
                            act.wait_ge(bank_done, i * 6 + (3 * (G_up + g2) + b + 1))
                        else:
                            act.wait_ge(unit_used, i * 4 + (u_up + 2 * g2 + 2))
                        if not (isinstance(n, int) and n < 2):
                            act.wait_ge(up_evac, n + (32 * layer - 1))
                        a.activation(relu_t[:, b % 2], ps[:, 4 * g2 + b], ACT.Relu).then_inc(relu_ready, 1)

                def down_part(j, n, s):
                    act.wait_ge(unit_used, j * 2 + (u_down + KU * n + s - 1))
                    if n == 0:
                        act.wait_ge(up_evac, j * 8 + (32 * layer + 4 * s + 4))
                    src = u_sq[:, 4 * s:4 * s + 4] if isinstance(j, int) and j == 0 else u_sq[:, bass.ds(j * 8 + 4 * s, 4)]
                    a.activation(act_hi[:, 4 * s:4 * s + 4], src, ACT.Copy).then_inc(down_hi, 1)

                def pair(i, last=False):
                    for g2 in range(2):
                        w_hi_at(i * 2 + g2, u_up + 2, 0)
                        if last and g2 == 1:
                            down_part(0, 0, 0)
                            w_hi_at(i * 2 + g2, u_up + 2, 1)
                            down_part(0, 0, 1)
                        else:
                            w_hi_at(i * 2 + g2, u_up + 2, 1)
                        relus(i, g2)

                pair(0)
                with act.Fori(1, UPG // 2 - 1) as i:
                    pair(i)
                pair(UPG // 2 - 1, last=True)
                for n in range(2):
                    if n:
                        for s in range(2):
                            down_part(0, n, s)
                            w_hi_at(0, u_down + KU * n, s)
                        first_squares(n_post, G_down)
                    with act.Fori(1, KU // 2) as j:
                        for s in range(2):
                            down_part(j, n, s)
                            w_hi_at(j, u_down + KU * n, s)
                w_hi(u_down + DU, 0)
                post_norm(n_post, G_down, True)

            mlp(0, U_UP, U_DOWN, G_UP, G_DOWN, TURN_X1, SET_X1, 8 * 2, 1)
            for half in range(2):
                for c in range(4 * half, 4 * half + 4):
                    acts_out(TURN_X2, C * SET_Q + 4 * half + c, c, 8 * 4, xq_hi)
                for c in range(4 * half, 4 * half + 4):
                    acts_out(TURN_X2, C * SET_Q + 4 * half + 4 + c, c, GC_KV, act_hi)
            w_hi(U_Q2 + 1, 1)
            x_stats(TURN_X2)
            act.wait_ge(ang_ready, 1)
            a.activation(trig[:], ang[:], ACT.Sin).then_inc(trig_ready, 1)
            act.wait_ge(lams_ready, 1)
            a.activation(lam_e[:], lam_s[:], ACT.Exp).then_inc(lame_ready, 1)

            def rope_hi(G):
                dst = q_hi if G < G_K2 else k_hi
                for t in range(T):
                    act.wait_ge(rope_turned, 4 * (G - G_Q2) + t + 1)
                    a.activation(dst[:, 4 * (G % 2):4 * (G % 2) + 4, P * t:P * t + P],
                                 ps[:, 4 * (G % 2) + t].rearrange("p (h k) -> p h k", h=4), ACT.Copy).then_inc(qk_hi, 1)

            for G in range(G_Q2, G_V2):
                u = U_Q2 + 2 * (G - G_Q2)
                w_hi(u + 2, 0)
                if G > G_Q2:
                    rope_hi(G - 1)
                w_hi(u + 3, 1)
            for g in range(2):
                u = U_V2 + 2 * g
                w_hi(u + 2, 0)
                if g == 0:
                    rope_hi(G_V2 - 1)
                w_hi(u + 3, 1)
                for t in range(T):
                    wait_bank(act, G_V2 + g, t)
                    a.activation(v_hi[:, t, g * COLS:(g + 1) * COLS], ps[:, 4 * g + t], ACT.Copy,
                                 scale=rx[:, t:t + 1]).then_inc(v_hi_s, 1)

            steps = [(J, h) for J in reversed(range(T)) for h in range(A_HEADS)]

            def exps(i):
                J, h = steps[i]
                n = P * (J + 1)
                act.wait_ge(max_ready, i + 1)
                if i >= 2:
                    act.wait_ge(diff_ready, i - 1)
                for m in range(2):
                    a.activation(probs[:, i % 2, m, 0:n], ps[:, 2 * (i % 2) + m, 0:n], ACT.Exp, scale=A_DIM ** -0.5,
                                 bias=nmax[:, i % 2, m:m + 1], accum_out=lsum[:, i % 2, m:m + 1]).then_inc(exp_ready, 1)

            def pt_split(i):
                J, h = steps[i]
                n = P * (J + 1)
                act.wait_ge(pt_done, i + 1)
                if i >= 2:
                    act.wait_ge(o_done, i - 1)
                a.activation(pt_hi[:, i % 2, 0:n], ps[:, 4 + i % 2, 0:n], ACT.Copy).then_inc(pt_hi_s, 1)

            def copy_o(q):
                act.wait_ge(o_done, A_HEADS * (q + 1))
                for b in range(2):
                    a.activation(o_nat[:, T - 1 - q, b * COLS:(b + 1) * COLS], ps[:, 6 + b], ACT.Copy).then_inc(o_copied, 1)

            exps(0)
            for i in range(len(steps)):
                if i + 1 < len(steps):
                    exps(i + 1)
                pt_split(i)
                if i >= A_HEADS and i % A_HEADS == 1:
                    copy_o(i // A_HEADS - 1)
            copy_o(T - 1)
            act.wait_ge(ovar_ready, 1)
            a.activation(orms[:], oss[:], ACT.Sqrt, scale=1.0 / (2 * A_DIM), bias=epsc[:, 0:1]).then_inc(ostd_ready, 1)
            for c in range(C):
                acts_out(TURN_YA, C * SET_YA + c, c, GC_BHEAD, q_hi)
            w_hi(U_OUT2 + 2, 0)
            w_hi(U_OUT2 + 3, 1)
            first_squares(2, G_OUT2)
            w_hi(U_OUT2 + 4, 0)
            post_norm(2, G_OUT2, False)
            mlp(1, U_UP2, U_DOWN2, G_UP2, G_DOWN2, TURN_X3, SET_X3, 8 * 6, 3)

        @block.vector
        def _(dve):
            v = nc.vector
            own = [0]

            def done(ins):
                own[0] += 1
                ins.then_inc(dve_self, 1)
                dve.wait_ge(dve_self, own[0])

            def f32(ap):
                return ap.bitcast(F32)

            def turned_chunk(c):
                return ps[:, T * (c % 2):T * (c % 2) + T, P * (c // 2):P * (c // 2) + P]

            def acts_out(n, c, gc, hi, lo):
                dve.wait_ge(acts_hi, n + 1)
                v.scalar_tensor_tensor(out=lo[:, c].rearrange("p (t k) -> p t k", t=T), in0=turned_chunk(c),
                                       scalar=gcols[:, gc + c:gc + c + 1],
                                       in1=f32(hi[:, c]).rearrange("p (t k) -> p t k", t=T),
                                       op0=ALU.mult, op1=ALU.subtract).then_inc(acts_ready, 1)

            def x_scale(n, t, last=False):
                dve.wait_ge(rmsx_ready, T * n + t + 1)
                ins = v.reciprocal(rx[:, t:t + 1], rmsx[:, t:t + 1])
                if last:
                    ins.then_inc(rx_ready, 1)
                else:
                    done(ins)

            def post_bias(n, mlp):
                for t in range(T):
                    dve.wait_ge(sq0, T * n + t + 1)
                    if mlp:
                        v.tensor_scalar(bias0[:, t:t + 1], ssq[:, t, 0:1], rx4[:, t:t + 1], EPS, ALU.mult,
                                        ALU.add).then_inc(bias0_ready, 1)
                    else:
                        v.tensor_scalar(bias0[:, t:t + 1], ssq[:, t, 0:1], 1.0 / D_MODEL, EPS, ALU.mult,
                                        ALU.add).then_inc(bias0_ready, 1)

            def post_norm(n, mlp):
                dve.wait_ge(gpost_in, 16 * (n + 1))
                for t in range(T):
                    dve.wait_ge(rms_ready, T * n + t + 1)
                    done(v.reciprocal(fac[:, t:t + 1], rms[:, t:t + 1]))
                    if mlp:
                        done(v.tensor_tensor(fac[:, t:t + 1], fac[:, t:t + 1], rx2[:, t:t + 1], ALU.mult))
                    for b in range(2):
                        ins = v.scalar_tensor_tensor(out=tmp[:, t % 2, b * COLS:(b + 1) * COLS], in0=ps[:, 4 * b + t],
                                                     scalar=fac[:, t:t + 1], in1=gpost[:, b * COLS:(b + 1) * COLS],
                                                     op0=ALU.mult, op1=ALU.mult)
                    ins.then_inc(gpost_used, 1)
                    dve.wait_ge(gpost_used, T * n + t + 1)
                    v.tensor_tensor(x_sb[:, t], x_sb[:, t], tmp[:, t % 2], ALU.add).then_inc(nat_ready, 1)

            done(v.memset(epsc[:], EPS))
            dve.wait_ge(gcols_turned, 1)
            v.tensor_copy(gcols[:], ps[:, 7, 0:GROWS]).then_inc(gcols_ready, 1)
            for t in range(T):
                x_scale(0, t)
                v.tensor_scalar(y_nat[:, t], x_sb[:, t], rx[:, t:t + 1], None, ALU.mult).then_inc(nat_ready, 1)
            dve.wait_ge(gate_in, 32)
            v.memset(f32(mv_hi[:, :, :, M_V:VW]), 1.0).then_inc(ones_ready, 1)
            dve.wait_ge(gw_hi, 1)
            v.tensor_tensor(wg_lo[:], wg_raw[:], f32(wg_hi[:]), ALU.subtract).then_inc(gw_ready, 1)
            v.tensor_scalar(gate_b15[:], gate_b[:], 1.0 / CAP, None, ALU.mult).then_inc(gw_ready, 1)
            v.tensor_scalar(gcols[:, GC_BHEAD:GC_BHEAD + 8], gcols[:, GC_BHEAD:GC_BHEAD + 8], 1.0 - LAM_INIT, None,
                            ALU.mult).then_inc(gcols_ready, 1)
            for c in range(C):
                acts_out(C * SET_X0 + c, c, 0, act_hi, act_lo)
            for h in range(M_HEADS):
                dve.wait_ge(m_hi, h + 1)
                v.tensor_tensor(mq_lo[:, h], ps[:, h], f32(mq_hi[:, h]), ALU.subtract).then_inc(m_evac, 1)
            dve.wait_ge(sp_ready, 1)

            def blk(r, J):
                return r[:, P * J:P * J + P]

            for J in range(T):
                done(v.tensor_tensor_scan(blk(b_row, J), blk(sp_row, J), blk(sp_row, J), 0.0, ALU.add, ALU.max))
            done(v.scalar_tensor_tensor(out=a_row[:], in0=g_raw[0:M_HEADS, :], scalar=CAP, in1=b_row[:], op0=ALU.mult,
                                        op1=ALU.add))
            done(v.memset(carry[:], 0.0))
            done(v.memset(dcum[:], 0.0))
            for J in range(T):
                last = P * J + P - 1
                done(v.tensor_tensor_scan(blk(m_row, J), blk(a_row, J), blk(a_row, J), carry[:, J:J + 1], ALU.max, ALU.max))
                if J + 1 < T:
                    done(v.tensor_tensor(carry[:, J + 1:J + 2], m_row[:, last:last + 1], b_row[:, last:last + 1], ALU.subtract))
                    for k in range(J + 1):
                        done(v.tensor_tensor(dcum[:, k, J + 1:J + 2], dcum[:, k, J:J + 1], b_row[:, last:last + 1], ALU.add))
            for k in range(T):
                for J in range(k, T):
                    o = KSTART[k] + P * (J - k)
                    done(v.tensor_scalar(r_row[:, o:o + P], blk(m_row, J), dcum[:, k, J:J + 1], -1.0, ALU.add, ALU.mult))
            v.tensor_tensor(b_row[:], b_row[:], m_row[:], ALU.subtract).then_inc(mneg_ready, 1)
            v.engine_nop().then_inc(rows_ready, 1)
            dve.wait_ge(e_ready, 1)
            done(v.tensor_scalar(e_row[:], e_row[:], 3e38, None, ALU.min))
            dve.wait_ge(r_hi_ready, 1)
            v.tensor_tensor(r_lo[:], r_row[:], f32(r_hi[:]), ALU.subtract).then_inc(rows_ready, 1)
            for h in range(M_HEADS):
                dve.wait_ge(m_hi, M_HEADS + h + 1)
                v.scalar_tensor_tensor(out=mk_lo[:, h], in0=ps[:, 4 + h], scalar=M_QK ** -0.5, in1=f32(mk_hi[:, h]),
                                       op0=ALU.mult, op1=ALU.subtract).then_inc(m_evac, 1)
            dve.wait_ge(acol_turned, 1)
            v.tensor_copy(acol[:], ps[:, 3, 0:2 * T * M_HEADS].rearrange("p (t h) -> p t h", h=M_HEADS)).then_inc(acol_ready, 1)
            for g in range(2):
                for t in range(T):
                    dve.wait_ge(m_hi, 2 * M_HEADS + T * g + t + 1)
                    v.tensor_tensor(mv_lo[:, t, 2 * g:2 * g + 2, 0:M_V], ps[:, 4 * g + t].rearrange("p (h e) -> p h e", h=2),
                                    f32(mv_hi[:, t, 2 * g:2 * g + 2, 0:M_V]), ALU.subtract).then_inc(m_evac, 1)
            def head_weights(h):
                for k in range(T):
                    w = P * (T - k)
                    dve.wait_ge(decay_ready, T * h + k + 1)
                    dve.wait_ge(s_done, T * h + T)
                    sl = slice(KSTART[k], KSTART[k] + w)
                    b, o = divmod(KSTART[k], COLS)
                    v.tensor_tensor(decay[:, h % 2, sl], decay[:, h % 2, sl], ps[:, 3 + b, o:o + w],
                                    ALU.mult).then_inc(p_ready, 1)
                for k in range(T):
                    w = P * (T - k)
                    dve.wait_ge(p_hi_ready, T * h + k + 1)
                    sl = slice(KSTART[k], KSTART[k] + w)
                    v.tensor_tensor(p_lo[:, h % 2, sl], decay[:, h % 2, sl], f32(p_hi[:, h % 2, sl]),
                                    ALU.subtract).then_inc(p_lo_ready, 1)

            def head_out(h):
                for J in range(T):
                    dve.wait_ge(av_sq, T * h + J + 1)
                    if h == 0 and J == 0:
                        dve.wait_ge(sig_ready, 2 * T)
                    sl = slice(h * M_V, (h + 1) * M_V)
                    v.tensor_tensor(y_nat[:, J, sl], y_nat[:, J, sl], ps[:, 6 + J % 2, 0:M_V], ALU.mult).then_inc(av_evac, 1)

            head_weights(0)
            for h in range(1, M_HEADS):
                head_weights(h)
                head_out(h - 1)
            head_out(M_HEADS - 1)
            done(v.scalar_tensor_tensor(out=den2[:], in0=den[:], scalar=-1.0, in1=den[:], op0=ALU.mult, op1=ALU.max))
            done(v.tensor_tensor(den2[:], den2[:], acol[:, T:2 * T, :], ALU.max))
            done(v.reciprocal(den[:], den2[:]))
            done(v.tensor_tensor(mss[:], mss[:], den[:], ALU.mult))
            v.tensor_tensor(mss[:], mss[:], den[:], ALU.mult).then_inc(mvar_ready, 1)
            dve.wait_ge(mstd_ready, 1)
            done(v.reciprocal(den2[:], mfac[:]))
            done(v.tensor_tensor(den2[:], den2[:], den[:], ALU.mult))
            for t in range(T):
                dve.wait_ge(av_evac, T * M_HEADS)
                for h in range(M_HEADS):
                    sl = slice(h * M_V, (h + 1) * M_V)
                    ins = v.tensor_scalar(y_nat[:, t, sl], y_nat[:, t, sl], den2[:, t, h:h + 1], None, ALU.mult)
                ins.then_inc(nat_ready, 1)
            for c in range(C):
                acts_out(C * SET_YM + c, c, GC_AHEAD, act_hi, act_lo)
            post_bias(0, False)
            post_norm(0, False)

            def mlp(layer, u_down, aset, gc, n_norm, n_post):
                for c in range(C):
                    acts_out(C * aset + c, c, gc, act_hi, act_lo)
                for t in range(T):
                    x_scale(n_norm, t)
                done(v.tensor_tensor(rx2[:], rx[:], rx[:], ALU.mult))
                done(v.scalar_tensor_tensor(out=rx4[:], in0=rx2[:], scalar=1.0 / D_MODEL, in1=rx2[:], op0=ALU.mult,
                                            op1=ALU.mult))

                def squares(i, g2):
                    for b in range(4):
                        n = i * 8 + (4 * g2 + b)
                        dve.wait_ge(relu_ready, n + (32 * layer + 1))
                        dst = u_sq[:, n] if isinstance(n, int) else u_sq[:, bass.ds(n, 1)].rearrange("p a s -> p (a s)")
                        v.tensor_tensor(dst, relu_t[:, b % 2], ps[:, 4 * g2 + b], ALU.mult).then_inc(up_evac, 1)

                def down_part(j, n, s):
                    dve.wait_ge(down_hi, j * 2 + (DU * layer + KU * n + s + 1))
                    src = u_sq[:, 4 * s:4 * s + 4] if isinstance(j, int) and j == 0 else u_sq[:, bass.ds(j * 8 + 4 * s, 4)]
                    v.tensor_tensor(act_lo[:, 4 * s:4 * s + 4], src, f32(act_hi[:, 4 * s:4 * s + 4]),
                                    ALU.subtract).then_inc(down_ready, 1)

                squares(0, 0)
                squares(0, 1)
                with dve.Fori(1, UPG // 2 - 1) as i:
                    for g2 in range(2):
                        squares(i, g2)
                squares(UPG // 2 - 1, 0)
                down_part(0, 0, 0)
                down_part(0, 0, 1)
                squares(UPG // 2 - 1, 1)
                for n in range(2):
                    if n:
                        for s in range(2):
                            down_part(0, n, s)
                        post_bias(n_post, True)
                    with dve.Fori(1, KU // 2) as j:
                        for s in range(2):
                            down_part(j, n, s)
                post_norm(n_post, True)

            mlp(0, U_DOWN, SET_X1, 8 * 2, 1, 1)
            for half in range(2):
                for c in range(4 * half, 4 * half + 4):
                    acts_out(C * SET_Q + 4 * half + c, c, 8 * 4, xq_hi, xq_lo)
                for c in range(4 * half, 4 * half + 4):
                    acts_out(C * SET_Q + 4 * half + 4 + c, c, GC_KV, act_hi, act_lo)
            for t in range(T):
                x_scale(2, t, last=True)
            dve.wait_ge(pos_in, 32)
            done(v.tensor_copy(pos_f[:], pos_i[:]))
            for t in range(T):
                done(v.tensor_scalar(ang[:, 0, t], inv[:], pos_f[:, t:t + 1], None, ALU.mult))
            MAGIC = 1.5 * 2.0 ** 23
            for m in range(2):
                done(v.tensor_scalar(turns[:, m], ang[:, 0], 1.0 / (2 * math.pi), 0.25 * m, ALU.mult, ALU.add))
            done(v.tensor_scalar(turns[:], turns[:], MAGIC, None, ALU.add))
            done(v.tensor_scalar(turns[:], turns[:], MAGIC, None, ALU.subtract))
            done(v.tensor_copy(ang[:, 1], ang[:, 0]))
            for part in TWO_PI:
                done(v.scalar_tensor_tensor(out=ang[:], in0=turns[:], scalar=-part, in1=ang[:], op0=ALU.mult, op1=ALU.add))
            done(v.tensor_scalar(ang[:, 1], ang[:, 1], math.pi / 2, None, ALU.add))
            v.tensor_scalar(ang[:], ang[:], 3.1415925, -3.1415925, ALU.min, ALU.max).then_inc(ang_ready, 1)
            dve.wait_ge(lam_in_s, 16)
            for m in range(2):
                done(v.tensor_tensor(lam_pr[:, m], lam_in[:, 2 * m], lam_in[:, 2 * m + 1], ALU.mult))
            v.tensor_reduce(lam_s[:], lam_pr[:], AX.X, ALU.add).then_inc(lams_ready, 1)
            dve.wait_ge(trig_ready, 1)
            dve.wait_ge(rx_ready, T)
            for t in range(T):
                done(v.tensor_scalar(trig[:, :, t], trig[:, :, t], rx[:, t:t + 1], None, ALU.mult))
            dve.wait_ge(lame_ready, 1)
            done(v.memset(lam2[:], 1.0))
            done(v.scalar_tensor_tensor(out=lam2[:, 1:2], in0=lam_e[:, 1:2], scalar=-LAM_INIT, in1=lam_e[:, 0:1],
                                        op0=ALU.add, op1=ALU.subtract))

            def rotate(G):
                for t in range(T):
                    wait_bank(dve, G, t)
                    src = ps[:, 4 * (G % 2) + t].rearrange("p (m a d) -> p m a d", a=2, d=HALF)
                    cos = trig[:, 1, t:t + 1, :]
                    sin = trig[:, 0, t:t + 1, :]
                    if G > G_Q2:
                        dve.wait_ge(rope_turned, 4 * (G - 1 - G_Q2) + t + 1)
                    ta = scr_a[:].rearrange("p (m a d) -> p m a d", a=2, d=HALF)
                    tb = scr_b[:].rearrange("p (m a d) -> p m a d", a=2, d=HALF)
                    dst = roped[:, t].rearrange("p (m a d) -> p m a d", a=2, d=HALF)
                    own[0] += 3
                    v.tensor_tensor(scr_a[:].rearrange("p (m d) -> p m d", d=HALF),
                                    ps[:, 4 * (G % 2) + t].rearrange("p (m d) -> p m d", d=HALF),
                                    cos.to_broadcast([P, 16, HALF]), ALU.mult).then_inc(dve_self, 1)
                    v.tensor_tensor(tb[:, :, 0], src[:, :, 1], sin.to_broadcast([P, 8, HALF]), ALU.mult).then_inc(dve_self, 1)
                    v.tensor_tensor(tb[:, :, 1], src[:, :, 0], sin.to_broadcast([P, 8, HALF]), ALU.mult).then_inc(dve_self, 1)
                    dve.wait_ge(dve_self, own[0])
                    v.tensor_tensor(dst[:, :, 0], ta[:, :, 0], tb[:, :, 0], ALU.subtract)
                    own[0] += 1
                    v.tensor_tensor(dst[:, :, 1], ta[:, :, 1], tb[:, :, 1], ALU.add).then_inc(rope_ready, 1)
                    dve.wait_ge(rope_ready, 4 * (G - G_Q2) + t + 1)
                    own[0] -= 1

            def rope_lo(G):
                hi, lo = (q_hi, q_lo) if G < G_K2 else (k_hi, k_lo)
                for t in range(T):
                    dve.wait_ge(qk_hi, 4 * (G - G_Q2) + t + 1)
                    hs = slice(4 * (G % 2), 4 * (G % 2) + 4)
                    v.tensor_tensor(lo[:, hs, P * t:P * t + P], ps[:, 4 * (G % 2) + t].rearrange("p (h k) -> p h k", h=4),
                                    f32(hi[:, hs, P * t:P * t + P]), ALU.subtract).then_inc(qk_ready, 1)

            for G in range(G_Q2, G_V2):
                rotate(G)
                rope_lo(G)
            for g in range(2):
                for t in range(T):
                    dve.wait_ge(v_hi_s, T * g + t + 1)
                    sl = slice(g * COLS, (g + 1) * COLS)
                    v.scalar_tensor_tensor(out=v_lo[:, t, sl], in0=ps[:, 4 * g + t], scalar=rx[:, t:t + 1],
                                           in1=f32(v_hi[:, t, sl]), op0=ALU.mult, op1=ALU.subtract).then_inc(v_ready, 1)

            steps = [(J, h) for J in reversed(range(T)) for h in range(A_HEADS)]

            def maxima(i):
                J, h = steps[i]
                n = P * (J + 1)
                s = i % 2
                dve.wait_ge(scores_done, i + 1)
                done(v.tensor_reduce(smax[:, s], ps[:, 2 * s:2 * s + 2, 0:n], AX.X, ALU.max))
                v.tensor_scalar(nmax[:, s], smax[:, s], -(A_DIM ** -0.5), None, ALU.mult).then_inc(max_ready, 1)

            def difference(i):
                J, h = steps[i]
                n = P * (J + 1)
                s = i % 2
                dve.wait_ge(exp_ready, 2 * i + 2)
                done(v.reciprocal(linv[:, s], lsum[:, s]))
                done(v.tensor_tensor(linv[:, s], linv[:, s], lam2[:], ALU.mult))
                done(v.tensor_scalar(probs[:, s, 1, 0:n], probs[:, s, 1, 0:n], linv[:, s, 1:2], None, ALU.mult))
                if i >= 2:
                    dve.wait_ge(pt_done, i - 1)
                v.scalar_tensor_tensor(out=pdiff[:, s, 0:n], in0=probs[:, s, 0, 0:n], scalar=linv[:, s, 0:1],
                                       in1=probs[:, s, 1, 0:n], op0=ALU.mult, op1=ALU.add).then_inc(diff_ready, 1)

            def pt_split(i):
                J, h = steps[i]
                n = P * (J + 1)
                dve.wait_ge(pt_hi_s, i + 1)
                v.tensor_tensor(pt_lo[:, i % 2, 0:n], ps[:, 4 + i % 2, 0:n], f32(pt_hi[:, i % 2, 0:n]),
                                ALU.subtract).then_inc(pt_ready, 1)

            def o_squares(q):
                t = T - 1 - q
                for b in range(2):
                    dve.wait_ge(o_copied, 2 * q + b + 1)
                    sl = slice(b * COLS, (b + 1) * COLS)
                    done(v.tensor_tensor(junk[:], o_nat[:, t, sl], o_nat[:, t, sl], ALU.mult))
                    done(v.tensor_reduce(oss[:, t, 4 * b:4 * b + 4], junk[:].rearrange("p (h e) -> p h e", h=4), AX.X, ALU.add))

            maxima(0)
            for i in range(len(steps)):
                if i + 1 < len(steps):
                    maxima(i + 1)
                difference(i)
                if i >= 1:
                    pt_split(i - 1)
                if i >= A_HEADS and i % A_HEADS == 3:
                    o_squares(i // A_HEADS - 1)
            pt_split(len(steps) - 1)
            o_squares(T - 1)
            v.engine_nop().then_inc(ovar_ready, 1)
            dve.wait_ge(ostd_ready, 1)
            done(v.reciprocal(oss[:], orms[:]))
            for t in range(T):
                v.tensor_tensor(o_nat[:, t].rearrange("p (h e) -> p h e", h=A_HEADS),
                                o_nat[:, t].rearrange("p (h e) -> p h e", h=A_HEADS),
                                oss[:, t].rearrange("p (h a) -> p h a", a=1).to_broadcast([P, A_HEADS, 2 * A_DIM]),
                                ALU.mult).then_inc(nat_ready, 1)
            for c in range(C):
                acts_out(C * SET_YA + c, c, GC_BHEAD, q_hi, q_lo)
            post_bias(2, False)
            post_norm(2, False)
            mlp(1, U_DOWN2, SET_X3, 8 * 6, 3, 3)

        @block.tensor
        def _(pe):
            def three(out, s_hi, s_lo, m_hi_, m_lo_, first, last):
                pe.matmul(out, s_hi, m_hi_, start=first, stop=False)
                pe.matmul(out, s_hi, m_lo_, start=False, stop=False)
                return pe.matmul(out, s_lo, m_hi_, start=False, stop=last)

            def unit(u, s, bank0, acts, weights_still, first, last, bank_wait=None):
                pe.wait_ge(weights_ready, u + 1)
                for b in range(4):
                    if bank_wait:
                        bank_wait(b)
                    for k in range(UC):
                        cut = slice(P * b, P * b + P)
                        if weights_still:
                            mm = three(ps[:, bank0 + b], whi[:, s, k, cut], wlo[:, s, k, cut], acts[0][:, k], acts[1][:, k],
                                       first and k == 0, last and k == UC - 1)
                        else:
                            mm = three(ps[:, bank0 + b], acts[0][:, k, cut], acts[1][:, k, cut], whi[:, s, k], wlo[:, s, k],
                                       first and k == 0, last and k == UC - 1)
                    if last and b < 3:
                        mm.then_inc(bank_done, 1)
                mm.then_inc(unit_used, 1)

            def group(u, g2, acts, weights_still, unit_wait=None, bank_wait=None, between=None):
                for s in range(2):
                    if unit_wait:
                        unit_wait(s)
                    part = tuple(t[:, UC * s:UC * s + UC] for t in acts)
                    unit(u + s, s, 4 * g2, part, weights_still, s == 0, s == 1, bank_wait if s == 0 else None)
                    if s == 0 and between:
                        between()

            def turn(n, src):
                for t in range(T):
                    pe.wait_ge(nat_ready, T * n + t + 1)
                    for c in range(C):
                        mm = pe.transpose(ps[:, T * (c % 2) + t, P * (c // 2):P * (c // 2) + P], src[:, t, P * c:P * c + P],
                                          ident[:])
                    mm.then_inc(turned, 1)

            def after_set(n0, n1):
                def first(s):
                    pe.wait_ge(acts_ready, n0 if s == 0 else n1)
                return first

            acts = (act_hi, act_lo)
            pe.wait_ge(consts_ready, 2)
            pe.wait_ge(grows_in, 64)
            pe.transpose(ps[:, 7, 0:GROWS], grows[:], ident[0:GROWS, 0:GROWS]).then_inc(gcols_turned, 1)
            pe.wait_ge(gcols_ready, 1)
            turn(TURN_X0, y_nat)
            group(U_QK, 0, acts, True, after_set(7, 8))
            pe.wait_ge(gw_ready, 1)
            for c in range(C):
                mm = three(ps[0:8, 4], wg_hi[:, c], wg_lo[:, c], act_hi[:, c], act_lo[:, c], c == 0, c == C - 1)
            mm.then_inc(gates_done, 1)
            group(U_QK + 2, 1, acts, True, bank_wait=lambda b: pe.wait_ge(tanh_ready, 1))
            pe.wait_ge(m_evac, 4)
            pe.wait_ge(rows_ready, 2)
            for t in range(T):
                pe.transpose(ps[:, 3, M_HEADS * t:M_HEADS * (t + 1)], a_row[:, P * t:P * t + P], ident[0:M_HEADS, 0:M_HEADS])
            for t in range(T, 2 * T):
                mm = pe.transpose(ps[:, 3, M_HEADS * t:M_HEADS * (t + 1)], e_row[:, P * (t - T):P * (t - T) + P],
                                  ident[0:M_HEADS, 0:M_HEADS])
            mm.then_inc(acol_turned, 1)

            def v_bank(b):
                if b == 3:
                    pe.wait_ge(acol_ready, 1)

            group(U_V, 0, acts, False, bank_wait=v_bank)
            group(U_V + 2, 1, acts, False, bank_wait=lambda b: pe.wait_ge(m_evac, 4 + b + 1))
            group(U_O, 0, acts, False, bank_wait=lambda b: pe.wait_ge(m_evac, 8 + b + 1))
            group(U_O + 2, 1, acts, False, bank_wait=lambda b: pe.wait_ge(m_evac, 12 + b + 1))

            def head_scores(h):
                for k in range(T):
                    w = P * (T - k)
                    b, o = divmod(KSTART[k], COLS)
                    if h == 0:
                        pe.wait_ge(sig_ready, 2 * T)
                        pe.wait_ge(consts_r_ready, 4)
                    else:
                        pe.wait_ge(decay_ready, T * h)
                        pe.wait_ge(p_ready, T * h)
                    sl = slice(KSTART[k], KSTART[k] + w)
                    pe.matmul(ps[:, b, o:o + w], sel_r[:, h], r_hi[:, sl], start=True, stop=False)
                    pe.matmul(ps[:, b, o:o + w], sel_r[:, h], r_lo[:, sl], start=False, stop=False)
                    pe.matmul(ps[:, b, o:o + P], ident_r[:], mask_st[:], start=False, stop=True).then_inc(bcast_done, 1)
                    three(ps[:, 3 + b, o:o + w], mk_hi[:, h, P * k:P * k + P], mk_lo[:, h, P * k:P * k + P],
                          mq_hi[:, h, P * k:SEQ], mq_lo[:, h, P * k:SEQ], True, True).then_inc(s_done, 1)

            def head_values(h):
                for J in range(T):
                    pe.wait_ge(p_lo_ready, T * h + J + 1)
                    n = T * h + J
                    if n >= 2:
                        pe.wait_ge(av_evac, n - 1)
                    for k in range(J + 1):
                        o = KSTART[k] + P * (J - k)
                        bank = ps[:, 6 + J % 2]
                        hi, lo = p_hi[:, h % 2, o:o + P], p_lo[:, h % 2, o:o + P]
                        pe.matmul(bank[:, 0:VW], hi, mv_hi[:, k, h], start=(k == 0), stop=False)
                        pe.matmul(bank[:, 0:VW], lo, mv_hi[:, k, h], start=False, stop=False)
                        mm = pe.matmul(bank[:, 0:M_V], hi, mv_lo[:, k, h, 0:M_V], start=False, stop=(k == J))
                    mm.then_inc(av_done, 1)

            pe.wait_ge(ones_ready, 1)
            head_scores(0)
            for h in range(1, M_HEADS):
                head_scores(h)
                head_values(h - 1)
            head_values(M_HEADS - 1)
            turn(TURN_YM, y_nat)

            def two_groups(u, aset, acts):
                group(u, 0, acts, False, after_set(C * aset + 7, C * aset + 8))
                group(u + 2, 1, acts, False)

            two_groups(U_OUT, SET_YM, acts)

            def mlp(layer, turn_n, aset, u_up, u_down):
                turn(turn_n, x_sb)

                def pair(i):
                    for g2 in range(2):
                        def bank(b):
                            if isinstance(i, int) and i == 0:
                                if g2 and b == 0:
                                    pe.wait_ge(acts_ready, C * aset + 8)
                            else:
                                pe.wait_ge(up_evac, i * 8 + (32 * layer + 4 * (g2 - 2) + b + 1))
                        wait = after_set(C * aset + 7, C * aset + 8) if isinstance(i, int) and i == 0 and g2 == 0 else None
                        group(i * 4 + (u_up + 2 * g2), g2, acts, True, wait, bank)

                pair(0)
                with pe.Fori(1, UPG // 2) as i:
                    pair(i)
                for n in range(2):
                    def down_unit(j, s, first=False, last=False, bank=None):
                        pe.wait_ge(down_ready, j * 2 + (DU * layer + KU * n + s + 1))
                        unit(j * 2 + (u_down + KU * n + s), s, 4 * n, tuple(t[:, UC * s:UC * s + UC] for t in acts), False,
                             first, last, bank)

                    down_unit(0, 0, first=True, bank=lambda b: pe.wait_ge(up_evac, 32 * layer + 24 + 4 * n + b + 1))
                    down_unit(0, 1)
                    with pe.Fori(1, KU // 2 - 1) as j:
                        down_unit(j, 0)
                        down_unit(j, 1)
                    down_unit(KU // 2 - 1, 0)
                    down_unit(KU // 2 - 1, 1, last=True)

            mlp(0, TURN_X1, SET_X1, U_UP, U_DOWN)

            turn(TURN_X2, x_sb)

            def rope_turn(G):
                for t in range(T):
                    pe.wait_ge(rope_ready, 4 * (G - G_Q2) + t + 1)
                    for h in range(4):
                        mm = pe.transpose(ps[:, 4 * (G % 2) + t, P * h:P * h + P], roped[:, t, P * h:P * h + P], ident[:])
                    mm.then_inc(rope_turned, 1)

            xq = (xq_hi, xq_lo)
            group(U_Q2, 0, xq, False, lambda s: pe.wait_ge(acts_ready, C * SET_Q + 15))
            group(U_Q2 + 2, 1, xq, False, unit_wait=lambda s: pe.wait_ge(acts_ready, C * SET_Q + 16),
                  between=lambda: rope_turn(G_Q2))
            for n in range(4):
                group(U_K2 + 2 * n, n % 2, acts, False,
                      bank_wait=lambda b: pe.wait_ge(qk_ready, 4 * n + b + 1),
                      between=(lambda: rope_turn(G_K2 - 1 + n)) if n < 3 else None)

            steps = [(J, h) for J in reversed(range(T)) for h in range(A_HEADS)]

            def scores(i):
                J, h = steps[i]
                n = P * (J + 1)
                if i == 0:
                    pe.wait_ge(v_ready, T)
                elif i >= 2:
                    pe.wait_ge(exp_ready, 2 * (i - 1))
                qs = slice(P * J, P * J + P)
                rows = [slice(A_DIM * m, A_DIM * m + A_DIM) for m in range(2)]
                for part, (a_, b_) in enumerate(((q_hi, k_hi), (q_hi, k_lo), (q_lo, k_hi))):
                    for m in range(2):
                        pe.matmul(ps[:, 2 * (i % 2) + m, 0:n], a_[rows[m], h, qs], b_[rows[m], h, 0:n],
                                  start=(part == 0), stop=False)
                for m in range(2):
                    mm = pe.matmul(ps[:, 2 * (i % 2) + m, P * J:n], ident_r[:], mask_ts[:], start=False, stop=True)
                mm.then_inc(scores_done, 1)

            def turn_diff(i):
                J, h = steps[i]
                pe.wait_ge(diff_ready, i + 1)
                if i == 0:
                    pe.wait_ge(v_ready, 2 * T)
                elif i >= 2:
                    pe.wait_ge(pt_ready, i - 1)
                for k in range(J + 1):
                    mm = pe.transpose(ps[:, 4 + i % 2, P * k:P * k + P], pdiff[:, i % 2, P * k:P * k + P], ident[:])
                mm.then_inc(pt_done, 1)

            def values(i):
                J, h = steps[i]
                pe.wait_ge(pt_ready, i + 1)
                if h == 0 and i:
                    pe.wait_ge(o_copied, 2 * (i // A_HEADS))
                out_ = ps[:, 6 + h // 4, P * (h % 4):P * (h % 4) + P]
                for k in range(J + 1):
                    hi, lo = pt_hi[:, i % 2, P * k:P * k + P], pt_lo[:, i % 2, P * k:P * k + P]
                    hs = slice(P * h, P * h + P)
                    mm = three(out_, hi, lo, v_hi[:, k, hs], v_lo[:, k, hs], k == 0, k == J)
                mm.then_inc(o_done, 1)

            scores(0)
            for i in range(len(steps)):
                if i + 1 < len(steps):
                    scores(i + 1)
                turn_diff(i)
                if i >= 1:
                    values(i - 1)
            values(len(steps) - 1)
            turn(TURN_YA, o_nat)
            two_groups(U_OUT2, SET_YA, (q_hi, q_lo))
            mlp(1, TURN_X3, SET_X3, U_UP2, U_DOWN2)


INPUTS = ("x", "positions", "norm_g", "a_w_in", "a_b_gates", "a_g_head", "a_w_out", "kv_norm_g", "w_kv",
          "b_w_q", "b_lam", "b_g_head", "b_w_out", "mlp_w_up", "mlp_w_down")


def kernel(**inputs):
    import concourse.bacc as bacc
    from concourse.bass_utils import run_bass_kernel_spmd

    nc = bacc.Bacc("TRN2", target_bir_lowering=False, num_devices=1)
    arrays = {f"in_{name}": np.ascontiguousarray(inputs[name]) for name in INPUTS}
    freq = 1.0 / (np.float32(10000.0) ** (np.arange(0, A_DIM, 2, dtype=np.float32) / np.float32(A_DIM)))
    arrays["inv_freq"] = freq.astype(np.float32).reshape(1, HALF)
    args = [nc.dram_tensor(n, a.shape, mybir.dt.from_np(a.dtype), kind="ExternalInput").ap() for n, a in arrays.items()]
    out = nc.dram_tensor("out", (1, SEQ, D_MODEL), F32, kind="ExternalOutput").ap()
    trunk(nc, *args, out)
    result = run_bass_kernel_spmd(nc, [arrays], core_ids=[0])
    return result.results[0]["out"]
```

```python
import math
from contextlib import ExitStack

import numpy as np

import concourse.bass as bass
from concourse import mybir

F32 = mybir.dt.float32
F32R = mybir.dt.float32r
I32 = mybir.dt.int32
ALU = mybir.AluOpType
ACT = mybir.ActivationFunctionType
AX = mybir.AxisListType

P = 128
SEQ, D_MODEL, D_FF = 512, 1024, 4096
T = SEQ // P
C = D_MODEL // P
COLS = 512
UC = 4
EPS = 1e-6
MASKED = -1e30

M_HEADS, M_V, M_QK = 4, 256, 128
CAP = 15.0
VW = M_V + 2
BLK = T * (T + 1) // 2
A_HEADS, A_DIM = 8, 64
HALF = A_DIM // 2
LAM_INIT = 0.8 - 0.6 * math.exp(-0.3)

U_QK, U_V, U_O, U_OUT, U_UP, U_DOWN = 0, 4, 8, 12, 16, 32
U_Q2, U_K2, U_V2, U_OUT2, U_UP2, U_DOWN2, UNITS = 48, 52, 56, 60, 64, 80, 96
G_QK, G_V, G_O, G_OUT, G_UP, G_DOWN = 0, 2, 4, 6, 8, 16
G_Q2, G_K2, G_V2, G_OUT2, G_UP2, G_DOWN2 = 18, 20, 22, 24, 26, 34
UPG = D_FF // COLS
DU = 16
KU = D_FF // (UC * P)
TURN_X0, TURN_YM, TURN_X1, TURN_X2, TURN_YA, TURN_X3 = range(6)
GC_AHEAD, GC_KV, GC_BHEAD = 64, 72, 80
GROWS = 88
KSTART = (0, 512, 1024, 896)
TWO_PI = (6.28125, 0.0019340515136718750, 1.2554228305816650390625e-06, 2.1219957914e-11)


def trunk(nc, x, positions, norm_g, a_w_in, a_b_gates, a_g_head, a_w_out, kv_norm_g, w_kv, b_w_q,
          b_lam, b_g_head, b_w_out, mlp_w_up, mlp_w_down, inv_freq, out):
    def chunks(w):
        return w.rearrange("(c p) n -> p c n", p=P)

    w_in, w_out = chunks(a_w_in[0]), chunks(a_w_out[0])
    w_q2, w_kv2, w_out2 = chunks(b_w_q[0]), chunks(w_kv), chunks(b_w_out[0])
    w_up = [chunks(mlp_w_up[n]) for n in range(2)]
    w_down = [chunks(mlp_w_down[n]) for n in range(2)]
    x_rows = x[0].rearrange("(t p) d -> t p d", p=P)
    out_rows = out[0].rearrange("(t p) d -> t p d", p=P)

    with ExitStack() as ctx:
        base = nc.sbuf_base
        at = [(base + 63) // 64 * 64]

        def place(name, shape, dtype, offset=None):
            size = int(np.prod(shape[1:])) * 4
            if offset is None:
                offset = at[0]
                at[0] += (size + 31) // 32 * 32
            return nc.alloc_sbuf_tensor_at(name, shape, dtype, offset=offset)

        def sem(name):
            return ctx.enter_context(nc.semaphore(name))

        x_sb = place("x_sb", [P, T, D_MODEL], F32)
        wraw = place("wraw", [P, 2, UC, COLS], F32)
        whi = place("whi", [P, 2, UC, COLS], F32R)
        wlo = place("wlo", [P, 2, UC, COLS], F32R)
        KB = 1024
        ra = at[0]
        at[0] += 32 * KB
        act_hi = place("act_hi", [P, C, SEQ], F32R, ra)
        act_lo = place("act_lo", [P, C, SEQ], F32R, ra + 16 * KB)
        decay = place("decay", [P, 2, BLK * P], F32, ra)
        p_hi = place("p_hi", [P, 2, BLK * P], F32R, ra + 10 * KB)
        p_lo = place("p_lo", [P, 2, BLK * P], F32R, ra + 20 * KB)
        o_nat = place("o_nat", [P, T, D_MODEL], F32, ra)
        probs = place("probs", [P, 2, 2, SEQ], F32, ra + 16 * KB)
        pt_hi = place("pt_hi", [P, 2, SEQ], F32R, ra + 24 * KB)
        pt_lo = place("pt_lo", [P, 2, SEQ], F32R, ra + 28 * KB)
        ru = at[0]
        at[0] += 65 * KB
        u_sq = place("u_sq", [P, D_FF // P, SEQ], F32, ru)
        mq_hi = place("mq_hi", [P, M_HEADS, SEQ], F32R, ru)
        mq_lo = place("mq_lo", [P, M_HEADS, SEQ], F32R, ru + 8 * KB)
        mk_hi = place("mk_hi", [P, M_HEADS, SEQ], F32R, ru + 16 * KB)
        mk_lo = place("mk_lo", [P, M_HEADS, SEQ], F32R, ru + 24 * KB)
        mv_hi = place("mv_hi", [P, T, M_HEADS, VW], F32R, ru + 32 * KB)
        mv_lo_at = ru + 32 * KB + T * M_HEADS * VW * 4
        mv_end = mv_lo_at + T * M_HEADS * VW * 4
        mv_lo = place("mv_lo", [P, T, M_HEADS, VW], F32R, mv_lo_at)
        q_hi = place("q_hi", [P, A_HEADS, SEQ], F32R, ru)
        q_lo = place("q_lo", [P, A_HEADS, SEQ], F32R, ru + 16 * KB)
        k_hi = place("k_hi", [P, A_HEADS, SEQ], F32R, ru + 32 * KB)
        k_lo = place("k_lo", [P, A_HEADS, SEQ], F32R, ru + 48 * KB)
        re = at[0]
        at[0] += 32 * KB
        y_nat = place("y_nat", [P, T, D_MODEL], F32, re)
        rg = re + 16 * KB
        g_raw = place("g_raw", [2 * M_HEADS, SEQ], F32, rg)
        f_raw = place("f_raw", [M_HEADS, SEQ], F32, rg + 2 * KB)
        sp_row = place("sp_row", [M_HEADS, SEQ], F32, rg + 4 * KB)
        b_row = place("b_row", [M_HEADS, SEQ], F32, rg + 6 * KB)
        m_row = place("m_row", [M_HEADS, SEQ], F32, rg + 8 * KB)
        a_row = place("a_row", [M_HEADS, SEQ], F32, rg + 10 * KB)
        e_row = place("e_row", [M_HEADS, SEQ], F32, rg + 12 * KB)
        junk_m = place("junk_m", [P, M_V], F32, rg + 10 * KB)
        r_row = place("r_row", [M_HEADS, BLK * P], F32, re)
        r_hi = place("r_hi", [M_HEADS, BLK * P], F32R, rg)
        r_lo = place("r_lo", [M_HEADS, BLK * P], F32R, rg + 5 * KB)
        sel = place("sel", [M_HEADS, M_HEADS, P], F32, rg + 14 * KB)
        v_hi = place("v_hi", [P, T, D_MODEL], F32R, re)
        v_lo = place("v_lo", [P, T, D_MODEL], F32R, re + 16 * KB)
        roped = place("roped", [P, T, COLS], F32, re)
        relu_t = place("relu_t", [P, 2, COLS], F32, re)
        yg = place("yg", [P, T, D_MODEL], F32, re + 16 * KB)
        gpost = place("gpost", [P, D_MODEL], F32)
        rs = at[0]
        at[0] += 4 * KB
        scr_a = place("scr_a", [P, COLS], F32, rs)
        scr_b = place("scr_b", [P, COLS], F32, rs + 2 * KB)
        pdiff = place("pdiff", [P, 2, SEQ], F32, rs)
        lam_in = place("lam_in", [P, 4, A_DIM], F32, rs)
        lam_pr = place("lam_pr", [P, 2, A_DIM], F32, rs + 1 * KB)
        ang = place("ang", [P, 2, T, HALF], F32, rs + 2 * KB)
        turns = place("turns", [P, 2, T, HALF], F32, rs + 3 * KB)
        rj = at[0]
        junk = place("junk", [P, COLS], F32)
        sel_r = place("sel_r", [M_HEADS, M_HEADS, P], F32R, rj)
        ident = place("ident", [P, P], F32)
        ident_r = place("ident_r", [P, P], F32R)
        mask_st = place("mask_st", [P, P], F32R)
        mask_ts = place("mask_ts", [P, P], F32R)
        grows = place("grows", [GROWS, P], F32, mv_end)
        gcols = place("gcols", [P, GROWS], F32)
        wg_raw = place("wg_raw", [P, C, 8], F32, mv_lo_at)
        wg_hi = place("wg_hi", [P, C, 8], F32R, mv_lo_at + 256)
        wg_lo = place("wg_lo", [P, C, 8], F32R, mv_lo_at + 512)
        gate_b = place("gate_b", [8, 1], F32, mv_lo_at + 768)
        gate_b15 = place("gate_b15", [8, 1], F32, mv_lo_at + 800)
        pos_i = place("pos_i", [P, T], I32)
        pos_f = place("pos_f", [P, T], F32)
        inv = place("inv", [P, HALF], F32)
        trig = place("trig", [P, 2, T, HALF], F32)
        lam_s = place("lam_s", [P, 2], F32)
        lam_e = place("lam_e", [P, 2], F32)
        lam2 = place("lam2", [P, 2], F32)
        ssq = place("ssq", [P, T, 2], F32)
        bias0 = place("bias0", [P, T], F32)
        rms = place("rms", [P, T], F32)
        fac = place("fac", [P, T], F32)
        ssx = place("ssx", [P, T], F32)
        rmsx = place("rmsx", [P, T], F32)
        rx = place("rx", [P, T], F32)
        rx2 = place("rx2", [P, T], F32)
        rx4 = place("rx4", [P, T], F32)
        dcum = place("dcum", [M_HEADS, T, T], F32)
        carry = place("carry", [M_HEADS, T], F32)
        acol = place("acol", [P, 2 * T, M_HEADS], F32)
        den = place("den", [P, T, M_HEADS], F32)
        den2 = place("den2", [P, T, M_HEADS], F32)
        mss = place("mss", [P, T, M_HEADS], F32)
        mfac = place("mfac", [P, T, M_HEADS], F32)
        smax = place("smax", [P, 2, 2], F32)
        nmax = place("nmax", [P, 2, 2], F32)
        lsum = place("lsum", [P, 2, 2], F32)
        linv = place("linv", [P, 2, 2], F32)
        oss = place("oss", [P, T, A_HEADS], F32)
        orms = place("orms", [P, T, A_HEADS], F32)
        epsc = place("epsc", [P, 1], F32)
        assert at[0] <= nc.sbuf_usable_end, at[0]

        ps = ctx.enter_context(nc.psum_tensor("ps", [P, 8, COLS], F32))

        x_in = [sem(f"x_in{t}") for t in range(T)]
        grows_in, gate_in, pos_in, lam_in_s = (sem(n) for n in ("grows_in", "gate_in", "pos_in", "lam_in"))
        gpost_in = sem("gpost_in")
        raw_loaded = [sem(f"raw_loaded{s}") for s in range(2)]
        gained = sem("gained")
        whi_ready, weights_ready, unit_used = sem("whi_ready"), sem("weights_ready"), sem("unit_used")
        bank_done = sem("bank_done")
        consts_ready, gcols_turned, gcols_ready = sem("consts_ready"), sem("gcols_turned"), sem("gcols_ready")
        consts_r_ready = sem("consts_r_ready")
        nat_ready, turned = sem("nat_ready"), sem("turned")
        acts_hi, acts_ready = sem("acts_hi"), sem("acts_ready")
        act_self, dve_self = sem("act_self"), sem("dve_self")
        sq0, sq1, rms_ready = sem("sq0"), sem("sq1"), sem("rms_ready")
        bias0_ready = sem("bias0_ready")
        rmsx_ready, rx_ready = sem("rmsx_ready"), sem("rx_ready")
        gw_scaled, gw_hi, gw_ready, gates_done = sem("gw_scaled"), sem("gw_hi"), sem("gw_ready"), sem("gates_done")
        tanh_ready, f_rows_in = sem("tanh_ready"), sem("f_rows_in")
        sp_ready, mneg_ready, e_ready = sem("sp_ready"), sem("mneg_ready"), sem("e_ready")
        rows_ready, r_hi_ready = sem("rows_ready"), sem("r_hi_ready")
        acol_turned, acol_ready = sem("acol_turned"), sem("acol_ready")
        m_hi, m_evac = sem("m_hi"), sem("m_evac")
        ones_ready = sem("ones_ready")
        sig_ready = sem("sig_ready")
        bcast_done, decay_ready, s_done = sem("bcast_done"), sem("decay_ready"), sem("s_done")
        p_ready, p_hi_ready, p_lo_ready = sem("p_ready"), sem("p_hi_ready"), sem("p_lo_ready")
        linv_ready, e2_scaled = sem("linv_ready"), sem("e2_scaled")
        av_done, av_sq, av_evac = sem("av_done"), sem("av_sq"), sem("av_evac")
        mvar_ready, mstd_ready = sem("mvar_ready"), sem("mstd_ready")
        relu_ready, up_evac = sem("relu_ready"), sem("up_evac")
        down_hi, down_ready = sem("down_hi"), sem("down_ready")
        ang_ready, trig_ready = sem("ang_ready"), sem("trig_ready")
        lams_ready, lame_ready = sem("lams_ready"), sem("lame_ready")
        rope_ready, rope_turned, qk_hi, qk_ready = sem("rope_ready"), sem("rope_turned"), sem("qk_hi"), sem("qk_ready")
        v_hi_s, v_ready = sem("v_hi_s"), sem("v_ready")
        scores_done, max_ready, exp_ready = sem("scores_done"), sem("max_ready"), sem("exp_ready")
        diff_ready, pt_done, pt_hi_s, pt_ready = sem("diff_ready"), sem("pt_done"), sem("pt_hi_s"), sem("pt_ready")
        o_done, o_copied, ovar_ready, ostd_ready = sem("o_done"), sem("o_copied"), sem("ovar_ready"), sem("ostd_ready")
        o_squared, o_summed = sem("o_squared"), sem("o_summed")
        stored = sem("stored")

        def wait_bank(eng, G, b):
            if b < 3:
                eng.wait_ge(bank_done, 3 * G + b + 1)
            elif G < G_DOWN:
                eng.wait_ge(unit_used, 2 * G + 2)
            elif G < G_Q2:
                eng.wait_ge(unit_used, U_DOWN + KU * (G - G_DOWN + 1))
            elif G < G_DOWN2:
                eng.wait_ge(unit_used, U_Q2 + 2 * (G - G_Q2) + 2)
            else:
                eng.wait_ge(unit_used, U_DOWN2 + KU * (G - G_DOWN2 + 1))

        def is_gained(u):
            return u < U_DOWN or U_Q2 <= u < U_DOWN2

        def n_gained(u):
            return u + 1 if u < U_DOWN else u + 1 - DU

        def gain_col(u):
            for last, col in ((U_OUT, 0), (U_UP, GC_AHEAD), (U_DOWN, 8 * 2), (U_K2, 8 * 4), (U_OUT2, GC_KV),
                              (U_UP2, GC_BHEAD), (U_DOWN2, 8 * 6)):
                if u < last:
                    return col + UC * (u % 2)

        order = [tuple(range(T))] * 6
        order[TURN_YA] = (1, 3, 2, 0)

        block = ctx.enter_context(nc.Block())

        @block.sync
        def _(sp):
            def load(u, s, src):
                if not (isinstance(u, int) and u < 2):
                    sp.wait_ge(weights_ready, u - 1)
                sp.dma_start(wraw[:, s], src).then_inc(raw_loaded[s], 16)

            def short_stage(u0, w, col0, groups):
                for g in range(groups):
                    for s in range(2):
                        load(u0 + 2 * g + s, s, w[:, UC * s:UC * s + UC, col0 + g * COLS:col0 + (g + 1) * COLS])

            def mlp(layer, u_up, u_down):
                w1, w2 = w_up[layer], w_down[layer]
                with sp.Fori(0, UPG) as g:
                    for s in range(2):
                        load(g * 2 + (u_up + s), s, w1[:, UC * s:UC * s + UC, bass.ds(g * COLS, COLS)])
                load_gpost(2 * layer + 1, layer, 3)
                for n in range(2):
                    with sp.Fori(0, KU // 2) as j:
                        for s in range(2):
                            load(j * 2 + (u_down + KU * n + s), s,
                                 w2[:, bass.ds(j * (2 * UC) + UC * s, UC), n * COLS:(n + 1) * COLS])

            def load_gpost(n, layer, i):
                if n:
                    sp.wait_ge(nat_ready, T * (TURN_X1, TURN_X2, TURN_X3)[n - 1] + T)
                sp.dma_start(gpost[:], norm_g[layer, i:i + 1, :].to_broadcast([P, D_MODEL])).then_inc(gpost_in, 16)

            sp.dma_start(grows[0:64, :], norm_g.rearrange("l i (c p) -> (l i c) p", p=P)).then_inc(grows_in, 16)
            sp.dma_start(x_sb[:, 0], x_rows[0]).then_inc(x_in[0], 16)
            sp.dma_start(grows[64:72, :], a_g_head.rearrange("l (c p) -> (l c) p", p=P)).then_inc(grows_in, 16)
            sp.dma_start(grows[72:80, :], kv_norm_g.rearrange("(c p) -> c p", p=P)).then_inc(grows_in, 16)
            sp.dma_start(grows[80:88, :], b_g_head.rearrange("l (c p) -> (l c) p", p=P)).then_inc(grows_in, 16)
            sp.dma_start(x_sb[:, 1], x_rows[1]).then_inc(x_in[1], 16)
            load(0, 0, w_in[:, 0:UC, 0:COLS])
            for t in range(2, T):
                sp.dma_start(x_sb[:, t], x_rows[t]).then_inc(x_in[t], 16)
            load(1, 1, w_in[:, UC:2 * UC, 0:COLS])
            sp.dma_start(wg_raw[:], w_in[:, :, 3 * D_MODEL:3 * D_MODEL + 8]).then_inc(gate_in, 16)
            sp.dma_start(gate_b[:], a_b_gates.rearrange("l g -> g l")).then_inc(gate_in, 16)
            load_gpost(0, 0, 1)
            sp.dma_start(pos_i[:], positions[0].rearrange("(t p) -> p t", p=P), allow_slow_non_contiguous=True).then_inc(pos_in, 16)
            sp.dma_start(inv[:], inv_freq.to_broadcast([P, HALF])).then_inc(pos_in, 16)
            short_stage(U_QK + 2, w_in, COLS, 1)
            sp.wait_ge(tanh_ready, 1)
            sp.dma_start(f_raw[:], g_raw[M_HEADS:2 * M_HEADS, :]).then_inc(f_rows_in, 16)
            short_stage(U_V, w_in, D_MODEL, 4)
            short_stage(U_OUT, w_out, 0, 2)
            mlp(0, U_UP, U_DOWN)
            sp.dma_start(lam_in[:], b_lam.rearrange("l a d -> l (a d)").to_broadcast([P, 4 * A_DIM])).then_inc(lam_in_s, 16)
            short_stage(U_Q2, w_q2, 0, 2)
            load_gpost(2, 1, 1)
            short_stage(U_K2, w_kv2, 0, 4)
            short_stage(U_OUT2, w_out2, 0, 2)
            mlp(1, U_UP2, U_DOWN2)
            for t in range(T):
                sp.wait_ge(nat_ready, 6 * T + t + 1)
                sp.dma_start(out_rows[t], x_sb[:, t]).then_inc(stored, 16)
            sp.wait_ge(stored, 16 * T)

        @block.gpsimd
        def _(pool):
            g = nc.gpsimd
            g.memset(ident[:], 0.0).then_inc(consts_ready, 1)
            pool.wait_ge(consts_ready, 1)
            g.affine_select(out=ident[:], in_=ident[:], compare_op=ALU.not_equal, fill=1.0, base=0,
                            pattern=[[-1, P]], channel_multiplier=1).then_inc(consts_ready, 1)
            g.memset(sel[:], 0.0).then_inc(consts_ready, 1)
            pool.wait_ge(consts_ready, 3)
            g.affine_select(out=sel[:], in_=sel[:], compare_op=ALU.not_equal, fill=1.0, base=0,
                            pattern=[[-1, M_HEADS], [0, P]], channel_multiplier=1).then_inc(consts_ready, 1)
            g.memset(scr_a[:, 0:2 * P], 0.0).then_inc(consts_ready, 1)
            pool.wait_ge(consts_ready, 5)
            g.affine_select(out=scr_a[:, 0:P], in_=scr_a[:, 0:P], compare_op=ALU.is_ge, fill=MASKED, base=0,
                            pattern=[[1, P]], channel_multiplier=-1).then_inc(consts_ready, 1)
            g.affine_select(out=scr_a[:, P:2 * P], in_=scr_a[:, P:2 * P], compare_op=ALU.is_ge, fill=MASKED, base=0,
                            pattern=[[-1, P]], channel_multiplier=1).then_inc(consts_ready, 1)

            def lo_part(u, s):
                pool.wait_ge(whi_ready, u + 1)
                g.tensor_tensor(wlo[:, s], wraw[:, s], whi[:, s].bitcast(F32), ALU.subtract).then_inc(weights_ready, 1)

            with pool.Fori(0, U_OUT2 // 2 + 1) as j:
                for s in range(2):
                    lo_part(j * 2 + s, s)
            for q in range(T):
                for b in range(2):
                    pool.wait_ge(o_copied, 2 * q + b + 1)
                    if q or b:
                        pool.wait_ge(o_summed, 2 * q + b)
                    part = o_nat[:, T - 1 - q, b * COLS:(b + 1) * COLS]
                    g.tensor_tensor(junk[:], part, part, ALU.mult).then_inc(o_squared, 1)
            with pool.Fori(U_OUT2 // 2 + 1, UNITS // 2) as j:
                for s in range(2):
                    lo_part(j * 2 + s, s)

        @block.scalar
        def _(act):
            a = nc.scalar
            own = [0]

            def done(ins):
                own[0] += 1
                ins.then_inc(act_self, 1)
                act.wait_ge(act_self, own[0])

            def w_hi(u):
                s = u % 2
                if u < UNITS:
                    if is_gained(u):
                        act.wait_ge(gained, n_gained(u))
                    else:
                        act.wait_ge(raw_loaded[s], 16 * (u // 2 + 1))
                    if u >= 2:
                        act.wait_ge(unit_used, u - 1)
                    a.activation(whi[:, s], wraw[:, s], ACT.Copy).then_inc(whi_ready, 1)

            def w_hi_at(j, u0, s):
                if isinstance(j, int):
                    return w_hi(u0 + 2 * j + s)
                if is_gained(u0):
                    act.wait_ge(gained, j * 2 + (n_gained(u0) + s))
                else:
                    act.wait_ge(raw_loaded[s], j * 16 + 16 * (u0 // 2 + 1))
                act.wait_ge(unit_used, j * 2 + (u0 + s - 1))
                a.activation(whi[:, s], wraw[:, s], ACT.Copy).then_inc(whi_ready, 1)

            def tile_hi(turn, t, dst):
                for j in range(2):
                    act.wait_ge(turned, T * turn + order[turn].index(t) + 1)
                    a.activation(dst[:, 4 * j:4 * j + 4, P * t:P * t + P],
                                 ps[:, 4 * j + t].rearrange("p (c k) -> p c k", c=4), ACT.Copy).then_inc(acts_hi, 1)

            def x_squares(t, first):
                if first:
                    act.wait_ge(x_in[t], 16)
                done(a.activation(y_nat[:, t] if first else yg[:, 0], x_sb[:, t], ACT.Square, accum_out=ssx[:, t:t + 1]))
                a.activation(rmsx[:, t:t + 1], ssx[:, t:t + 1], ACT.Sqrt, scale=1.0 / D_MODEL,
                             bias=epsc[:, 0:1]).then_inc(rmsx_ready, 1)

            def first_squares(n, G):
                for t in range(T):
                    wait_bank(act, G, t)
                    a.activation(junk[:], ps[:, t], ACT.Square, accum_out=ssq[:, t, 0:1]).then_inc(sq0, 1)
                    act.wait_ge(sq0, T * n + t + 1)

            def norm_root(n, G, t, mlp):
                wait_bank(act, G + 1, t)
                a.activation(junk[:], ps[:, 4 + t], ACT.Square, accum_out=ssq[:, t, 1:2]).then_inc(sq1, 1)
                act.wait_ge(sq1, T * n + t + 1)
                act.wait_ge(bias0_ready, T * n + t + 1)
                a.activation(rms[:, t:t + 1], ssq[:, t, 1:2], ACT.Sqrt,
                             scale=rx4[:, t:t + 1] if mlp else 1.0 / D_MODEL,
                             bias=bias0[:, t:t + 1]).then_inc(rms_ready, 1)

            def norm_and_turn(n, G, mlp, turn, u_next):
                for t in range(3):
                    norm_root(n, G, t, mlp)
                tile_hi(turn, 0, act_hi)
                norm_root(n, G, 3, mlp)
                tile_hi(turn, 1, act_hi)
                tile_hi(turn, 2, act_hi)
                w_hi(u_next + 1)
                tile_hi(turn, 3, act_hi)
                x_stats(turn)

            def x_stats(turn):
                for t in range(T):
                    act.wait_ge(nat_ready, T * turn + t + 1)
                    x_squares(t, False)

            act.wait_ge(gcols_ready, 1)
            x_squares(0, True)
            x_squares(1, True)
            tile_hi(TURN_X0, 0, act_hi)
            tile_hi(TURN_X0, 1, act_hi)
            w_hi(0)
            x_squares(2, True)
            x_squares(3, True)
            tile_hi(TURN_X0, 2, act_hi)
            tile_hi(TURN_X0, 3, act_hi)
            w_hi(1)
            act.wait_ge(consts_ready, 7)
            a.activation(ident_r[:], ident[:], ACT.Copy).then_inc(consts_r_ready, 1)
            a.activation(sel_r[:], sel[:], ACT.Copy).then_inc(consts_r_ready, 1)
            a.activation(mask_st[:], scr_a[:, 0:P], ACT.Copy).then_inc(consts_r_ready, 1)
            a.activation(mask_ts[:], scr_a[:, P:2 * P], ACT.Copy).then_inc(consts_r_ready, 1)
            act.wait_ge(gw_scaled, 1)
            a.activation(wg_hi[:], wg_raw[:], ACT.Copy).then_inc(gw_hi, 1)
            w_hi(2)
            w_hi(3)
            for h in range(M_HEADS):
                wait_bank(act, G_QK, h)
                a.activation(mq_hi[:, h], ps[:, h], ACT.Copy).then_inc(m_hi, 1)
            act.wait_ge(gates_done, 1)
            act.wait_ge(gw_ready, 2)
            a.activation(g_raw[:], ps[0:8, 4], ACT.Tanh, scale=1.0 / CAP, bias=gate_b15[:, 0:1]).then_inc(tanh_ready, 1)
            act.wait_ge(f_rows_in, 16)
            done(a.activation(e_row[:], f_raw[:], ACT.Exp, scale=-CAP))
            a.activation(sp_row[:], e_row[:], ACT.Ln, bias=1.0).then_inc(sp_ready, 1)
            w_hi(4)
            act.wait_ge(mneg_ready, 1)
            a.activation(e_row[:], b_row[:], ACT.Exp).then_inc(e_ready, 1)
            act.wait_ge(rows_ready, 1)
            a.activation(r_hi[:], r_row[:], ACT.Copy).then_inc(r_hi_ready, 1)
            w_hi(5)
            for h in range(M_HEADS):
                wait_bank(act, G_QK + 1, h)
                a.activation(mk_hi[:, h], ps[:, 4 + h], ACT.Copy, scale=M_QK ** -0.5).then_inc(m_hi, 1)
            for g in range(2):
                w_hi(U_V + 2 * g + 2)
                w_hi(U_V + 2 * g + 3)
                for t in range(T):
                    wait_bank(act, G_V + g, t)
                    a.activation(mv_hi[:, t, 2 * g:2 * g + 2, 0:M_V],
                                 ps[:, 4 * g + t].rearrange("p (h e) -> p h e", h=2), ACT.Copy).then_inc(m_hi, 1)
            for g in range(2):
                w_hi(U_O + 2 * g + 2)
                if g == 0:
                    w_hi(U_O + 2 * g + 3)
                for t in range(T):
                    wait_bank(act, G_O + g, t)
                    a.activation(y_nat[:, t, g * COLS:(g + 1) * COLS], ps[:, 4 * g + t], ACT.Sigmoid).then_inc(sig_ready, 1)
            act.wait_ge(acol_ready, 1)

            def head_decay(h, k):
                w = P * (T - k)
                act.wait_ge(bcast_done, T * h + T)
                if h >= 2:
                    act.wait_ge(p_lo_ready, T * (h - 2) + k + 1)
                b, o = divmod(KSTART[k], COLS)
                a.activation(decay[:, h % 2, KSTART[k]:KSTART[k] + w], ps[:, b, o:o + w], ACT.Exp,
                             bias=acol[:, k, h:h + 1]).then_inc(decay_ready, 1)

            def head_hi(h, k):
                act.wait_ge(p_ready, T * h + k + 1)
                if h >= 2:
                    act.wait_ge(av_done, T * (h - 1))
                sl = slice(KSTART[k], KSTART[k] + P * (T - k))
                a.activation(p_hi[:, h % 2, sl], decay[:, h % 2, sl], ACT.Copy).then_inc(p_hi_ready, 1)

            def head_squares(h, J):
                n = T * h + J
                act.wait_ge(av_done, n + 1)
                if n:
                    act.wait_ge(av_sq, n)
                a.activation(junk_m[:], ps[:, 6 + J % 2, 0:M_V], ACT.Square, accum_out=mss[:, J, h:h + 1]).then_inc(av_sq, 1)

            for h in range(M_HEADS):
                for k in range(T):
                    head_decay(h, k)
                    if h:
                        head_squares(h - 1, k)
                if h == 0:
                    w_hi(U_OUT + 1)
                for k in range(T):
                    head_hi(h, k)
            for k in range(T):
                head_squares(M_HEADS - 1, k)
            act.wait_ge(mvar_ready, 1)
            a.activation(mfac[:], mss[:], ACT.Sqrt, scale=1.0 / M_V, bias=epsc[:, 0:1]).then_inc(mstd_ready, 1)
            for t in range(T):
                tile_hi(TURN_YM, t, act_hi)
            w_hi(U_OUT + 2)
            w_hi(U_OUT + 3)
            first_squares(0, G_OUT)
            w_hi(U_UP)
            norm_and_turn(0, G_OUT, False, TURN_X1, U_UP)

            def mlp(layer, u_up, u_down, G_up, G_down, n_post):
                def relus(i, g2):
                    for b in range(4):
                        n = i * 8 + (4 * g2 + b)
                        if b < 3:
                            act.wait_ge(bank_done, i * 6 + (3 * (G_up + g2) + b + 1))
                        else:
                            act.wait_ge(unit_used, i * 4 + (u_up + 2 * g2 + 2))
                        if not (isinstance(n, int) and n < 2):
                            act.wait_ge(up_evac, n + (32 * layer - 1))
                        a.activation(relu_t[:, b % 2], ps[:, 4 * g2 + b], ACT.Relu).then_inc(relu_ready, 1)

                def down_part(j, n, s):
                    act.wait_ge(unit_used, j * 2 + (u_down + KU * n + s - 1))
                    if n == 0:
                        act.wait_ge(up_evac, j * 8 + (32 * layer + 4 * s + 4))
                    src = u_sq[:, 4 * s:4 * s + 4] if isinstance(j, int) and j == 0 else u_sq[:, bass.ds(j * 8 + 4 * s, 4)]
                    a.activation(act_hi[:, 4 * s:4 * s + 4], src, ACT.Copy).then_inc(down_hi, 1)

                def pair(i, last=False):
                    for g2 in range(2):
                        w_hi_at(i * 2 + g2, u_up + 2, 0)
                        if last and g2 == 1:
                            down_part(0, 0, 0)
                            w_hi_at(i * 2 + g2, u_up + 2, 1)
                            down_part(0, 0, 1)
                        else:
                            w_hi_at(i * 2 + g2, u_up + 2, 1)
                        relus(i, g2)

                pair(0)
                with act.Fori(1, UPG // 2 - 1) as i:
                    pair(i)
                pair(UPG // 2 - 1, last=True)
                for n in range(2):
                    if n:
                        for s in range(2):
                            down_part(0, n, s)
                            w_hi_at(0, u_down + KU * n, s)
                        first_squares(n_post, G_down)
                    with act.Fori(1, KU // 2) as j:
                        for s in range(2):
                            down_part(j, n, s)
                            w_hi_at(j, u_down + KU * n, s)
                w_hi(u_down + DU)

            mlp(0, U_UP, U_DOWN, G_UP, G_DOWN, 1)
            norm_and_turn(1, G_DOWN, True, TURN_X2, U_Q2)
            act.wait_ge(ang_ready, 1)
            a.activation(trig[:], ang[:], ACT.Sin).then_inc(trig_ready, 1)
            act.wait_ge(lams_ready, 1)
            a.activation(lam_e[:], lam_s[:], ACT.Exp).then_inc(lame_ready, 1)

            def rope_hi(G):
                dst = q_hi if G < G_K2 else k_hi
                for t in range(T):
                    act.wait_ge(rope_turned, 4 * (G - G_Q2) + t + 1)
                    a.activation(dst[:, 4 * (G % 2):4 * (G % 2) + 4, P * t:P * t + P],
                                 ps[:, 4 * (G % 2) + t].rearrange("p (h k) -> p h k", h=4), ACT.Copy).then_inc(qk_hi, 1)

            for G in range(G_Q2, G_V2):
                u = U_Q2 + 2 * (G - G_Q2)
                w_hi(u + 2)
                if G > G_Q2:
                    rope_hi(G - 1)
                w_hi(u + 3)
            for g in range(2):
                u = U_V2 + 2 * g
                w_hi(u + 2)
                if g == 0:
                    rope_hi(G_V2 - 1)
                w_hi(u + 3)
                for t in range(T):
                    wait_bank(act, G_V2 + g, t)
                    a.activation(v_hi[:, t, g * COLS:(g + 1) * COLS], ps[:, 4 * g + t], ACT.Copy,
                                 scale=rx[:, t:t + 1]).then_inc(v_hi_s, 1)

            steps = [(J, h) for J in reversed(range(T)) for h in range(A_HEADS)]

            def exps(i):
                J, h = steps[i]
                n = P * (J + 1)
                act.wait_ge(max_ready, i + 1)
                if i >= 2:
                    act.wait_ge(diff_ready, i - 1)
                for m in range(2):
                    a.activation(probs[:, i % 2, m, 0:n], ps[:, 2 * (i % 2) + m, 0:n], ACT.Exp, scale=A_DIM ** -0.5,
                                 bias=nmax[:, i % 2, m:m + 1], accum_out=lsum[:, i % 2, m:m + 1]).then_inc(exp_ready, 1)

            def scale_second(i):
                J, h = steps[i]
                n = P * (J + 1)
                act.wait_ge(linv_ready, i + 1)
                act.wait_ge(exp_ready, 2 * i + 2)
                a.activation(probs[:, i % 2, 1, 0:n], probs[:, i % 2, 1, 0:n], ACT.Copy,
                             scale=linv[:, i % 2, 1:2]).then_inc(e2_scaled, 1)

            def pt_split(i):
                J, h = steps[i]
                n = P * (J + 1)
                act.wait_ge(pt_done, i + 1)
                if i >= 2:
                    act.wait_ge(o_done, i - 1)
                a.activation(pt_hi[:, i % 2, 0:n], ps[:, 4 + i % 2, 0:n], ACT.Copy).then_inc(pt_hi_s, 1)

            def copy_o(q):
                act.wait_ge(o_done, A_HEADS * (q + 1))
                for b in range(2):
                    a.activation(o_nat[:, T - 1 - q, b * COLS:(b + 1) * COLS], ps[:, 6 + b], ACT.Copy).then_inc(o_copied, 1)

            def o_roots(n, t0, t1):
                act.wait_ge(ovar_ready, n + 1)
                a.activation(orms[:, t0:t1], oss[:, t0:t1], ACT.Sqrt, scale=1.0 / (2 * A_DIM),
                             bias=epsc[:, 0:1]).then_inc(ostd_ready, 1)

            exps(0)
            for i in range(len(steps) + 1):
                if i >= 1:
                    pt_split(i - 1)
                if i >= 10 and i % A_HEADS == 2:
                    copy_o(i // A_HEADS - 1)
                if i < len(steps):
                    scale_second(i)
                if i + 1 < len(steps):
                    exps(i + 1)
            o_roots(0, 1, T)
            copy_o(T - 1)
            tile_hi(TURN_YA, 1, q_hi)
            tile_hi(TURN_YA, 3, q_hi)
            o_roots(1, 0, 1)
            tile_hi(TURN_YA, 2, q_hi)
            tile_hi(TURN_YA, 0, q_hi)
            w_hi(U_OUT2 + 2)
            w_hi(U_OUT2 + 3)
            first_squares(2, G_OUT2)
            w_hi(U_UP2)
            norm_and_turn(2, G_OUT2, False, TURN_X3, U_UP2)
            mlp(1, U_UP2, U_DOWN2, G_UP2, G_DOWN2, 3)
            for t in range(T):
                norm_root(3, G_DOWN2, t, True)

        @block.vector
        def _(dve):
            v = nc.vector
            own = [0]

            def done(ins):
                own[0] += 1
                ins.then_inc(dve_self, 1)
                dve.wait_ge(dve_self, own[0])

            def f32(ap):
                return ap.bitcast(F32)

            def tile_lo(turn, t, hi, lo):
                for j in range(2):
                    n = order[turn].index(t)
                    dve.wait_ge(acts_hi, 2 * (T * turn + n) + j + 1)
                    cut = (slice(None), slice(4 * j, 4 * j + 4), slice(P * t, P * t + P))
                    v.tensor_tensor(lo[cut], ps[:, 4 * j + t].rearrange("p (c k) -> p c k", c=4), f32(hi[cut]),
                                    ALU.subtract).then_inc(acts_ready, 1)

            def gain(u, j=None):
                s = u % 2
                if j is None:
                    if u >= UNITS or not is_gained(u):
                        return
                    dve.wait_ge(raw_loaded[s], 16 * (u // 2 + 1))
                else:
                    dve.wait_ge(raw_loaded[s], j * 16 + 16 * (u // 2 + 1))
                for k in range(UC):
                    c = gain_col(u) + k
                    ins = v.tensor_scalar(wraw[:, s, k], wraw[:, s, k], gcols[:, c:c + 1], None, ALU.mult)
                ins.then_inc(gained, 1)

            def x_scale(n, t, last=False):
                dve.wait_ge(rmsx_ready, T * n + t + 1)
                ins = v.reciprocal(rx[:, t:t + 1], rmsx[:, t:t + 1])
                if last:
                    ins.then_inc(rx_ready, 1)
                else:
                    done(ins)

            def post_first(n, mlp):
                dve.wait_ge(gpost_in, 16 * (n + 1))
                for t in range(T):
                    dve.wait_ge(sq0, T * n + t + 1)
                    v.tensor_scalar(bias0[:, t:t + 1], ssq[:, t, 0:1], rx4[:, t:t + 1] if mlp else 1.0 / D_MODEL, EPS,
                                    ALU.mult, ALU.add).then_inc(bias0_ready, 1)
                    done(v.tensor_tensor(yg[:, t, 0:COLS], ps[:, t], gpost[:, 0:COLS], ALU.mult))

            def post_tile(n, t, mlp):
                dve.wait_ge(sq1, T * n + t + 1)
                done(v.tensor_tensor(yg[:, t, COLS:2 * COLS], ps[:, 4 + t], gpost[:, COLS:2 * COLS], ALU.mult))
                dve.wait_ge(rms_ready, T * n + t + 1)
                done(v.reciprocal(fac[:, t:t + 1], rms[:, t:t + 1]))
                if mlp:
                    done(v.tensor_tensor(fac[:, t:t + 1], fac[:, t:t + 1], rx2[:, t:t + 1], ALU.mult))
                v.scalar_tensor_tensor(out=x_sb[:, t], in0=yg[:, t], scalar=fac[:, t:t + 1], in1=x_sb[:, t],
                                       op0=ALU.mult, op1=ALU.add).then_inc(nat_ready, 1)

            def norm_and_turn(n, mlp, turn):
                for t in range(3):
                    post_tile(n, t, mlp)
                tile_lo(turn, 0, act_hi, act_lo)
                post_tile(n, 3, mlp)
                for t in range(1, T):
                    tile_lo(turn, t, act_hi, act_lo)

            done(v.memset(epsc[:], EPS))
            dve.wait_ge(gcols_turned, 1)
            v.tensor_copy(gcols[:], ps[:, 7, 0:GROWS]).then_inc(gcols_ready, 1)
            for t in range(T):
                x_scale(0, t)
                v.tensor_scalar(y_nat[:, t], x_sb[:, t], rx[:, t:t + 1], None, ALU.mult).then_inc(nat_ready, 1)
                if t == 1:
                    tile_lo(TURN_X0, 0, act_hi, act_lo)
                    tile_lo(TURN_X0, 1, act_hi, act_lo)
                    gain(0)
            tile_lo(TURN_X0, 2, act_hi, act_lo)
            tile_lo(TURN_X0, 3, act_hi, act_lo)
            gain(1)
            dve.wait_ge(gate_in, 32)
            for c in range(C):
                ins = v.tensor_scalar(wg_raw[:, c], wg_raw[:, c], gcols[:, c:c + 1], None, ALU.mult)
            ins.then_inc(gw_scaled, 1)
            v.memset(f32(mv_hi[:, :, :, M_V:VW]), 1.0).then_inc(ones_ready, 1)
            v.tensor_scalar(gcols[:, GC_BHEAD:GC_BHEAD + 8], gcols[:, GC_BHEAD:GC_BHEAD + 8], 1.0 - LAM_INIT, None,
                            ALU.mult).then_inc(gcols_ready, 1)
            dve.wait_ge(gw_hi, 1)
            v.tensor_tensor(wg_lo[:], wg_raw[:], f32(wg_hi[:]), ALU.subtract).then_inc(gw_ready, 1)
            v.tensor_scalar(gate_b15[:], gate_b[:], 1.0 / CAP, None, ALU.mult).then_inc(gw_ready, 1)
            gain(2)
            gain(3)
            for h in range(M_HEADS):
                dve.wait_ge(m_hi, h + 1)
                v.tensor_tensor(mq_lo[:, h], ps[:, h], f32(mq_hi[:, h]), ALU.subtract).then_inc(m_evac, 1)
            dve.wait_ge(sp_ready, 1)

            def blk(r, J):
                return r[:, P * J:P * J + P]

            for J in range(T):
                done(v.tensor_tensor_scan(blk(b_row, J), blk(sp_row, J), blk(sp_row, J), 0.0, ALU.add, ALU.max))
            done(v.scalar_tensor_tensor(out=a_row[:], in0=g_raw[0:M_HEADS, :], scalar=CAP, in1=b_row[:], op0=ALU.mult,
                                        op1=ALU.add))
            gain(4)
            gain(5)
            done(v.memset(carry[:], 0.0))
            done(v.memset(dcum[:], 0.0))
            for J in range(T):
                last = P * J + P - 1
                done(v.tensor_tensor_scan(blk(m_row, J), blk(a_row, J), blk(a_row, J), carry[:, J:J + 1], ALU.max, ALU.max))
                if J + 1 < T:
                    done(v.tensor_tensor(carry[:, J + 1:J + 2], m_row[:, last:last + 1], b_row[:, last:last + 1], ALU.subtract))
                    for k in range(J + 1):
                        done(v.tensor_tensor(dcum[:, k, J + 1:J + 2], dcum[:, k, J:J + 1], b_row[:, last:last + 1], ALU.add))
            for k in range(T):
                for J in range(k, T):
                    o = KSTART[k] + P * (J - k)
                    done(v.tensor_scalar(r_row[:, o:o + P], blk(m_row, J), dcum[:, k, J:J + 1], -1.0, ALU.add, ALU.mult))
            v.tensor_tensor(b_row[:], b_row[:], m_row[:], ALU.subtract).then_inc(mneg_ready, 1)
            v.engine_nop().then_inc(rows_ready, 1)
            dve.wait_ge(e_ready, 1)
            done(v.tensor_scalar(e_row[:], e_row[:], 3e38, None, ALU.min))
            dve.wait_ge(r_hi_ready, 1)
            v.tensor_tensor(r_lo[:], r_row[:], f32(r_hi[:]), ALU.subtract).then_inc(rows_ready, 1)
            for h in range(M_HEADS):
                dve.wait_ge(m_hi, M_HEADS + h + 1)
                v.scalar_tensor_tensor(out=mk_lo[:, h], in0=ps[:, 4 + h], scalar=M_QK ** -0.5, in1=f32(mk_hi[:, h]),
                                       op0=ALU.mult, op1=ALU.subtract).then_inc(m_evac, 1)
            dve.wait_ge(acol_turned, 1)
            v.tensor_copy(acol[:], ps[:, 3, 0:2 * T * M_HEADS].rearrange("p (t h) -> p t h", h=M_HEADS)).then_inc(acol_ready, 1)
            for g in range(2):
                gain(U_V + 2 * g + 2)
                gain(U_V + 2 * g + 3)
                for t in range(T):
                    dve.wait_ge(m_hi, 2 * M_HEADS + T * g + t + 1)
                    v.tensor_tensor(mv_lo[:, t, 2 * g:2 * g + 2, 0:M_V], ps[:, 4 * g + t].rearrange("p (h e) -> p h e", h=2),
                                    f32(mv_hi[:, t, 2 * g:2 * g + 2, 0:M_V]), ALU.subtract).then_inc(m_evac, 1)
            for u in range(U_O + 2, U_O + 6):
                gain(u)
            def head_product(h, k):
                sl = slice(KSTART[k], KSTART[k] + P * (T - k))
                dve.wait_ge(decay_ready, T * h + k + 1)
                dve.wait_ge(s_done, T * h + T)
                b, o = divmod(KSTART[k], COLS)
                v.tensor_tensor(decay[:, h % 2, sl], decay[:, h % 2, sl], ps[:, 3 + b, o:o + P * (T - k)],
                                ALU.mult).then_inc(p_ready, 1)

            def head_lo(h, k):
                sl = slice(KSTART[k], KSTART[k] + P * (T - k))
                dve.wait_ge(p_hi_ready, T * h + k + 1)
                v.tensor_tensor(p_lo[:, h % 2, sl], decay[:, h % 2, sl], f32(p_hi[:, h % 2, sl]),
                                ALU.subtract).then_inc(p_lo_ready, 1)

            def head_out(h, J):
                dve.wait_ge(av_sq, T * h + J + 1)
                if h == 0 and J == 0:
                    dve.wait_ge(sig_ready, 2 * T)
                sl = slice(h * M_V, (h + 1) * M_V)
                v.tensor_copy(den[:, J, h:h + 1], ps[:, 6 + J % 2, M_V:M_V + 1])
                v.tensor_tensor(y_nat[:, J, sl], y_nat[:, J, sl], ps[:, 6 + J % 2, 0:M_V], ALU.mult).then_inc(av_evac, 1)

            for h in range(M_HEADS):
                for k in range(T):
                    head_product(h, k)
                    if h:
                        head_out(h - 1, k)
                for k in range(T):
                    head_lo(h, k)
            for k in range(T):
                head_out(M_HEADS - 1, k)
            dve.wait_ge(av_evac, T * M_HEADS)
            done(v.scalar_tensor_tensor(out=den2[:], in0=den[:], scalar=-1.0, in1=den[:], op0=ALU.mult, op1=ALU.max))
            done(v.tensor_tensor(den2[:], den2[:], acol[:, T:2 * T, :], ALU.max))
            done(v.reciprocal(den[:], den2[:]))
            done(v.tensor_tensor(mss[:], mss[:], den[:], ALU.mult))
            v.tensor_tensor(mss[:], mss[:], den[:], ALU.mult).then_inc(mvar_ready, 1)
            dve.wait_ge(mstd_ready, 1)
            done(v.reciprocal(den2[:], mfac[:]))
            done(v.tensor_tensor(den2[:], den2[:], den[:], ALU.mult))
            for t in range(T):
                for h in range(M_HEADS):
                    sl = slice(h * M_V, (h + 1) * M_V)
                    ins = v.tensor_scalar(y_nat[:, t, sl], y_nat[:, t, sl], den2[:, t, h:h + 1], None, ALU.mult)
                ins.then_inc(nat_ready, 1)
                if t:
                    tile_lo(TURN_YM, t - 1, act_hi, act_lo)
            tile_lo(TURN_YM, T - 1, act_hi, act_lo)
            gain(U_OUT + 2)
            gain(U_OUT + 3)
            gain(U_UP)
            post_first(0, False)
            gain(U_UP + 1)
            norm_and_turn(0, False, TURN_X1)

            def mlp(layer, u_up, u_down, n_norm, n_post):
                gain(u_up + 2)
                for t in range(T):
                    x_scale(n_norm, t)
                done(v.tensor_tensor(rx2[:], rx[:], rx[:], ALU.mult))
                done(v.scalar_tensor_tensor(out=rx4[:], in0=rx2[:], scalar=1.0 / D_MODEL, in1=rx2[:], op0=ALU.mult,
                                            op1=ALU.mult))

                def squares(i, g2):
                    for b in range(4):
                        n = i * 8 + (4 * g2 + b)
                        dve.wait_ge(relu_ready, n + (32 * layer + 1))
                        dst = u_sq[:, n] if isinstance(n, int) else u_sq[:, bass.ds(n, 1)].rearrange("p a s -> p (a s)")
                        v.tensor_tensor(dst, relu_t[:, b % 2], ps[:, 4 * g2 + b], ALU.mult).then_inc(up_evac, 1)

                def down_part(j, n, s):
                    dve.wait_ge(down_hi, j * 2 + (DU * layer + KU * n + s + 1))
                    src = u_sq[:, 4 * s:4 * s + 4] if isinstance(j, int) and j == 0 else u_sq[:, bass.ds(j * 8 + 4 * s, 4)]
                    v.tensor_tensor(act_lo[:, 4 * s:4 * s + 4], src, f32(act_hi[:, 4 * s:4 * s + 4]),
                                    ALU.subtract).then_inc(down_ready, 1)

                gain(u_up + 3)
                squares(0, 0)
                gain(u_up + 4)
                gain(u_up + 5)
                squares(0, 1)
                with dve.Fori(1, UPG // 2 - 1) as i:
                    for g2 in range(2):
                        gain(u_up + 2 + 2 * g2, i * 2)
                        gain(u_up + 3 + 2 * g2, i * 2)
                        squares(i, g2)
                gain(u_up + 2 * UPG - 2)
                gain(u_up + 2 * UPG - 1)
                squares(UPG // 2 - 1, 0)
                down_part(0, 0, 0)
                down_part(0, 0, 1)
                squares(UPG // 2 - 1, 1)
                for n in range(2):
                    if n:
                        for s in range(2):
                            down_part(0, n, s)
                        post_first(n_post, True)
                    with dve.Fori(1, KU // 2) as j:
                        for s in range(2):
                            down_part(j, n, s)
                gain(u_down + DU)
                gain(u_down + DU + 1)

            mlp(0, U_UP, U_DOWN, 1, 1)
            norm_and_turn(1, True, TURN_X2)
            gain(U_Q2 + 2)
            for t in range(T):
                x_scale(2, t, last=True)
            dve.wait_ge(pos_in, 32)
            done(v.tensor_copy(pos_f[:], pos_i[:]))
            for t in range(T):
                done(v.tensor_scalar(ang[:, 0, t], inv[:], pos_f[:, t:t + 1], None, ALU.mult))
            MAGIC = 1.5 * 2.0 ** 23
            for m in range(2):
                done(v.tensor_scalar(turns[:, m], ang[:, 0], 1.0 / (2 * math.pi), 0.25 * m, ALU.mult, ALU.add))
            done(v.tensor_scalar(turns[:], turns[:], MAGIC, None, ALU.add))
            done(v.tensor_scalar(turns[:], turns[:], MAGIC, None, ALU.subtract))
            done(v.tensor_copy(ang[:, 1], ang[:, 0]))
            for part in TWO_PI:
                done(v.scalar_tensor_tensor(out=ang[:], in0=turns[:], scalar=-part, in1=ang[:], op0=ALU.mult, op1=ALU.add))
            done(v.tensor_scalar(ang[:, 1], ang[:, 1], math.pi / 2, None, ALU.add))
            v.tensor_scalar(ang[:], ang[:], 3.1415925, -3.1415925, ALU.min, ALU.max).then_inc(ang_ready, 1)
            dve.wait_ge(lam_in_s, 16)
            for m in range(2):
                done(v.tensor_tensor(lam_pr[:, m], lam_in[:, 2 * m], lam_in[:, 2 * m + 1], ALU.mult))
            v.tensor_reduce(lam_s[:], lam_pr[:], AX.X, ALU.add).then_inc(lams_ready, 1)
            dve.wait_ge(trig_ready, 1)
            dve.wait_ge(rx_ready, T)
            for t in range(T):
                done(v.tensor_scalar(trig[:, :, t], trig[:, :, t], rx[:, t:t + 1], None, ALU.mult))
            dve.wait_ge(lame_ready, 1)
            done(v.memset(lam2[:], 1.0))
            done(v.scalar_tensor_tensor(out=lam2[:, 1:2], in0=lam_e[:, 1:2], scalar=-LAM_INIT, in1=lam_e[:, 0:1],
                                        op0=ALU.add, op1=ALU.subtract))

            def rotate(G):
                for t in range(T):
                    wait_bank(dve, G, t)
                    src = ps[:, 4 * (G % 2) + t].rearrange("p (m a d) -> p m a d", a=2, d=HALF)
                    cos = trig[:, 1, t:t + 1, :]
                    sin = trig[:, 0, t:t + 1, :]
                    if G > G_Q2:
                        dve.wait_ge(rope_turned, 4 * (G - 1 - G_Q2) + t + 1)
                    ta = scr_a[:].rearrange("p (m a d) -> p m a d", a=2, d=HALF)
                    tb = scr_b[:].rearrange("p (m a d) -> p m a d", a=2, d=HALF)
                    dst = roped[:, t].rearrange("p (m a d) -> p m a d", a=2, d=HALF)
                    own[0] += 3
                    v.tensor_tensor(scr_a[:].rearrange("p (m d) -> p m d", d=HALF),
                                    ps[:, 4 * (G % 2) + t].rearrange("p (m d) -> p m d", d=HALF),
                                    cos.to_broadcast([P, 16, HALF]), ALU.mult).then_inc(dve_self, 1)
                    v.tensor_tensor(tb[:, :, 0], src[:, :, 1], sin.to_broadcast([P, 8, HALF]), ALU.mult).then_inc(dve_self, 1)
                    v.tensor_tensor(tb[:, :, 1], src[:, :, 0], sin.to_broadcast([P, 8, HALF]), ALU.mult).then_inc(dve_self, 1)
                    dve.wait_ge(dve_self, own[0])
                    v.tensor_tensor(dst[:, :, 0], ta[:, :, 0], tb[:, :, 0], ALU.subtract)
                    own[0] += 1
                    v.tensor_tensor(dst[:, :, 1], ta[:, :, 1], tb[:, :, 1], ALU.add).then_inc(rope_ready, 1)
                    dve.wait_ge(rope_ready, 4 * (G - G_Q2) + t + 1)
                    own[0] -= 1

            def rope_lo(G):
                hi, lo = (q_hi, q_lo) if G < G_K2 else (k_hi, k_lo)
                for t in range(T):
                    dve.wait_ge(qk_hi, 4 * (G - G_Q2) + t + 1)
                    hs = slice(4 * (G % 2), 4 * (G % 2) + 4)
                    v.tensor_tensor(lo[:, hs, P * t:P * t + P], ps[:, 4 * (G % 2) + t].rearrange("p (h k) -> p h k", h=4),
                                    f32(hi[:, hs, P * t:P * t + P]), ALU.subtract).then_inc(qk_ready, 1)

            gain(U_Q2 + 3)
            for G in range(G_Q2, G_V2):
                rotate(G)
                gain(U_Q2 + 2 * (G - G_Q2) + 4)
                rope_lo(G)
                gain(U_Q2 + 2 * (G - G_Q2) + 5)
            for g in range(2):
                gain(U_OUT2 + g)
                for t in range(T):
                    dve.wait_ge(v_hi_s, T * g + t + 1)
                    sl = slice(g * COLS, (g + 1) * COLS)
                    v.scalar_tensor_tensor(out=v_lo[:, t, sl], in0=ps[:, 4 * g + t], scalar=rx[:, t:t + 1],
                                           in1=f32(v_hi[:, t, sl]), op0=ALU.mult, op1=ALU.subtract).then_inc(v_ready, 1)

            steps = [(J, h) for J in reversed(range(T)) for h in range(A_HEADS)]

            def maxima(i):
                J, h = steps[i]
                n = P * (J + 1)
                s = i % 2
                dve.wait_ge(scores_done, i + 1)
                done(v.tensor_reduce(smax[:, s], ps[:, 2 * s:2 * s + 2, 0:n], AX.X, ALU.max))
                v.tensor_scalar(nmax[:, s], smax[:, s], -(A_DIM ** -0.5), None, ALU.mult).then_inc(max_ready, 1)

            def inverse_sums(i):
                s = i % 2
                dve.wait_ge(exp_ready, 2 * i + 2)
                done(v.reciprocal(linv[:, s], lsum[:, s]))
                v.tensor_tensor(linv[:, s], linv[:, s], lam2[:], ALU.mult).then_inc(linv_ready, 1)

            def difference(i):
                J, h = steps[i]
                n = P * (J + 1)
                s = i % 2
                dve.wait_ge(e2_scaled, i + 1)
                if i >= 2:
                    dve.wait_ge(pt_done, i - 1)
                v.scalar_tensor_tensor(out=pdiff[:, s, 0:n], in0=probs[:, s, 0, 0:n], scalar=linv[:, s, 0:1],
                                       in1=probs[:, s, 1, 0:n], op0=ALU.mult, op1=ALU.add).then_inc(diff_ready, 1)

            def pt_split(i):
                J, h = steps[i]
                n = P * (J + 1)
                dve.wait_ge(pt_hi_s, i + 1)
                v.tensor_tensor(pt_lo[:, i % 2, 0:n], ps[:, 4 + i % 2, 0:n], f32(pt_hi[:, i % 2, 0:n]),
                                ALU.subtract).then_inc(pt_ready, 1)

            def o_sums(q):
                for b in range(2):
                    dve.wait_ge(o_squared, 2 * q + b + 1)
                    ins = v.tensor_reduce(oss[:, T - 1 - q, 4 * b:4 * b + 4], junk[:].rearrange("p (h e) -> p h e", h=4), AX.X,
                                          ALU.add)
                    ins.then_inc(o_summed, 1)

            def o_scale(n, tiles):
                dve.wait_ge(ostd_ready, n + 1)
                for t in tiles:
                    done(v.reciprocal(oss[:, t], orms[:, t]))
                    heads = o_nat[:, t].rearrange("p (h e) -> p h e", h=A_HEADS)
                    v.tensor_tensor(heads, heads, oss[:, t].rearrange("p (h a) -> p h a", a=1).to_broadcast(
                        [P, A_HEADS, 2 * A_DIM]), ALU.mult).then_inc(nat_ready, 1)

            maxima(0)
            for i in range(len(steps) + 1):
                if i < len(steps):
                    inverse_sums(i)
                if i + 1 < len(steps):
                    maxima(i + 1)
                if i >= 1:
                    pt_split(i - 1)
                if i < len(steps):
                    difference(i)
                if i >= 12 and i % A_HEADS == 4:
                    o_sums(i // A_HEADS - 1)
            dve.wait_ge(o_summed, 6)
            v.engine_nop().then_inc(ovar_ready, 1)
            o_scale(0, order[TURN_YA][:3])
            tile_lo(TURN_YA, 1, q_hi, q_lo)
            o_sums(T - 1)
            dve.wait_ge(o_summed, 8)
            v.engine_nop().then_inc(ovar_ready, 1)
            tile_lo(TURN_YA, 3, q_hi, q_lo)
            o_scale(1, order[TURN_YA][3:])
            tile_lo(TURN_YA, 2, q_hi, q_lo)
            tile_lo(TURN_YA, 0, q_hi, q_lo)
            gain(U_OUT2 + 2)
            gain(U_OUT2 + 3)
            gain(U_UP2)
            post_first(2, False)
            gain(U_UP2 + 1)
            norm_and_turn(2, False, TURN_X3)
            mlp(1, U_UP2, U_DOWN2, 3, 3)
            for t in range(T):
                post_tile(3, t, True)

        @block.tensor
        def _(pe):
            def three(out, s_hi, s_lo, m_hi_, m_lo_, first, last):
                pe.matmul(out, s_hi, m_hi_, start=first, stop=False)
                pe.matmul(out, s_hi, m_lo_, start=False, stop=False)
                return pe.matmul(out, s_lo, m_hi_, start=False, stop=last)

            def unit(u, s, bank0, acts, weights_still, first, last, bank_wait=None, tiles=range(T), hook=None):
                pe.wait_ge(weights_ready, u + 1)
                for n, b in enumerate(tiles):
                    if hook and n == T - 1:
                        hook()
                    if bank_wait:
                        bank_wait(b)
                    for k in range(UC):
                        cut = slice(P * b, P * b + P)
                        if weights_still:
                            mm = three(ps[:, bank0 + b], whi[:, s, k, cut], wlo[:, s, k, cut], acts[0][:, k], acts[1][:, k],
                                       first and k == 0, last and k == UC - 1)
                        else:
                            mm = three(ps[:, bank0 + b], acts[0][:, k, cut], acts[1][:, k, cut], whi[:, s, k], wlo[:, s, k],
                                       first and k == 0, last and k == UC - 1)
                    if last and n < T - 1:
                        mm.then_inc(bank_done, 1)
                mm.then_inc(unit_used, 1)

            def group(u, g2, acts, weights_still, bank_wait=None, between=None, hook=None):
                for s in range(2):
                    part = tuple(t[:, UC * s:UC * s + UC] for t in acts)
                    unit(u + s, s, 4 * g2, part, weights_still, s == 0, s == 1, bank_wait if s == 0 else None,
                         hook=hook if s == 1 else None)
                    if s == 0 and between:
                        between()

            def turn_tile(n, src, t):
                pe.wait_ge(nat_ready, T * n + order[n].index(t) + 1)
                if n == TURN_YA and t == order[n][1]:
                    pe.wait_ge(o_copied, 2 * T)
                for c in range(C):
                    mm = pe.transpose(ps[:, T * (c // T) + t, P * (c % T):P * (c % T) + P], src[:, t, P * c:P * c + P], ident[:])
                mm.then_inc(turned, 1)

            def wait_tile(n, t, j):
                pe.wait_ge(acts_ready, 2 * (T * n + order[n].index(t)) + j + 1)

            def turn_then_still(n, src, u, acts, first_turned):
                def part(s, banks, cols, first, stop):
                    for b in banks:
                        for k in range(UC):
                            c = UC * s + k
                            cut = slice(P * b, P * b + P)
                            ops = ((whi, acts[0]), (whi, acts[1]), (wlo, acts[0]))
                            for m, (w, x_) in enumerate(ops):
                                mm = pe.matmul(ps[:, b, cols], w[:, s, k, cut], x_[:, c, cols],
                                               start=first and k == 0 and m == 0, stop=stop and k == UC - 1 and m == 2,
                                               skip_group_check=True)
                        if stop and b < T - 1:
                            mm.then_inc(bank_done, 1)
                    return mm

                for t in range(first_turned, 2):
                    turn_tile(n, src, t)
                pe.wait_ge(weights_ready, u + 1)
                wait_tile(n, 1, 0)
                part(0, (0, 1), slice(0, 2 * P), True, False)
                turn_tile(n, src, 2)
                turn_tile(n, src, 3)
                wait_tile(n, 3, 0)
                part(0, (0, 1), slice(2 * P, SEQ), False, False)
                part(0, (2, 3), slice(0, SEQ), True, False).then_inc(unit_used, 1)
                pe.wait_ge(weights_ready, u + 2)
                wait_tile(n, 3, 1)
                part(1, range(T), slice(0, SEQ), False, True).then_inc(unit_used, 1)

            def turn_then_moving(n, src, u, acts, first_turned, hook=None):
                tiles = order[n]
                for i in range(first_turned, 2):
                    turn_tile(n, src, tiles[i])
                for s in range(2):
                    part = tuple(t[:, UC * s:UC * s + UC] for t in acts)
                    pe.wait_ge(weights_ready, u + s + 1)
                    for i, t in enumerate(range(T) if s else tiles):
                        wait_tile(n, t, s)
                        for k in range(UC):
                            cut = slice(P * t, P * t + P)
                            mm = three(ps[:, t], part[0][:, k, cut], part[1][:, k, cut], whi[:, s, k], wlo[:, s, k],
                                       s == 0 and k == 0, s == 1 and k == UC - 1)
                        if s == 1 and i < T - 1:
                            mm.then_inc(bank_done, 1)
                        if s == 0 and i + 2 < T:
                            turn_tile(n, src, tiles[i + 2])
                    mm.then_inc(unit_used, 1)

            acts = (act_hi, act_lo)
            pe.wait_ge(consts_ready, 2)
            pe.wait_ge(grows_in, 64)
            pe.transpose(ps[:, 7, 0:GROWS], grows[:], ident[0:GROWS, 0:GROWS]).then_inc(gcols_turned, 1)
            pe.wait_ge(gcols_ready, 1)
            turn_then_still(TURN_X0, y_nat, U_QK, acts, 0)
            pe.wait_ge(gw_ready, 1)
            for c in range(C):
                mm = three(ps[0:8, 4], wg_hi[:, c], wg_lo[:, c], act_hi[:, c], act_lo[:, c], c == 0, c == C - 1)
            mm.then_inc(gates_done, 1)
            group(U_QK + 2, 1, acts, True, bank_wait=lambda b: pe.wait_ge(tanh_ready, 1))
            pe.wait_ge(m_evac, 4)
            pe.wait_ge(rows_ready, 2)
            for t in range(T):
                pe.transpose(ps[:, 3, M_HEADS * t:M_HEADS * (t + 1)], a_row[:, P * t:P * t + P], ident[0:M_HEADS, 0:M_HEADS])
            for t in range(T, 2 * T):
                mm = pe.transpose(ps[:, 3, M_HEADS * t:M_HEADS * (t + 1)], e_row[:, P * (t - T):P * (t - T) + P],
                                  ident[0:M_HEADS, 0:M_HEADS])
            mm.then_inc(acol_turned, 1)

            def v_bank(b):
                if b == 3:
                    pe.wait_ge(acol_ready, 1)

            group(U_V, 0, acts, False, bank_wait=v_bank)
            group(U_V + 2, 1, acts, False, bank_wait=lambda b: pe.wait_ge(m_evac, 4 + b + 1))
            group(U_O, 0, acts, False, bank_wait=lambda b: pe.wait_ge(m_evac, 8 + b + 1))
            group(U_O + 2, 1, acts, False, bank_wait=lambda b: pe.wait_ge(m_evac, 12 + b + 1))

            def head_scores(h):
                for k in range(T):
                    w = P * (T - k)
                    b, o = divmod(KSTART[k], COLS)
                    if h == 0:
                        pe.wait_ge(sig_ready, 2 * T)
                        pe.wait_ge(consts_r_ready, 4)
                    else:
                        pe.wait_ge(decay_ready, T * h)
                        pe.wait_ge(p_ready, T * h)
                    sl = slice(KSTART[k], KSTART[k] + w)
                    pe.matmul(ps[:, b, o:o + w], sel_r[:, h], r_hi[:, sl], start=True, stop=False)
                    pe.matmul(ps[:, b, o:o + w], sel_r[:, h], r_lo[:, sl], start=False, stop=False)
                    pe.matmul(ps[:, b, o:o + P], ident_r[:], mask_st[:], start=False, stop=True).then_inc(bcast_done, 1)
                    three(ps[:, 3 + b, o:o + w], mk_hi[:, h, P * k:P * k + P], mk_lo[:, h, P * k:P * k + P],
                          mq_hi[:, h, P * k:SEQ], mq_lo[:, h, P * k:SEQ], True, True).then_inc(s_done, 1)

            def head_values(h):
                for J in range(T):
                    pe.wait_ge(p_lo_ready, T * h + J + 1)
                    n = T * h + J
                    if n >= 2:
                        pe.wait_ge(av_evac, n - 1)
                    for k in range(J + 1):
                        o = KSTART[k] + P * (J - k)
                        bank = ps[:, 6 + J % 2]
                        hi, lo = p_hi[:, h % 2, o:o + P], p_lo[:, h % 2, o:o + P]
                        pe.matmul(bank[:, 0:VW], hi, mv_hi[:, k, h], start=(k == 0), stop=False)
                        pe.matmul(bank[:, 0:VW], lo, mv_hi[:, k, h], start=False, stop=False)
                        mm = pe.matmul(bank[:, 0:M_V], hi, mv_lo[:, k, h, 0:M_V], start=False, stop=(k == J))
                    mm.then_inc(av_done, 1)

            pe.wait_ge(ones_ready, 1)
            head_scores(0)
            for h in range(1, M_HEADS):
                head_scores(h)
                head_values(h - 1)
            head_values(M_HEADS - 1)

            turn_then_moving(TURN_YM, y_nat, U_OUT, acts, 0)
            group(U_OUT + 2, 1, acts, False, hook=lambda: turn_tile(TURN_X1, x_sb, 0))

            def mlp(layer, turn_n, u_up, u_down, next_turn):
                turn_then_still(turn_n, x_sb, u_up, acts, 1)
                group(u_up + 2, 1, acts, True)

                def pair(i):
                    for g2 in range(2):
                        group(i * 4 + (u_up + 2 * g2), g2, acts, True,
                              lambda b: pe.wait_ge(up_evac, i * 8 + (32 * layer + 4 * (g2 - 2) + b + 1)))

                with pe.Fori(1, UPG // 2) as i:
                    pair(i)
                for n in range(2):
                    def down_unit(j, s, first=False, last=False, bank=None, hook=None):
                        pe.wait_ge(down_ready, j * 2 + (DU * layer + KU * n + s + 1))
                        unit(j * 2 + (u_down + KU * n + s), s, 4 * n, tuple(t[:, UC * s:UC * s + UC] for t in acts), False,
                             first, last, bank, hook=hook)

                    down_unit(0, 0, first=True, bank=lambda b: pe.wait_ge(up_evac, 32 * layer + 24 + 4 * n + b + 1))
                    down_unit(0, 1)
                    with pe.Fori(1, KU // 2 - 1) as j:
                        down_unit(j, 0)
                        down_unit(j, 1)
                    down_unit(KU // 2 - 1, 0)
                    down_unit(KU // 2 - 1, 1, last=True, hook=next_turn if n else None)

            mlp(0, TURN_X1, U_UP, U_DOWN, lambda: turn_tile(TURN_X2, x_sb, 0))

            def rope_turn(G):
                for t in range(T):
                    pe.wait_ge(rope_ready, 4 * (G - G_Q2) + t + 1)
                    for h in range(4):
                        mm = pe.transpose(ps[:, 4 * (G % 2) + t, P * h:P * h + P], roped[:, t, P * h:P * h + P], ident[:])
                    mm.then_inc(rope_turned, 1)

            turn_then_moving(TURN_X2, x_sb, U_Q2, acts, 1)
            group(U_Q2 + 2, 1, acts, False, between=lambda: rope_turn(G_Q2))
            for n in range(4):
                group(U_K2 + 2 * n, n % 2, acts, False,
                      bank_wait=lambda b: pe.wait_ge(qk_ready, 4 * n + b + 1),
                      between=(lambda: rope_turn(G_K2 - 1 + n)) if n < 3 else None)

            steps = [(J, h) for J in reversed(range(T)) for h in range(A_HEADS)]

            def scores(i):
                J, h = steps[i]
                n = P * (J + 1)
                if i == 0:
                    pe.wait_ge(v_ready, T)
                elif i >= 2:
                    pe.wait_ge(exp_ready, 2 * (i - 1))
                qs = slice(P * J, P * J + P)
                rows = [slice(A_DIM * m, A_DIM * m + A_DIM) for m in range(2)]
                for part, (a_, b_) in enumerate(((q_hi, k_hi), (q_hi, k_lo), (q_lo, k_hi))):
                    for m in range(2):
                        pe.matmul(ps[:, 2 * (i % 2) + m, 0:n], a_[rows[m], h, qs], b_[rows[m], h, 0:n],
                                  start=(part == 0), stop=False)
                for m in range(2):
                    mm = pe.matmul(ps[:, 2 * (i % 2) + m, P * J:n], ident_r[:], mask_ts[:], start=False, stop=True)
                mm.then_inc(scores_done, 1)

            def turn_diff(i):
                J, h = steps[i]
                pe.wait_ge(diff_ready, i + 1)
                if i == 0:
                    pe.wait_ge(v_ready, 2 * T)
                elif i >= 2:
                    pe.wait_ge(pt_ready, i - 1)
                for k in range(J + 1):
                    mm = pe.transpose(ps[:, 4 + i % 2, P * k:P * k + P], pdiff[:, i % 2, P * k:P * k + P], ident[:])
                mm.then_inc(pt_done, 1)

            def values(i):
                J, h = steps[i]
                pe.wait_ge(pt_ready, i + 1)
                if h == 0 and i:
                    pe.wait_ge(o_copied, 2 * (i // A_HEADS))
                out_ = ps[:, 6 + h // 4, P * (h % 4):P * (h % 4) + P]
                for k in range(J + 1):
                    hi, lo = pt_hi[:, i % 2, P * k:P * k + P], pt_lo[:, i % 2, P * k:P * k + P]
                    hs = slice(P * h, P * h + P)
                    mm = three(out_, hi, lo, v_hi[:, k, hs], v_lo[:, k, hs], k == 0, k == J)
                mm.then_inc(o_done, 1)

            scores(0)
            scores(1)
            for i in range(len(steps) + 2):
                if 1 <= i <= len(steps):
                    turn_diff(i - 1)
                if i + 2 < len(steps):
                    scores(i + 2)
                if i >= 2:
                    values(i - 2)
            turn_then_moving(TURN_YA, o_nat, U_OUT2, (q_hi, q_lo), 0)
            group(U_OUT2 + 2, 1, (q_hi, q_lo), False, hook=lambda: turn_tile(TURN_X3, x_sb, 0))
            mlp(1, TURN_X3, U_UP2, U_DOWN2, None)


INPUTS = ("x", "positions", "norm_g", "a_w_in", "a_b_gates", "a_g_head", "a_w_out", "kv_norm_g", "w_kv",
          "b_w_q", "b_lam", "b_g_head", "b_w_out", "mlp_w_up", "mlp_w_down")


def kernel(**inputs):
    import concourse.bacc as bacc
    from concourse.bass_utils import run_bass_kernel_spmd

    nc = bacc.Bacc("TRN2", target_bir_lowering=False, num_devices=1)
    arrays = {f"in_{name}": np.ascontiguousarray(inputs[name]) for name in INPUTS}
    freq = 1.0 / (np.float32(10000.0) ** (np.arange(0, A_DIM, 2, dtype=np.float32) / np.float32(A_DIM)))
    arrays["inv_freq"] = freq.astype(np.float32).reshape(1, HALF)
    args = [nc.dram_tensor(n, a.shape, mybir.dt.from_np(a.dtype), kind="ExternalInput").ap() for n, a in arrays.items()]
    out = nc.dram_tensor("out", (1, SEQ, D_MODEL), F32, kind="ExternalOutput").ap()
    trunk(nc, *args, out)
    result = run_bass_kernel_spmd(nc, [arrays], core_ids=[0])
    return result.results[0]["out"]
```

```python
import math
from contextlib import ExitStack

import numpy as np

import concourse.bass as bass
from concourse import mybir

F32 = mybir.dt.float32
F32R = mybir.dt.float32r
I32 = mybir.dt.int32
ALU = mybir.AluOpType
ACT = mybir.ActivationFunctionType
AX = mybir.AxisListType

P = 128
SEQ, D_MODEL, D_FF = 512, 1024, 4096
T = SEQ // P
C = D_MODEL // P
COLS = 512
UC = 4
EPS = 1e-6
MASKED = -1e30

M_HEADS, M_V, M_QK = 4, 256, 128
CAP = 15.0
VW = M_V + 2
BLK = T * (T + 1) // 2
A_HEADS, A_DIM = 8, 64
HALF = A_DIM // 2
LAM_INIT = 0.8 - 0.6 * math.exp(-0.3)

U_QK, U_V, U_O, U_OUT, U_UP, U_DOWN = 0, 4, 8, 12, 16, 32
U_Q2, U_K2, U_V2, U_OUT2, U_UP2, U_DOWN2, UNITS = 48, 52, 56, 60, 64, 80, 96
G_QK, G_V, G_O, G_OUT, G_UP, G_DOWN = 0, 2, 4, 6, 8, 16
G_Q2, G_K2, G_V2, G_OUT2, G_UP2, G_DOWN2 = 18, 20, 22, 24, 26, 34
UPG = D_FF // COLS
DU = 16
KU = D_FF // (UC * P)
TURN_X0, TURN_YM, TURN_X1, TURN_X2, TURN_YA, TURN_X3 = range(6)
GC_AHEAD, GC_KV, GC_BHEAD = 64, 72, 80
GROWS = 88
KSTART = (0, 512, 1024, 896)
TWO_PI = (6.28125, 0.0019340515136718750, 1.2554228305816650390625e-06, 2.1219957914e-11)


def trunk(nc, x, positions, norm_g, a_w_in, a_b_gates, a_g_head, a_w_out, kv_norm_g, w_kv, b_w_q,
          b_lam, b_g_head, b_w_out, mlp_w_up, mlp_w_down, inv_freq, out):
    def chunks(w):
        return w.rearrange("(c p) n -> p c n", p=P)

    w_in, w_out = chunks(a_w_in[0]), chunks(a_w_out[0])
    w_q2, w_kv2, w_out2 = chunks(b_w_q[0]), chunks(w_kv), chunks(b_w_out[0])
    w_up = [chunks(mlp_w_up[n]) for n in range(2)]
    w_down = [chunks(mlp_w_down[n]) for n in range(2)]
    x_rows = x[0].rearrange("(t p) d -> t p d", p=P)
    out_rows = out[0].rearrange("(t p) d -> t p d", p=P)

    with ExitStack() as ctx:
        base = nc.sbuf_base
        at = [(base + 63) // 64 * 64]

        def place(name, shape, dtype, offset=None):
            size = int(np.prod(shape[1:])) * 4
            if offset is None:
                offset = at[0]
                at[0] += (size + 31) // 32 * 32
            return nc.alloc_sbuf_tensor_at(name, shape, dtype, offset=offset)

        def sem(name):
            return ctx.enter_context(nc.semaphore(name))

        x_sb = place("x_sb", [P, T, D_MODEL], F32)
        wraw = place("wraw", [P, 2, UC, COLS], F32)
        whi = place("whi", [P, 2, UC, COLS], F32R)
        wlo = place("wlo", [P, 2, UC, COLS], F32R)
        KB = 1024
        ra = at[0]
        at[0] += 32 * KB
        act_hi = place("act_hi", [P, C, SEQ], F32R, ra)
        act_lo = place("act_lo", [P, C, SEQ], F32R, ra + 16 * KB)
        decay = place("decay", [P, 2, BLK * P], F32, ra)
        p_hi = place("p_hi", [P, 2, BLK * P], F32R, ra + 10 * KB)
        p_lo = place("p_lo", [P, 2, BLK * P], F32R, ra + 20 * KB)
        o_nat = place("o_nat", [P, T, D_MODEL], F32, ra)
        probs = place("probs", [P, 2, 2, SEQ], F32, ra + 16 * KB)
        pt_hi = place("pt_hi", [P, 2, SEQ], F32R, ra + 24 * KB)
        pt_lo = place("pt_lo", [P, 2, SEQ], F32R, ra + 28 * KB)
        ru = at[0]
        at[0] += 65 * KB
        u_sq = place("u_sq", [P, D_FF // P, SEQ], F32, ru)
        mq_hi = place("mq_hi", [P, M_HEADS, SEQ], F32R, ru)
        mq_lo = place("mq_lo", [P, M_HEADS, SEQ], F32R, ru + 8 * KB)
        mk_hi = place("mk_hi", [P, M_HEADS, SEQ], F32R, ru + 16 * KB)
        mk_lo = place("mk_lo", [P, M_HEADS, SEQ], F32R, ru + 24 * KB)
        mv_hi = place("mv_hi", [P, T, M_HEADS, VW], F32R, ru + 32 * KB)
        mv_lo_at = ru + 32 * KB + T * M_HEADS * VW * 4
        mv_end = mv_lo_at + T * M_HEADS * VW * 4
        mv_lo = place("mv_lo", [P, T, M_HEADS, VW], F32R, mv_lo_at)
        q_hi = place("q_hi", [P, A_HEADS, SEQ], F32R, ru)
        q_lo = place("q_lo", [P, A_HEADS, SEQ], F32R, ru + 16 * KB)
        k_hi = place("k_hi", [P, A_HEADS, SEQ], F32R, ru + 32 * KB)
        k_lo = place("k_lo", [P, A_HEADS, SEQ], F32R, ru + 48 * KB)
        re = at[0]
        at[0] += 32 * KB
        y_nat = place("y_nat", [P, T, D_MODEL], F32, re)
        rg = re + 16 * KB
        g_raw = place("g_raw", [2 * M_HEADS, SEQ], F32, rg)
        f_raw = place("f_raw", [M_HEADS, SEQ], F32, rg + 2 * KB)
        sp_row = place("sp_row", [M_HEADS, SEQ], F32, rg + 4 * KB)
        b_row = place("b_row", [M_HEADS, SEQ], F32, rg + 6 * KB)
        m_row = place("m_row", [M_HEADS, SEQ], F32, rg + 8 * KB)
        a_row = place("a_row", [M_HEADS, SEQ], F32, rg + 10 * KB)
        e_row = place("e_row", [M_HEADS, SEQ], F32, rg + 12 * KB)
        junk_m = place("junk_m", [P, M_V], F32, rg + 10 * KB)
        r_row = place("r_row", [M_HEADS, BLK * P], F32, re)
        r_hi = place("r_hi", [M_HEADS, BLK * P], F32R, rg)
        r_lo = place("r_lo", [M_HEADS, BLK * P], F32R, rg + 5 * KB)
        sel = place("sel", [M_HEADS, M_HEADS, P], F32, rg + 14 * KB)
        v_hi = place("v_hi", [P, T, D_MODEL], F32R, re)
        v_lo = place("v_lo", [P, T, D_MODEL], F32R, re + 16 * KB)
        roped = place("roped", [P, T, COLS], F32, re)
        relu_t = place("relu_t", [P, 2, COLS], F32, re)
        yg = place("yg", [P, T, D_MODEL], F32, re + 16 * KB)
        gpost = place("gpost", [P, D_MODEL], F32)
        rs = at[0]
        at[0] += 4 * KB
        scr_a = place("scr_a", [P, COLS], F32, rs)
        scr_b = place("scr_b", [P, COLS], F32, rs + 2 * KB)
        pdiff = place("pdiff", [P, 2, SEQ], F32, rs)
        lam_in = place("lam_in", [P, 4, A_DIM], F32, rs)
        lam_pr = place("lam_pr", [P, 2, A_DIM], F32, rs + 1 * KB)
        ang = place("ang", [P, 2, T, HALF], F32, rs + 2 * KB)
        turns = place("turns", [P, 2, T, HALF], F32, rs + 3 * KB)
        rj = at[0]
        junk = place("junk", [P, COLS], F32)
        sel_r = place("sel_r", [M_HEADS, M_HEADS, P], F32R, rj)
        ident = place("ident", [P, P], F32)
        ident_r = place("ident_r", [P, P], F32R)
        mask_st = place("mask_st", [P, P], F32R)
        mask_ts = place("mask_ts", [P, P], F32R)
        grows = place("grows", [GROWS, P], F32, mv_end)
        gcols = place("gcols", [P, GROWS], F32)
        wg_raw = place("wg_raw", [P, C, 8], F32, mv_lo_at)
        wg_hi = place("wg_hi", [P, C, 8], F32R, mv_lo_at + 256)
        wg_lo = place("wg_lo", [P, C, 8], F32R, mv_lo_at + 512)
        gate_b = place("gate_b", [8, 1], F32, mv_lo_at + 768)
        gate_b15 = place("gate_b15", [8, 1], F32, mv_lo_at + 800)
        pos_i = place("pos_i", [P, T], I32)
        pos_f = place("pos_f", [P, T], F32)
        inv = place("inv", [P, HALF], F32)
        trig = place("trig", [P, 2, T, HALF], F32)
        lam_s = place("lam_s", [P, 2], F32)
        lam_e = place("lam_e", [P, 2], F32)
        lam2 = place("lam2", [P, 2], F32)
        ssq = place("ssq", [P, T, 2], F32)
        bias0 = place("bias0", [P, T], F32)
        rms = place("rms", [P, T], F32)
        fac = place("fac", [P, T], F32)
        ssx = place("ssx", [P, T], F32)
        rmsx = place("rmsx", [P, T], F32)
        rx = place("rx", [P, T], F32)
        rx2 = place("rx2", [P, T], F32)
        rx4 = place("rx4", [P, T], F32)
        dcum = place("dcum", [M_HEADS, T, T], F32)
        carry = place("carry", [M_HEADS, T], F32)
        acol = place("acol", [P, 2 * T, M_HEADS], F32)
        den = place("den", [P, T, M_HEADS], F32)
        den2 = place("den2", [P, T, M_HEADS], F32)
        mss = place("mss", [P, T, M_HEADS], F32)
        mfac = place("mfac", [P, T, M_HEADS], F32)
        small = mv_end + P * 4
        smax, nmax, lsum, linv = (place(n, [P, 2, 2, 4], F32, small + 64 * i)
                                  for i, n in enumerate(("smax", "nmax", "lsum", "linv")))
        assert small + 4 * 64 <= ru + 65 * KB
        oss = place("oss", [P, T, A_HEADS], F32)
        orms = place("orms", [P, T, A_HEADS], F32)
        epsc = place("epsc", [P, 1], F32)
        assert at[0] <= nc.sbuf_usable_end, at[0]

        ps = ctx.enter_context(nc.psum_tensor("ps", [P, 8, COLS], F32))

        x_in = [sem(f"x_in{t}") for t in range(T)]
        grows_in, gate_in, pos_in, lam_in_s = (sem(n) for n in ("grows_in", "gate_in", "pos_in", "lam_in"))
        gpost_in = sem("gpost_in")
        raw_loaded = [sem(f"raw_loaded{s}") for s in range(2)]
        gained = sem("gained")
        whi_ready, weights_ready, unit_used = sem("whi_ready"), sem("weights_ready"), sem("unit_used")
        bank_done = sem("bank_done")
        consts_ready, gcols_turned, gcols_ready = sem("consts_ready"), sem("gcols_turned"), sem("gcols_ready")
        consts_r_ready, eps_ready = sem("consts_r_ready"), sem("eps_ready")
        nat_ready, turned = sem("nat_ready"), sem("turned")
        acts_hi, acts_ready = sem("acts_hi"), sem("acts_ready")
        act_self, dve_self = sem("act_self"), sem("dve_self")
        sq0, sq1, rms_ready = sem("sq0"), sem("sq1"), sem("rms_ready")
        bias0_ready = sem("bias0_ready")
        rmsx_ready, rx_ready = sem("rmsx_ready"), sem("rx_ready")
        gw_scaled, gw_hi, gw_ready, gates_done = sem("gw_scaled"), sem("gw_hi"), sem("gw_ready"), sem("gates_done")
        tanh_ready, f_rows_in = sem("tanh_ready"), sem("f_rows_in")
        sp_ready, mneg_ready, e_ready = sem("sp_ready"), sem("mneg_ready"), sem("e_ready")
        rows_ready, r_hi_ready = sem("rows_ready"), sem("r_hi_ready")
        acol_turned, acol_ready = sem("acol_turned"), sem("acol_ready")
        m_hi, m_evac = sem("m_hi"), sem("m_evac")
        ones_ready = sem("ones_ready")
        sig_ready = sem("sig_ready")
        bcast_done, decay_ready, s_done = sem("bcast_done"), sem("decay_ready"), sem("s_done")
        p_ready, p_hi_ready, p_lo_ready = sem("p_ready"), sem("p_hi_ready"), sem("p_lo_ready")
        linv_ready, e2_scaled = sem("linv_ready"), sem("e2_scaled")
        av_done, av_sq, av_evac = sem("av_done"), sem("av_sq"), sem("av_evac")
        mvar_ready, mstd_ready = sem("mvar_ready"), sem("mstd_ready")
        relu_ready, up_evac = sem("relu_ready"), sem("up_evac")
        down_hi, down_ready = sem("down_hi"), sem("down_ready")
        ang_ready, trig_ready = sem("ang_ready"), sem("trig_ready")
        lams_ready, lame_ready = sem("lams_ready"), sem("lame_ready")
        rope_ready, rope_turned, qk_hi, qk_ready = sem("rope_ready"), sem("rope_turned"), sem("qk_hi"), sem("qk_ready")
        v_hi_s, v_ready = sem("v_hi_s"), sem("v_ready")
        scores_done, max_ready, exp_ready = sem("scores_done"), sem("max_ready"), sem("exp_ready")
        diff_ready, pt_done, pt_hi_s, pt_ready = sem("diff_ready"), sem("pt_done"), sem("pt_hi_s"), sem("pt_ready")
        o_done, o_copied, ovar_ready, ostd_ready = sem("o_done"), sem("o_copied"), sem("ovar_ready"), sem("ostd_ready")
        o_squared, o_summed = sem("o_squared"), sem("o_summed")
        stored = sem("stored")

        def wait_bank(eng, G, b):
            if b < 3:
                eng.wait_ge(bank_done, 3 * G + b + 1)
            elif G < G_DOWN:
                eng.wait_ge(unit_used, 2 * G + 2)
            elif G < G_Q2:
                eng.wait_ge(unit_used, U_DOWN + KU * (G - G_DOWN + 1))
            elif G < G_DOWN2:
                eng.wait_ge(unit_used, U_Q2 + 2 * (G - G_Q2) + 2)
            else:
                eng.wait_ge(unit_used, U_DOWN2 + KU * (G - G_DOWN2 + 1))

        def is_gained(u):
            return u < U_DOWN or U_Q2 <= u < U_DOWN2

        def n_gained(u):
            return u + 1 if u < U_DOWN else u + 1 - DU

        def gain_col(u):
            for last, col in ((U_OUT, 0), (U_UP, GC_AHEAD), (U_DOWN, 8 * 2), (U_K2, 8 * 4), (U_OUT2, GC_KV),
                              (U_UP2, GC_BHEAD), (U_DOWN2, 8 * 6)):
                if u < last:
                    return col + UC * (u % 2)

        steps = [(J, tuple(range(h, h + n))) for J, n in ((3, 1), (2, 1), (1, 2), (0, 2)) for h in range(0, A_HEADS, n)]

        def last_step(q, b):
            return next(i for i, (J, heads) in enumerate(steps) if J == T - 1 - q and 4 * b + 3 in heads)

        halves = [(q, b) for q in range(T) for b in range(2)]

        order = [tuple(range(T))] * 6
        order[TURN_YA] = (1, 3, 2, 0)
        turn_banks = ((4, 5), (2, 3), (6, 4), (7, 5))

        block = ctx.enter_context(nc.Block())

        @block.sync
        def _(sp):
            def load(u, s, src):
                if not (isinstance(u, int) and u < 2):
                    sp.wait_ge(weights_ready, u - 1)
                sp.dma_start(wraw[:, s], src).then_inc(raw_loaded[s], 16)

            def short_stage(u0, w, col0, groups):
                for g in range(groups):
                    for s in range(2):
                        load(u0 + 2 * g + s, s, w[:, UC * s:UC * s + UC, col0 + g * COLS:col0 + (g + 1) * COLS])

            def mlp(layer, u_up, u_down):
                w1, w2 = w_up[layer], w_down[layer]
                with sp.Fori(0, UPG) as g:
                    for s in range(2):
                        load(g * 2 + (u_up + s), s, w1[:, UC * s:UC * s + UC, bass.ds(g * COLS, COLS)])
                load_gpost(2 * layer + 1, layer, 3)
                for n in range(2):
                    with sp.Fori(0, KU // 2) as j:
                        for s in range(2):
                            load(j * 2 + (u_down + KU * n + s), s,
                                 w2[:, bass.ds(j * (2 * UC) + UC * s, UC), n * COLS:(n + 1) * COLS])

            def load_gpost(n, layer, i):
                if n:
                    sp.wait_ge(nat_ready, T * (TURN_X1, TURN_X2, TURN_X3)[n - 1] + T)
                sp.dma_start(gpost[:], norm_g[layer, i:i + 1, :].to_broadcast([P, D_MODEL])).then_inc(gpost_in, 16)

            sp.dma_start(grows[0:64, :], norm_g.rearrange("l i (c p) -> (l i c) p", p=P)).then_inc(grows_in, 16)
            sp.dma_start(x_sb[:, 0], x_rows[0]).then_inc(x_in[0], 16)
            sp.dma_start(grows[64:72, :], a_g_head.rearrange("l (c p) -> (l c) p", p=P)).then_inc(grows_in, 16)
            sp.dma_start(grows[72:80, :], kv_norm_g.rearrange("(c p) -> c p", p=P)).then_inc(grows_in, 16)
            sp.dma_start(grows[80:88, :], b_g_head.rearrange("l (c p) -> (l c) p", p=P)).then_inc(grows_in, 16)
            sp.dma_start(x_sb[:, 1], x_rows[1]).then_inc(x_in[1], 16)
            load(0, 0, w_in[:, 0:UC, 0:COLS])
            for t in range(2, T):
                sp.dma_start(x_sb[:, t], x_rows[t]).then_inc(x_in[t], 16)
            load(1, 1, w_in[:, UC:2 * UC, 0:COLS])
            sp.dma_start(wg_raw[:], w_in[:, :, 3 * D_MODEL:3 * D_MODEL + 8]).then_inc(gate_in, 16)
            sp.dma_start(gate_b[:], a_b_gates.rearrange("l g -> g l")).then_inc(gate_in, 16)
            load_gpost(0, 0, 1)
            sp.dma_start(pos_i[:], positions[0].rearrange("(t p) -> p t", p=P),
                         allow_slow_non_contiguous=True).then_inc(pos_in, 16)
            sp.dma_start(inv[:], inv_freq.to_broadcast([P, HALF])).then_inc(pos_in, 16)
            short_stage(U_QK + 2, w_in, COLS, 1)
            sp.wait_ge(tanh_ready, 1)
            sp.dma_start(f_raw[:], g_raw[M_HEADS:2 * M_HEADS, :]).then_inc(f_rows_in, 16)
            sp.wait_ge(consts_r_ready, 4)
            sp.dma_start(lam_in[:], b_lam.rearrange("l a d -> l (a d)").to_broadcast([P, 4 * A_DIM])).then_inc(lam_in_s, 16)
            short_stage(U_V, w_in, D_MODEL, 4)
            short_stage(U_OUT, w_out, 0, 2)
            mlp(0, U_UP, U_DOWN)
            short_stage(U_Q2, w_q2, 0, 2)
            load_gpost(2, 1, 1)
            short_stage(U_K2, w_kv2, 0, 4)
            short_stage(U_OUT2, w_out2, 0, 2)
            mlp(1, U_UP2, U_DOWN2)
            for t in range(T - 1):
                sp.wait_ge(nat_ready, 6 * T + t + 1)
                sp.dma_start(out_rows[t], x_sb[:, t]).then_inc(stored, 16)
            for c in range(2):
                sp.wait_ge(nat_ready, 7 * T + c)
                cut = slice(c * COLS, (c + 1) * COLS)
                sp.dma_start(out_rows[T - 1, :, cut], x_sb[:, T - 1, cut]).then_inc(stored, 16)
            sp.wait_ge(stored, 16 * (T + 1))

        @block.gpsimd
        def _(pool):
            g = nc.gpsimd
            g.memset(ident[:], 0.0).then_inc(consts_ready, 1)
            pool.wait_ge(consts_ready, 1)
            g.affine_select(out=ident[:], in_=ident[:], compare_op=ALU.not_equal, fill=1.0, base=0,
                            pattern=[[-1, P]], channel_multiplier=1).then_inc(consts_ready, 1)
            g.memset(sel[:], 0.0).then_inc(consts_ready, 1)
            pool.wait_ge(consts_ready, 3)
            g.affine_select(out=sel[:], in_=sel[:], compare_op=ALU.not_equal, fill=1.0, base=0,
                            pattern=[[-1, M_HEADS], [0, P]], channel_multiplier=1).then_inc(consts_ready, 1)
            g.memset(scr_a[:, 0:2 * P], 0.0).then_inc(consts_ready, 1)
            pool.wait_ge(consts_ready, 5)
            g.affine_select(out=scr_a[:, 0:P], in_=scr_a[:, 0:P], compare_op=ALU.is_ge, fill=MASKED, base=0,
                            pattern=[[1, P]], channel_multiplier=-1).then_inc(consts_ready, 1)
            g.affine_select(out=scr_a[:, P:2 * P], in_=scr_a[:, P:2 * P], compare_op=ALU.is_ge, fill=MASKED, base=0,
                            pattern=[[-1, P]], channel_multiplier=1).then_inc(consts_ready, 1)

            def lo_part(u, s):
                pool.wait_ge(whi_ready, u + 1)
                for k in range(UC):
                    ins = g.tensor_tensor(wlo[:, s, k], wraw[:, s, k], whi[:, s, k].bitcast(F32), ALU.subtract)
                ins.then_inc(weights_ready, 1)

            with pool.Fori(0, U_OUT2 // 2) as j:
                for s in range(2):
                    lo_part(j * 2 + s, s)
            lo_part(U_OUT2, 0)
            for q in range(T):
                for b in range(2):
                    pool.wait_ge(o_copied, 2 * q + b + 1)
                    if q or b:
                        pool.wait_ge(o_summed, 2 * q + b)
                    part = o_nat[:, T - 1 - q, b * COLS:(b + 1) * COLS]
                    g.tensor_tensor(junk[:], part, part, ALU.mult).then_inc(o_squared, 1)
                    if q == 0 and b == 0:
                        lo_part(U_OUT2 + 1, 1)
            with pool.Fori(U_OUT2 // 2 + 1, UNITS // 2) as j:
                for s in range(2):
                    lo_part(j * 2 + s, s)

        @block.scalar
        def _(act):
            a = nc.scalar
            own = [0]

            def done(ins):
                own[0] += 1
                ins.then_inc(act_self, 1)
                act.wait_ge(act_self, own[0])

            def w_hi(u):
                s = u % 2
                if u < UNITS:
                    if is_gained(u):
                        act.wait_ge(gained, n_gained(u))
                    else:
                        act.wait_ge(raw_loaded[s], 16 * (u // 2 + 1))
                    if u >= 2:
                        act.wait_ge(unit_used, u - 1)
                    a.activation(whi[:, s], wraw[:, s], ACT.Copy).then_inc(whi_ready, 1)

            def w_hi_at(j, u0, s):
                if isinstance(j, int):
                    return w_hi(u0 + 2 * j + s)
                if is_gained(u0):
                    act.wait_ge(gained, j * 2 + (n_gained(u0) + s))
                else:
                    act.wait_ge(raw_loaded[s], j * 16 + 16 * (u0 // 2 + 1))
                act.wait_ge(unit_used, j * 2 + (u0 + s - 1))
                a.activation(whi[:, s], wraw[:, s], ACT.Copy).then_inc(whi_ready, 1)

            def w_hi_chunk(u, k):
                act.wait_ge(gained, n_gained(u))
                act.wait_ge(unit_used, u - 1)
                ins = a.activation(whi[:, u % 2, k], wraw[:, u % 2, k], ACT.Copy)
                if k == UC - 1:
                    ins.then_inc(whi_ready, 1)

            def tile_hi(turn, t, dst):
                n = order[turn].index(t)
                for j in range(2):
                    act.wait_ge(turned, T * turn + n + 1)
                    a.activation(dst[:, 4 * j:4 * j + 4, P * t:P * t + P],
                                 ps[:, turn_banks[n][j]].rearrange("p (c k) -> p c k", c=4), ACT.Copy).then_inc(acts_hi, 1)

            def x_squares(t, first):
                if first:
                    act.wait_ge(x_in[t], 16)
                done(a.activation(y_nat[:, t] if first else yg[:, 0], x_sb[:, t], ACT.Square, accum_out=ssx[:, t:t + 1]))
                a.activation(rmsx[:, t:t + 1], ssx[:, t:t + 1], ACT.Sqrt, scale=1.0 / D_MODEL,
                             bias=epsc[:, 0:1]).then_inc(rmsx_ready, 1)

            def first_squares(n, G):
                for t in range(T):
                    wait_bank(act, G, t)
                    a.activation(junk[:], ps[:, t], ACT.Square, accum_out=ssq[:, t, 0:1]).then_inc(sq0, 1)
                    act.wait_ge(sq0, T * n + t + 1)

            def norm_root(n, G, t, mlp):
                wait_bank(act, G + 1, t)
                a.activation(junk[:], ps[:, 4 + t], ACT.Square, accum_out=ssq[:, t, 1:2]).then_inc(sq1, 1)
                act.wait_ge(sq1, T * n + t + 1)
                act.wait_ge(bias0_ready, T * n + t + 1)
                a.activation(rms[:, t:t + 1], ssq[:, t, 1:2], ACT.Sqrt,
                             scale=rx4[:, t:t + 1] if mlp else 1.0 / D_MODEL,
                             bias=bias0[:, t:t + 1]).then_inc(rms_ready, 1)

            def norm_and_turn(n, G, mlp, turn, u_next):
                for t in range(3):
                    norm_root(n, G, t, mlp)
                tile_hi(turn, 0, act_hi)
                tile_hi(turn, 1, act_hi)
                norm_root(n, G, 3, mlp)
                tile_hi(turn, 2, act_hi)
                if turn == TURN_X2:
                    w_hi(u_next + 1)
                tile_hi(turn, 3, act_hi)
                if turn != TURN_X2:
                    w_hi(u_next + 1)
                x_stats(turn)

            def x_stats(turn):
                for t in range(T):
                    act.wait_ge(nat_ready, T * turn + t + 1)
                    x_squares(t, False)

            act.wait_ge(eps_ready, 1)
            done(a.activation(rms[:, 0:1], epsc[:], ACT.Sqrt))
            x_squares(0, True)
            x_squares(1, True)
            tile_hi(TURN_X0, 0, act_hi)
            w_hi(0)
            tile_hi(TURN_X0, 1, act_hi)
            x_squares(2, True)
            x_squares(3, True)
            w_hi(1)
            tile_hi(TURN_X0, 2, act_hi)
            tile_hi(TURN_X0, 3, act_hi)
            act.wait_ge(consts_ready, 7)
            a.activation(ident_r[:], ident[:], ACT.Copy).then_inc(consts_r_ready, 1)
            a.activation(sel_r[:], sel[:], ACT.Copy).then_inc(consts_r_ready, 1)
            a.activation(mask_st[:], scr_a[:, 0:P], ACT.Copy).then_inc(consts_r_ready, 1)
            a.activation(mask_ts[:], scr_a[:, P:2 * P], ACT.Copy).then_inc(consts_r_ready, 1)
            act.wait_ge(gw_scaled, 1)
            a.activation(wg_hi[:], wg_raw[:], ACT.Copy).then_inc(gw_hi, 1)
            w_hi(2)
            w_hi(3)
            for h in range(M_HEADS):
                wait_bank(act, G_QK, h)
                a.activation(mq_hi[:, h], ps[:, h], ACT.Copy).then_inc(m_hi, 1)
            act.wait_ge(gates_done, 1)
            act.wait_ge(gw_ready, 2)
            a.activation(g_raw[:], ps[0:8, 4], ACT.Tanh, scale=1.0 / CAP, bias=gate_b15[:, 0:1]).then_inc(tanh_ready, 1)
            act.wait_ge(f_rows_in, 16)
            done(a.activation(e_row[:], f_raw[:], ACT.Exp, scale=-CAP))
            a.activation(sp_row[:], e_row[:], ACT.Ln, bias=1.0).then_inc(sp_ready, 1)
            w_hi(4)
            act.wait_ge(mneg_ready, 1)
            a.activation(e_row[:], b_row[:], ACT.Exp).then_inc(e_ready, 1)
            act.wait_ge(rows_ready, 1)
            a.activation(r_hi[:], r_row[:], ACT.Copy).then_inc(r_hi_ready, 1)
            w_hi(5)
            for h in range(M_HEADS):
                wait_bank(act, G_QK + 1, h)
                a.activation(mk_hi[:, h], ps[:, 4 + h], ACT.Copy, scale=M_QK ** -0.5).then_inc(m_hi, 1)
            act.wait_ge(ang_ready, 1)
            a.activation(trig[:], ang[:], ACT.Sin).then_inc(trig_ready, 1)
            act.wait_ge(lams_ready, 1)
            a.activation(lam_e[:], lam_s[:], ACT.Exp).then_inc(lame_ready, 1)
            for g in range(2):
                w_hi(U_V + 2 * g + 2)
                w_hi(U_V + 2 * g + 3)
                for t in range(T):
                    wait_bank(act, G_V + g, t)
                    a.activation(mv_hi[:, t, 2 * g:2 * g + 2, 0:M_V],
                                 ps[:, 4 * g + t].rearrange("p (h e) -> p h e", h=2), ACT.Copy).then_inc(m_hi, 1)
            def o_gate(g):
                for t in range(T):
                    wait_bank(act, G_O + g, t)
                    a.activation(y_nat[:, t, g * COLS:(g + 1) * COLS], ps[:, 4 * g + t], ACT.Sigmoid).then_inc(sig_ready, 1)

            def head_decay(h, k):
                w = P * (T - k)
                act.wait_ge(bcast_done, T * h + T)
                if h >= 2:
                    act.wait_ge(p_lo_ready, T * (h - 2) + k + 1)
                b, o = divmod(KSTART[k], COLS)
                a.activation(decay[:, h % 2, KSTART[k]:KSTART[k] + w], ps[:, b, o:o + w], ACT.Exp,
                             bias=acol[:, k, h:h + 1]).then_inc(decay_ready, 1)

            def head_hi(h, k):
                act.wait_ge(p_ready, T * h + k + 1)
                if h >= 2:
                    act.wait_ge(av_done, T * (h - 1))
                sl = slice(KSTART[k], KSTART[k] + P * (T - k))
                a.activation(p_hi[:, h % 2, sl], decay[:, h % 2, sl], ACT.Copy).then_inc(p_hi_ready, 1)

            def head_squares(h, J):
                n = T * h + J
                act.wait_ge(av_done, n + 1)
                if n:
                    act.wait_ge(av_sq, n)
                a.activation(junk_m[:], ps[:, 6 + J % 2, 0:M_V], ACT.Square, accum_out=mss[:, J, h:h + 1]).then_inc(av_sq, 1)

            def heads_root(n, hs):
                act.wait_ge(mvar_ready, n + 1)
                a.activation(mfac[:, :, hs], mss[:, :, hs], ACT.Sqrt, scale=1.0 / M_V).then_inc(mstd_ready, 1)

            w_hi(U_O + 2)
            w_hi(U_O + 3)
            o_gate(0)
            w_hi(U_OUT)
            act.wait_ge(acol_ready, 1)
            for h in range(M_HEADS):
                for k in range(T):
                    head_decay(h, k)
                if h == 0:
                    o_gate(1)
                    w_hi(U_OUT + 1)
                for k in range(T):
                    if h:
                        head_squares(h - 1, k)
                    head_hi(h, k)
            done(a.activation(rms[:, 0:1], epsc[:], ACT.Sqrt))
            for k in range(T):
                head_squares(M_HEADS - 1, k)
                if k == 0:
                    heads_root(0, slice(0, M_HEADS - 1))
            heads_root(1, slice(M_HEADS - 1, M_HEADS))
            for t in range(T):
                tile_hi(TURN_YM, t, act_hi)
            w_hi(U_OUT + 2)
            w_hi(U_OUT + 3)
            first_squares(0, G_OUT)
            w_hi(U_UP)
            norm_and_turn(0, G_OUT, False, TURN_X1, U_UP)

            def mlp(layer, u_up, u_down, G_up, G_down, n_post):
                def relus(i, g2):
                    for b in range(4):
                        n = i * 8 + (4 * g2 + b)
                        if b < 3:
                            act.wait_ge(bank_done, i * 6 + (3 * (G_up + g2) + b + 1))
                        else:
                            act.wait_ge(unit_used, i * 4 + (u_up + 2 * g2 + 2))
                        if not (isinstance(n, int) and n < 2):
                            act.wait_ge(up_evac, n + (32 * layer - 1))
                        a.activation(relu_t[:, b % 2], ps[:, 4 * g2 + b], ACT.Relu).then_inc(relu_ready, 1)

                def down_part(j, n, s):
                    act.wait_ge(unit_used, j * 2 + (u_down + KU * n + s - 1))
                    if n == 0:
                        act.wait_ge(up_evac, j * 8 + (32 * layer + 4 * s + 4))
                    src = u_sq[:, 4 * s:4 * s + 4] if isinstance(j, int) and j == 0 else u_sq[:, bass.ds(j * 8 + 4 * s, 4)]
                    a.activation(act_hi[:, 4 * s:4 * s + 4], src, ACT.Copy).then_inc(down_hi, 1)

                def pair(i, last=False):
                    for g2 in range(2):
                        w_hi_at(i * 2 + g2, u_up + 2, 0)
                        if last and g2 == 1:
                            down_part(0, 0, 0)
                            w_hi_at(i * 2 + g2, u_up + 2, 1)
                            down_part(0, 0, 1)
                        else:
                            w_hi_at(i * 2 + g2, u_up + 2, 1)
                        relus(i, g2)

                pair(0)
                with act.Fori(1, UPG // 2 - 1) as i:
                    pair(i)
                pair(UPG // 2 - 1, last=True)
                for n in range(2):
                    if n:
                        for s in range(2):
                            down_part(0, n, s)
                            w_hi_at(0, u_down + KU * n, s)
                        first_squares(n_post, G_down)
                    with act.Fori(1, KU // 2) as j:
                        for s in range(2):
                            down_part(j, n, s)
                            w_hi_at(j, u_down + KU * n, s)
                w_hi(u_down + DU)

            mlp(0, U_UP, U_DOWN, G_UP, G_DOWN, 1)
            norm_and_turn(1, G_DOWN, True, TURN_X2, U_Q2)

            def rope_hi(G):
                dst = q_hi if G < G_K2 else k_hi
                for t in range(T):
                    act.wait_ge(rope_turned, 4 * (G - G_Q2) + t + 1)
                    a.activation(dst[:, 4 * (G % 2):4 * (G % 2) + 4, P * t:P * t + P],
                                 ps[:, 4 * (G % 2) + t].rearrange("p (h k) -> p h k", h=4), ACT.Copy).then_inc(qk_hi, 1)

            for G in range(G_Q2, G_V2):
                u = U_Q2 + 2 * (G - G_Q2)
                w_hi(u + 2)
                if G > G_Q2:
                    rope_hi(G - 1)
                w_hi(u + 3)

            def v_part(g):
                for t in range(T):
                    wait_bank(act, G_V2 + g, t)
                    a.activation(v_hi[:, t, g * COLS:(g + 1) * COLS], ps[:, 4 * g + t], ACT.Copy,
                                 scale=rx[:, t:t + 1]).then_inc(v_hi_s, 1)

            w_hi(U_V2 + 2)
            rope_hi(G_V2 - 1)
            w_hi(U_V2 + 3)
            v_part(0)
            w_hi(U_OUT2)


            def exps(i):
                J, heads = steps[i]
                n = P * (J + 1)
                act.wait_ge(max_ready, i + 1)
                if i >= 2:
                    act.wait_ge(diff_ready, i - 1)
                for m in range(2):
                    for a_ in range(len(heads)):
                        cut = slice(n * a_, n * a_ + n)
                        ins = a.activation(probs[:, i % 2, m, cut], ps[:, 2 * (i % 2) + m, cut], ACT.Exp, scale=A_DIM ** -0.5,
                                           bias=nmax[:, i % 2, m, a_:a_ + 1], accum_out=lsum[:, i % 2, m, a_:a_ + 1])
                ins.then_inc(exp_ready, 1)

            def scale_second(i):
                J, heads = steps[i]
                n = P * (J + 1)
                act.wait_ge(linv_ready, i + 1)
                act.wait_ge(exp_ready, i + 1)
                for a_ in range(len(heads)):
                    cut = slice(n * a_, n * a_ + n)
                    ins = a.activation(probs[:, i % 2, 1, cut], probs[:, i % 2, 1, cut], ACT.Copy,
                                       scale=linv[:, i % 2, 1, a_:a_ + 1])
                ins.then_inc(e2_scaled, 1)

            def pt_split(i):
                J, heads = steps[i]
                n = P * (J + 1) * len(heads)
                act.wait_ge(pt_done, i + 1)
                if i >= 2:
                    act.wait_ge(o_done, i - 1)
                a.activation(pt_hi[:, i % 2, 0:n], ps[:, 4 + i % 2, 0:n], ACT.Copy).then_inc(pt_hi_s, 1)

            def copy_o(q, b):
                act.wait_ge(o_done, last_step(q, b) + 1)
                a.activation(o_nat[:, T - 1 - q, b * COLS:(b + 1) * COLS], ps[:, 6 + b], ACT.Copy).then_inc(o_copied, 1)

            def o_roots(n, t0, t1):
                act.wait_ge(ovar_ready, n + 1)
                a.activation(orms[:, t0:t1], oss[:, t0:t1], ACT.Sqrt, scale=1.0 / (2 * A_DIM),
                             bias=epsc[:, 0:1]).then_inc(ostd_ready, 1)

            exps(0)
            for i in range(len(steps) + 1):
                if i == 1:
                    v_part(1)
                if i >= 1:
                    pt_split(i - 1)
                if 7 <= i < 7 + UC:
                    w_hi_chunk(U_OUT2 + 1, i - 7)
                for q, b in halves:
                    if last_step(q, b) + 3 == i:
                        copy_o(q, b)
                if i < len(steps):
                    scale_second(i)
                if i + 1 < len(steps):
                    exps(i + 1)
                if i + 1 == len(steps):
                    done(a.activation(rms[:, 0:1], epsc[:], ACT.Sqrt))
            o_roots(0, 1, T)
            copy_o(T - 1, 1)
            tile_hi(TURN_YA, 1, q_hi)
            tile_hi(TURN_YA, 3, q_hi)
            o_roots(1, 0, 1)
            tile_hi(TURN_YA, 2, q_hi)
            tile_hi(TURN_YA, 0, q_hi)
            w_hi(U_OUT2 + 2)
            w_hi(U_OUT2 + 3)
            first_squares(2, G_OUT2)
            w_hi(U_UP2)
            norm_and_turn(2, G_OUT2, False, TURN_X3, U_UP2)
            mlp(1, U_UP2, U_DOWN2, G_UP2, G_DOWN2, 3)
            for t in range(T):
                norm_root(3, G_DOWN2, t, True)

        @block.vector
        def _(dve):
            v = nc.vector
            own = [0]

            def done(ins):
                own[0] += 1
                ins.then_inc(dve_self, 1)
                dve.wait_ge(dve_self, own[0])

            def f32(ap):
                return ap.bitcast(F32)

            def tile_lo(turn, t, hi, lo):
                for j in range(2):
                    n = order[turn].index(t)
                    dve.wait_ge(acts_hi, 2 * (T * turn + n) + j + 1)
                    cut = (slice(None), slice(4 * j, 4 * j + 4), slice(P * t, P * t + P))
                    v.tensor_tensor(lo[cut], ps[:, turn_banks[n][j]].rearrange("p (c k) -> p c k", c=4), f32(hi[cut]),
                                    ALU.subtract).then_inc(acts_ready, 1)

            def gain(u, j=None):
                s = u % 2
                if j is None:
                    if u >= UNITS or not is_gained(u):
                        return
                    dve.wait_ge(raw_loaded[s], 16 * (u // 2 + 1))
                else:
                    dve.wait_ge(raw_loaded[s], j * 16 + 16 * (u // 2 + 1))
                for k in range(UC):
                    gain_chunk(u, k)

            def gain_chunk(u, k):
                c = gain_col(u) + k
                ins = v.tensor_scalar(wraw[:, u % 2, k], wraw[:, u % 2, k], gcols[:, c:c + 1], None, ALU.mult)
                if k == UC - 1:
                    ins.then_inc(gained, 1)

            def x_scale(n, t, last=False):
                dve.wait_ge(rmsx_ready, T * n + t + 1)
                ins = v.reciprocal(rx[:, t:t + 1], rmsx[:, t:t + 1])
                if last:
                    ins.then_inc(rx_ready, 1)
                else:
                    done(ins)

            def post_first(n, mlp):
                dve.wait_ge(gpost_in, 16 * (n + 1))
                for t in range(T):
                    dve.wait_ge(sq0, T * n + t + 1)
                    v.tensor_scalar(bias0[:, t:t + 1], ssq[:, t, 0:1], rx4[:, t:t + 1] if mlp else 1.0 / D_MODEL, EPS,
                                    ALU.mult, ALU.add).then_inc(bias0_ready, 1)
                    done(v.tensor_tensor(yg[:, t, 0:COLS], ps[:, t], gpost[:, 0:COLS], ALU.mult))

            def post_tile(n, t, mlp):
                dve.wait_ge(sq1, T * n + t + 1)
                done(v.tensor_tensor(yg[:, t, COLS:2 * COLS], ps[:, 4 + t], gpost[:, COLS:2 * COLS], ALU.mult))
                dve.wait_ge(rms_ready, T * n + t + 1)
                done(v.reciprocal(fac[:, t:t + 1], rms[:, t:t + 1]))
                if mlp:
                    done(v.tensor_tensor(fac[:, t:t + 1], fac[:, t:t + 1], rx2[:, t:t + 1], ALU.mult))
                parts = 2 if n == 3 and t == T - 1 else 1
                for c in range(parts):
                    cut = slice(c * D_MODEL // parts, (c + 1) * D_MODEL // parts)
                    v.scalar_tensor_tensor(out=x_sb[:, t, cut], in0=yg[:, t, cut], scalar=fac[:, t:t + 1],
                                           in1=x_sb[:, t, cut], op0=ALU.mult, op1=ALU.add).then_inc(nat_ready, 1)

            def norm_and_turn(n, mlp, turn, u_next):
                for t in range(3):
                    post_tile(n, t, mlp)
                tile_lo(turn, 0, act_hi, act_lo)
                tile_lo(turn, 1, act_hi, act_lo)
                if turn == TURN_X2:
                    gain(u_next + 1)
                post_tile(n, 3, mlp)
                tile_lo(turn, 2, act_hi, act_lo)
                if turn != TURN_X2:
                    gain(u_next + 1)
                tile_lo(turn, 3, act_hi, act_lo)

            v.memset(epsc[:], EPS).then_inc(eps_ready, 1)
            dve.wait_ge(gcols_turned, 1)
            v.tensor_copy(gcols[:], ps[:, 7, 0:GROWS]).then_inc(gcols_ready, 1)
            dve.wait_ge(gcols_ready, 1)
            for t in range(T):
                x_scale(0, t)
                v.tensor_scalar(y_nat[:, t], x_sb[:, t], rx[:, t:t + 1], None, ALU.mult).then_inc(nat_ready, 1)
                if t == 1:
                    gain(0)
                    tile_lo(TURN_X0, 0, act_hi, act_lo)
                    tile_lo(TURN_X0, 1, act_hi, act_lo)
            gain(1)
            tile_lo(TURN_X0, 2, act_hi, act_lo)
            tile_lo(TURN_X0, 3, act_hi, act_lo)
            dve.wait_ge(gate_in, 32)
            for c in range(C):
                ins = v.tensor_scalar(wg_raw[:, c], wg_raw[:, c], gcols[:, c:c + 1], None, ALU.mult)
            ins.then_inc(gw_scaled, 1)
            v.memset(f32(mv_hi[:, :, :, M_V:VW]), 1.0).then_inc(ones_ready, 1)
            v.tensor_scalar(gcols[:, GC_BHEAD:GC_BHEAD + 8], gcols[:, GC_BHEAD:GC_BHEAD + 8], 1.0 - LAM_INIT, None,
                            ALU.mult).then_inc(gcols_ready, 1)
            dve.wait_ge(gw_hi, 1)
            v.tensor_tensor(wg_lo[:], wg_raw[:], f32(wg_hi[:]), ALU.subtract).then_inc(gw_ready, 1)
            v.tensor_scalar(gate_b15[:], gate_b[:], 1.0 / CAP, None, ALU.mult).then_inc(gw_ready, 1)
            gain(2)
            gain(3)
            for h in range(M_HEADS):
                dve.wait_ge(m_hi, h + 1)
                v.tensor_tensor(mq_lo[:, h], ps[:, h], f32(mq_hi[:, h]), ALU.subtract).then_inc(m_evac, 1)
            dve.wait_ge(sp_ready, 1)

            def blk(r, J):
                return r[:, P * J:P * J + P]

            for J in range(T):
                done(v.tensor_tensor_scan(blk(b_row, J), blk(sp_row, J), blk(sp_row, J), 0.0, ALU.add, ALU.max))
            done(v.scalar_tensor_tensor(out=a_row[:], in0=g_raw[0:M_HEADS, :], scalar=CAP, in1=b_row[:], op0=ALU.mult,
                                        op1=ALU.add))
            gain(4)
            gain(5)
            done(v.memset(carry[:], 0.0))
            done(v.memset(dcum[:], 0.0))
            for J in range(T):
                last = P * J + P - 1
                done(v.tensor_tensor_scan(blk(m_row, J), blk(a_row, J), blk(a_row, J), carry[:, J:J + 1], ALU.max, ALU.max))
                if J + 1 < T:
                    done(v.tensor_tensor(carry[:, J + 1:J + 2], m_row[:, last:last + 1], b_row[:, last:last + 1], ALU.subtract))
                    for k in range(J + 1):
                        done(v.tensor_tensor(dcum[:, k, J + 1:J + 2], dcum[:, k, J:J + 1], b_row[:, last:last + 1], ALU.add))
            for k in range(T):
                for J in range(k, T):
                    o = KSTART[k] + P * (J - k)
                    done(v.tensor_scalar(r_row[:, o:o + P], blk(m_row, J), dcum[:, k, J:J + 1], -1.0, ALU.add, ALU.mult))
            v.tensor_tensor(b_row[:], b_row[:], m_row[:], ALU.subtract).then_inc(mneg_ready, 1)
            v.engine_nop().then_inc(rows_ready, 1)
            dve.wait_ge(e_ready, 1)
            dve.wait_ge(r_hi_ready, 1)
            v.tensor_tensor(r_lo[:], r_row[:], f32(r_hi[:]), ALU.subtract).then_inc(rows_ready, 1)
            for h in range(M_HEADS):
                dve.wait_ge(m_hi, M_HEADS + h + 1)
                v.scalar_tensor_tensor(out=mk_lo[:, h], in0=ps[:, 4 + h], scalar=M_QK ** -0.5, in1=f32(mk_hi[:, h]),
                                       op0=ALU.mult, op1=ALU.subtract).then_inc(m_evac, 1)
            dve.wait_ge(acol_turned, 1)
            v.tensor_copy(acol[:], ps[:, 3, 0:2 * T * M_HEADS].rearrange("p (t h) -> p t h", h=M_HEADS)).then_inc(acol_ready, 1)
            dve.wait_ge(acol_ready, 1)
            done(v.tensor_tensor(acol[:, T:2 * T], acol[:, T:2 * T], acol[:, T:2 * T], ALU.mult))
            dve.wait_ge(pos_in, 32)
            done(v.tensor_copy(pos_f[:], pos_i[:]))
            for t in range(T):
                done(v.tensor_scalar(ang[:, 0, t], inv[:], pos_f[:, t:t + 1], None, ALU.mult))
            MAGIC = 1.5 * 2.0 ** 23
            for m in range(2):
                done(v.tensor_scalar(turns[:, m], ang[:, 0], 1.0 / (2 * math.pi), 0.25 * m, ALU.mult, ALU.add))
            done(v.tensor_scalar(turns[:], turns[:], MAGIC, None, ALU.add))
            done(v.tensor_scalar(turns[:], turns[:], MAGIC, None, ALU.subtract))
            done(v.tensor_copy(ang[:, 1], ang[:, 0]))
            for part in TWO_PI:
                done(v.scalar_tensor_tensor(out=ang[:], in0=turns[:], scalar=-part, in1=ang[:], op0=ALU.mult, op1=ALU.add))
            done(v.tensor_scalar(ang[:, 1], ang[:, 1], math.pi / 2, None, ALU.add))
            v.tensor_scalar(ang[:], ang[:], 3.1415925, -3.1415925, ALU.min, ALU.max).then_inc(ang_ready, 1)
            dve.wait_ge(lam_in_s, 16)
            for m in range(2):
                done(v.tensor_tensor(lam_pr[:, m], lam_in[:, 2 * m], lam_in[:, 2 * m + 1], ALU.mult))
            v.tensor_reduce(lam_s[:], lam_pr[:], AX.X, ALU.add).then_inc(lams_ready, 1)
            dve.wait_ge(lame_ready, 1)
            done(v.memset(lam2[:], 1.0))
            done(v.scalar_tensor_tensor(out=lam2[:, 1:2], in0=lam_e[:, 1:2], scalar=-LAM_INIT, in1=lam_e[:, 0:1],
                                        op0=ALU.add, op1=ALU.subtract))
            dve.wait_ge(trig_ready, 1)
            for g in range(2):
                gain(U_V + 2 * g + 2)
                gain(U_V + 2 * g + 3)
                for t in range(T):
                    dve.wait_ge(m_hi, 2 * M_HEADS + T * g + t + 1)
                    v.tensor_tensor(mv_lo[:, t, 2 * g:2 * g + 2, 0:M_V], ps[:, 4 * g + t].rearrange("p (h e) -> p h e", h=2),
                                    f32(mv_hi[:, t, 2 * g:2 * g + 2, 0:M_V]), ALU.subtract).then_inc(m_evac, 1)
            for u in range(U_O + 2, U_O + 6):
                gain(u)
            def head_product(h, k):
                sl = slice(KSTART[k], KSTART[k] + P * (T - k))
                dve.wait_ge(decay_ready, T * h + k + 1)
                dve.wait_ge(s_done, T * h + T)
                b, o = divmod(KSTART[k], COLS)
                v.tensor_tensor(decay[:, h % 2, sl], decay[:, h % 2, sl], ps[:, 3 + b, o:o + P * (T - k)],
                                ALU.mult).then_inc(p_ready, 1)

            def head_lo(h, k):
                sl = slice(KSTART[k], KSTART[k] + P * (T - k))
                dve.wait_ge(p_hi_ready, T * h + k + 1)
                v.tensor_tensor(p_lo[:, h % 2, sl], decay[:, h % 2, sl], f32(p_hi[:, h % 2, sl]),
                                ALU.subtract).then_inc(p_lo_ready, 1)

            def head_out(h, J):
                dve.wait_ge(av_sq, T * h + J + 1)
                if h == 0 and J == 0:
                    dve.wait_ge(sig_ready, 2 * T)
                sl = slice(h * M_V, (h + 1) * M_V)
                v.tensor_copy(den[:, J, h:h + 1], ps[:, 6 + J % 2, M_V:M_V + 1])
                v.tensor_tensor(y_nat[:, J, sl], y_nat[:, J, sl], ps[:, 6 + J % 2, 0:M_V], ALU.mult).then_inc(av_evac, 1)

            for h in range(M_HEADS):
                for k in range(T):
                    head_product(h, k)
                    if h and k % 2 == 0:
                        head_out(h - 1, k // 2)
                for k in range(T):
                    head_lo(h, k)
                    if h and k % 2 == 0:
                        head_out(h - 1, 2 + k // 2)
            def heads_var(hs):
                dve.wait_ge(av_evac, T * hs.stop)
                dve.wait_ge(av_sq, T * hs.stop)
                done(v.tensor_tensor(den2[:, :, hs], den[:, :, hs], den[:, :, hs], ALU.mult))
                done(v.tensor_tensor(den2[:, :, hs], den2[:, :, hs], acol[:, T:2 * T, hs], ALU.max))
                v.scalar_tensor_tensor(out=mss[:, :, hs], in0=den2[:, :, hs], scalar=M_V * EPS, in1=mss[:, :, hs],
                                       op0=ALU.mult, op1=ALU.add).then_inc(mvar_ready, 1)

            def heads_scale(n, hs):
                dve.wait_ge(mstd_ready, n + 1)
                done(v.reciprocal(den2[:, :, hs], mfac[:, :, hs]))

            def y_scale(t, h):
                sl = slice(h * M_V, (h + 1) * M_V)
                return v.tensor_scalar(y_nat[:, t, sl], y_nat[:, t, sl], den2[:, t, h:h + 1], None, ALU.mult)

            heads_var(slice(0, M_HEADS - 1))
            for t in range(T):
                head_out(M_HEADS - 1, t)
                if t == 0:
                    heads_scale(0, slice(0, M_HEADS - 1))
                if t < T - 1:
                    for h in range(M_HEADS - 1):
                        y_scale(t, h)
            heads_var(slice(M_HEADS - 1, M_HEADS))
            for h in range(M_HEADS - 1):
                y_scale(T - 1, h)
            heads_scale(1, slice(M_HEADS - 1, M_HEADS))
            for t in range(T):
                y_scale(t, M_HEADS - 1).then_inc(nat_ready, 1)
                if t:
                    tile_lo(TURN_YM, t - 1, act_hi, act_lo)
            tile_lo(TURN_YM, T - 1, act_hi, act_lo)
            gain(U_OUT + 2)
            gain(U_OUT + 3)
            gain(U_UP)
            post_first(0, False)
            norm_and_turn(0, False, TURN_X1, U_UP)

            def mlp(layer, u_up, u_down, n_norm, n_post):
                gain(u_up + 2)
                for t in range(T):
                    x_scale(n_norm, t)
                done(v.tensor_tensor(rx2[:], rx[:], rx[:], ALU.mult))
                done(v.scalar_tensor_tensor(out=rx4[:], in0=rx2[:], scalar=1.0 / D_MODEL, in1=rx2[:], op0=ALU.mult,
                                            op1=ALU.mult))

                def squares(i, g2):
                    for b in range(4):
                        n = i * 8 + (4 * g2 + b)
                        dve.wait_ge(relu_ready, n + (32 * layer + 1))
                        dst = u_sq[:, n] if isinstance(n, int) else u_sq[:, bass.ds(n, 1)].rearrange("p a s -> p (a s)")
                        v.tensor_tensor(dst, relu_t[:, b % 2], ps[:, 4 * g2 + b], ALU.mult).then_inc(up_evac, 1)

                def down_part(j, n, s):
                    dve.wait_ge(down_hi, j * 2 + (DU * layer + KU * n + s + 1))
                    src = u_sq[:, 4 * s:4 * s + 4] if isinstance(j, int) and j == 0 else u_sq[:, bass.ds(j * 8 + 4 * s, 4)]
                    v.tensor_tensor(act_lo[:, 4 * s:4 * s + 4], src, f32(act_hi[:, 4 * s:4 * s + 4]),
                                    ALU.subtract).then_inc(down_ready, 1)

                gain(u_up + 3)
                squares(0, 0)
                gain(u_up + 4)
                gain(u_up + 5)
                squares(0, 1)
                with dve.Fori(1, UPG // 2 - 1) as i:
                    for g2 in range(2):
                        gain(u_up + 2 + 2 * g2, i * 2)
                        gain(u_up + 3 + 2 * g2, i * 2)
                        squares(i, g2)
                gain(u_up + 2 * UPG - 2)
                gain(u_up + 2 * UPG - 1)
                squares(UPG // 2 - 1, 0)
                down_part(0, 0, 0)
                down_part(0, 0, 1)
                squares(UPG // 2 - 1, 1)
                for n in range(2):
                    if n:
                        for s in range(2):
                            down_part(0, n, s)
                        post_first(n_post, True)
                    with dve.Fori(1, KU // 2) as j:
                        for s in range(2):
                            down_part(j, n, s)
                gain(u_down + DU)

            mlp(0, U_UP, U_DOWN, 1, 1)
            norm_and_turn(1, True, TURN_X2, U_Q2)
            gain(U_Q2 + 2)
            for t in range(T):
                x_scale(2, t, last=True)
            dve.wait_ge(rx_ready, T)
            for t in range(T):
                done(v.tensor_scalar(trig[:, :, t], trig[:, :, t], rx[:, t:t + 1], None, ALU.mult))

            def rotate(G):
                for t in range(T):
                    wait_bank(dve, G, t)
                    src = ps[:, 4 * (G % 2) + t].rearrange("p (m a d) -> p m a d", a=2, d=HALF)
                    cos = trig[:, 1, t:t + 1, :]
                    sin = trig[:, 0, t:t + 1, :]
                    if G > G_Q2:
                        dve.wait_ge(rope_turned, 4 * (G - 1 - G_Q2) + t + 1)
                    ta = scr_a[:].rearrange("p (m a d) -> p m a d", a=2, d=HALF)
                    tb = scr_b[:].rearrange("p (m a d) -> p m a d", a=2, d=HALF)
                    dst = roped[:, t].rearrange("p (m a d) -> p m a d", a=2, d=HALF)
                    own[0] += 3
                    v.tensor_tensor(scr_a[:].rearrange("p (m d) -> p m d", d=HALF),
                                    ps[:, 4 * (G % 2) + t].rearrange("p (m d) -> p m d", d=HALF),
                                    cos.to_broadcast([P, 16, HALF]), ALU.mult).then_inc(dve_self, 1)
                    v.tensor_tensor(tb[:, :, 0], src[:, :, 1], sin.to_broadcast([P, 8, HALF]), ALU.mult).then_inc(dve_self, 1)
                    v.tensor_tensor(tb[:, :, 1], src[:, :, 0], sin.to_broadcast([P, 8, HALF]), ALU.mult).then_inc(dve_self, 1)
                    dve.wait_ge(dve_self, own[0])
                    v.tensor_tensor(dst[:, :, 0], ta[:, :, 0], tb[:, :, 0], ALU.subtract)
                    own[0] += 1
                    v.tensor_tensor(dst[:, :, 1], ta[:, :, 1], tb[:, :, 1], ALU.add).then_inc(rope_ready, 1)
                    dve.wait_ge(rope_ready, 4 * (G - G_Q2) + t + 1)
                    own[0] -= 1

            def rope_lo(G):
                hi, lo = (q_hi, q_lo) if G < G_K2 else (k_hi, k_lo)
                for t in range(T):
                    dve.wait_ge(qk_hi, 4 * (G - G_Q2) + t + 1)
                    hs = slice(4 * (G % 2), 4 * (G % 2) + 4)
                    v.tensor_tensor(lo[:, hs, P * t:P * t + P], ps[:, 4 * (G % 2) + t].rearrange("p (h k) -> p h k", h=4),
                                    f32(hi[:, hs, P * t:P * t + P]), ALU.subtract).then_inc(qk_ready, 1)

            gain(U_Q2 + 3)
            for G in range(G_Q2, G_V2):
                rotate(G)
                gain(U_Q2 + 2 * (G - G_Q2) + 4)
                rope_lo(G)
                gain(U_Q2 + 2 * (G - G_Q2) + 5)

            def v_part(g):
                for t in range(T):
                    dve.wait_ge(v_hi_s, T * g + t + 1)
                    sl = slice(g * COLS, (g + 1) * COLS)
                    v.scalar_tensor_tensor(out=v_lo[:, t, sl], in0=ps[:, 4 * g + t], scalar=rx[:, t:t + 1],
                                           in1=f32(v_hi[:, t, sl]), op0=ALU.mult, op1=ALU.subtract).then_inc(v_ready, 1)

            v_part(0)
            gain(U_OUT2)


            def maxima(i):
                J, heads = steps[i]
                n, nh, s = P * (J + 1), len(heads), i % 2
                dve.wait_ge(scores_done, i + 1)
                done(v.tensor_reduce(smax[:, s, :, 0:nh], ps[:, 2 * s:2 * s + 2, 0:nh * n].rearrange("p m (a k) -> p m a k", a=nh),
                                     AX.X, ALU.max))
                v.tensor_scalar(nmax[:, s, :, 0:nh], smax[:, s, :, 0:nh], -(A_DIM ** -0.5), None, ALU.mult).then_inc(max_ready, 1)

            def inverse_sums(i):
                nh, s = len(steps[i][1]), i % 2
                dve.wait_ge(exp_ready, i + 1)
                done(v.reciprocal(linv[:, s, :, 0:nh], lsum[:, s, :, 0:nh]))
                v.tensor_tensor(linv[:, s, :, 0:nh], linv[:, s, :, 0:nh],
                                lam2[:].rearrange("p (m a) -> p m a", a=1).to_broadcast([P, 2, nh]), ALU.mult).then_inc(linv_ready, 1)

            def difference(i):
                J, heads = steps[i]
                n, s = P * (J + 1), i % 2
                dve.wait_ge(e2_scaled, i + 1)
                if i >= 2:
                    dve.wait_ge(pt_done, i - 1)
                for a in range(len(heads)):
                    cut = slice(n * a, n * a + n)
                    ins = v.scalar_tensor_tensor(out=pdiff[:, s, cut], in0=probs[:, s, 0, cut], scalar=linv[:, s, 0, a:a + 1],
                                                 in1=probs[:, s, 1, cut], op0=ALU.mult, op1=ALU.add)
                ins.then_inc(diff_ready, 1)

            def pt_split(i):
                J, heads = steps[i]
                n = P * (J + 1) * len(heads)
                dve.wait_ge(pt_hi_s, i + 1)
                v.tensor_tensor(pt_lo[:, i % 2, 0:n], ps[:, 4 + i % 2, 0:n], f32(pt_hi[:, i % 2, 0:n]),
                                ALU.subtract).then_inc(pt_ready, 1)

            def o_sums(q, b):
                dve.wait_ge(o_squared, 2 * q + b + 1)
                v.tensor_reduce(oss[:, T - 1 - q, 4 * b:4 * b + 4], junk[:].rearrange("p (h e) -> p h e", h=4), AX.X,
                                ALU.add).then_inc(o_summed, 1)

            def o_scale(n, tiles):
                dve.wait_ge(ostd_ready, n + 1)
                for t in tiles:
                    done(v.reciprocal(oss[:, t], orms[:, t]))
                    heads = o_nat[:, t].rearrange("p (h e) -> p h e", h=A_HEADS)
                    v.tensor_tensor(heads, heads, oss[:, t].rearrange("p (h a) -> p h a", a=1).to_broadcast(
                        [P, A_HEADS, 2 * A_DIM]), ALU.mult).then_inc(nat_ready, 1)

            maxima(0)
            for i in range(len(steps) + 1):
                if i < len(steps):
                    inverse_sums(i)
                if i == 1:
                    v_part(1)
                if i + 1 < len(steps):
                    maxima(i + 1)
                if i >= 1:
                    pt_split(i - 1)
                if i < len(steps):
                    difference(i)
                if i == 3:
                    dve.wait_ge(raw_loaded[1], 16 * (U_OUT2 // 2 + 1))
                if 3 <= i < 3 + UC:
                    gain_chunk(U_OUT2 + 1, i - 3)
                for q, b in halves[:-3]:
                    if last_step(q, b) + 5 + b == i:
                        o_sums(q, b)
            o_sums(T - 2, 1)
            dve.wait_ge(o_summed, 6)
            v.engine_nop().then_inc(ovar_ready, 1)
            o_scale(0, order[TURN_YA][:2])
            o_sums(T - 1, 0)
            tile_lo(TURN_YA, 1, q_hi, q_lo)
            o_scale(0, order[TURN_YA][2:3])
            o_sums(T - 1, 1)
            dve.wait_ge(o_summed, 8)
            v.engine_nop().then_inc(ovar_ready, 1)
            tile_lo(TURN_YA, 3, q_hi, q_lo)
            o_scale(1, order[TURN_YA][3:])
            tile_lo(TURN_YA, 2, q_hi, q_lo)
            tile_lo(TURN_YA, 0, q_hi, q_lo)
            gain(U_OUT2 + 2)
            gain(U_OUT2 + 3)
            gain(U_UP2)
            post_first(2, False)
            norm_and_turn(2, False, TURN_X3, U_UP2)
            mlp(1, U_UP2, U_DOWN2, 3, 3)
            for t in range(T):
                post_tile(3, t, True)

        @block.tensor
        def _(pe):
            def three(out, s_hi, s_lo, m_hi_, m_lo_, first, last):
                pe.matmul(out, s_hi, m_hi_, start=first, stop=False)
                pe.matmul(out, s_hi, m_lo_, start=False, stop=False)
                return pe.matmul(out, s_lo, m_hi_, start=False, stop=last)

            def unit(u, s, bank0, acts, weights_still, first, last, bank_wait=None, tiles=range(T), hook=None):
                pe.wait_ge(weights_ready, u + 1)
                for n, b in enumerate(tiles):
                    if hook and n == T - 1:
                        hook()
                    if bank_wait:
                        bank_wait(b)
                    for k in range(UC):
                        cut = slice(P * b, P * b + P)
                        if weights_still:
                            mm = three(ps[:, bank0 + b], whi[:, s, k, cut], wlo[:, s, k, cut], acts[0][:, k], acts[1][:, k],
                                       first and k == 0, last and k == UC - 1)
                        else:
                            mm = three(ps[:, bank0 + b], acts[0][:, k, cut], acts[1][:, k, cut], whi[:, s, k], wlo[:, s, k],
                                       first and k == 0, last and k == UC - 1)
                    if last and n < T - 1:
                        mm.then_inc(bank_done, 1)
                mm.then_inc(unit_used, 1)

            def group(u, g2, acts, weights_still, bank_wait=None, between=None, hook=None):
                for s in range(2):
                    part = tuple(t[:, UC * s:UC * s + UC] for t in acts)
                    unit(u + s, s, 4 * g2, part, weights_still, s == 0, s == 1, bank_wait if s == 0 else None,
                         hook=hook if s == 1 else None)
                    if s == 0 and between:
                        between()

            def turn_tile(n, src, t):
                i = order[n].index(t)
                ahead = n in (TURN_X1, TURN_X2, TURN_X3) and i == 0
                pe.wait_ge(nat_ready, T * n + i + (2 if ahead else 1))
                if i >= 2:
                    wait_tile(n, order[n][0], i - 2)
                if n == TURN_YA and i == 2:
                    pe.wait_ge(o_copied, 2 * T)
                for c in range(C):
                    mm = pe.transpose(ps[:, turn_banks[i][c // T], P * (c % T):P * (c % T) + P], src[:, t, P * c:P * c + P],
                                      ident[:])
                mm.then_inc(turned, 1)

            def wait_tile(n, t, j):
                pe.wait_ge(acts_ready, 2 * (T * n + order[n].index(t)) + j + 1)

            def turn_two(n):
                turn_tile(n, x_sb, 0)
                turn_tile(n, x_sb, 1)

            def turn_then_still(n, src, u, acts, first_turned):
                ops = ((whi, acts[0]), (whi, acts[1]), (wlo, acts[0]))

                def part(s, banks, cols, first=False, stop=False, which=(0, 1, 2)):
                    for b in banks:
                        for m in which:
                            for k in range(UC):
                                mm = pe.matmul(ps[:, b, cols], ops[m][0][:, s, k, P * b:P * b + P],
                                               ops[m][1][:, UC * s + k, cols], start=first and k == 0 and m == 0,
                                               stop=stop and k == UC - 1 and m == which[-1], skip_group_check=True)
                        if stop and b < T - 1:
                            mm.then_inc(bank_done, 1)
                    return mm

                for t in range(first_turned, 2 + first_turned // 2):
                    turn_tile(n, src, t)
                half = slice(0, 2 * P)
                pe.wait_ge(whi_ready, u + 1)
                wait_tile(n, 1, 0)
                part(0, (0, 1), half, first=True, which=(0, 1))
                for t in range(2 + first_turned // 2, T):
                    turn_tile(n, src, t)
                pe.wait_ge(weights_ready, u + 1)
                part(0, (0, 1), half, which=(2,))
                wait_tile(n, 1, 1)
                part(0, (2, 3), half, first=True)
                wait_tile(n, 3, 0)
                part(0, range(T), slice(2 * P, SEQ)).then_inc(unit_used, 1)
                pe.wait_ge(weights_ready, u + 2)
                wait_tile(n, 3, 1)
                part(1, range(T), slice(0, SEQ), stop=True).then_inc(unit_used, 1)

            def turn_then_moving(n, src, u, acts, first_turned, hook=None):
                tiles = order[n]
                for i in range(first_turned, 2):
                    turn_tile(n, src, tiles[i])
                for s in range(2):
                    part = tuple(t[:, UC * s:UC * s + UC] for t in acts)
                    pe.wait_ge(weights_ready, u + s + 1)
                    for i, t in enumerate(range(T) if s else tiles):
                        wait_tile(n, t, 1 if i == 1 and t > 1 else s)
                        for k in range(UC):
                            cut = slice(P * t, P * t + P)
                            mm = three(ps[:, t], part[0][:, k, cut], part[1][:, k, cut], whi[:, s, k], wlo[:, s, k],
                                       s == 0 and k == 0, s == 1 and k == UC - 1)
                        if s == 1 and i < T - 1:
                            mm.then_inc(bank_done, 1)
                        if s == 0 and i + 2 < T:
                            turn_tile(n, src, tiles[i + 2])
                    mm.then_inc(unit_used, 1)

            acts = (act_hi, act_lo)
            pe.wait_ge(consts_ready, 2)
            pe.wait_ge(grows_in, 64)
            pe.transpose(ps[:, 7, 0:GROWS], grows[:], ident[0:GROWS, 0:GROWS]).then_inc(gcols_turned, 1)
            pe.wait_ge(gcols_ready, 1)
            turn_then_still(TURN_X0, y_nat, U_QK, acts, 0)
            pe.wait_ge(gw_ready, 1)
            for c in range(C):
                mm = three(ps[0:8, 4], wg_hi[:, c], wg_lo[:, c], act_hi[:, c], act_lo[:, c], c == 0, c == C - 1)
            mm.then_inc(gates_done, 1)
            group(U_QK + 2, 1, acts, True, bank_wait=lambda b: pe.wait_ge(tanh_ready, 1))
            pe.wait_ge(m_evac, 4)
            pe.wait_ge(rows_ready, 2)
            for t in range(T):
                pe.transpose(ps[:, 3, M_HEADS * t:M_HEADS * (t + 1)], a_row[:, P * t:P * t + P], ident[0:M_HEADS, 0:M_HEADS])
            for t in range(T, 2 * T):
                mm = pe.transpose(ps[:, 3, M_HEADS * t:M_HEADS * (t + 1)], e_row[:, P * (t - T):P * (t - T) + P],
                                  ident[0:M_HEADS, 0:M_HEADS])
            mm.then_inc(acol_turned, 1)

            def v_bank(b):
                if b == 3:
                    pe.wait_ge(acol_ready, 1)

            group(U_V, 0, acts, False, bank_wait=v_bank)
            group(U_V + 2, 1, acts, False, bank_wait=lambda b: pe.wait_ge(m_evac, 4 + b + 1))
            group(U_O, 0, acts, False, bank_wait=lambda b: pe.wait_ge(m_evac, 8 + b + 1))

            def head_rows(h):
                for k in range(T):
                    b, o = divmod(KSTART[k], COLS)
                    w = P * (T - k)
                    if h:
                        pe.wait_ge(decay_ready, T * h)
                    else:
                        pe.wait_ge(sig_ready, T)
                        pe.wait_ge(consts_r_ready, 4)
                    sl = slice(KSTART[k], KSTART[k] + w)
                    pe.matmul(ps[:, b, o:o + w], sel_r[:, h], r_hi[:, sl], start=True, stop=False)
                    pe.matmul(ps[:, b, o:o + w], sel_r[:, h], r_lo[:, sl], start=False, stop=False)
                    pe.matmul(ps[:, b, o:o + P], ident_r[:], mask_st[:], start=False, stop=True).then_inc(bcast_done, 1)

            def head_scores(h):
                for k in range(T):
                    b, o = divmod(KSTART[k], COLS)
                    if h:
                        pe.wait_ge(p_ready, T * h)
                    else:
                        pe.wait_ge(sig_ready, T + b)
                    three(ps[:, 3 + b, o:o + P * (T - k)], mk_hi[:, h, P * k:P * k + P], mk_lo[:, h, P * k:P * k + P],
                          mq_hi[:, h, P * k:SEQ], mq_lo[:, h, P * k:SEQ], True, True).then_inc(s_done, 1)

            def head_values(h):
                for J in range(T):
                    pe.wait_ge(p_lo_ready, T * h + J + 1)
                    n = T * h + J
                    if n >= 2:
                        pe.wait_ge(av_evac, n - 1)
                    else:
                        pe.wait_ge(sig_ready, 2 * T)
                    for k in range(J + 1):
                        o = KSTART[k] + P * (J - k)
                        bank = ps[:, 6 + J % 2]
                        hi, lo = p_hi[:, h % 2, o:o + P], p_lo[:, h % 2, o:o + P]
                        pe.matmul(bank[:, 0:VW], hi, mv_hi[:, k, h], start=(k == 0), stop=False)
                        pe.matmul(bank[:, 0:VW], lo, mv_hi[:, k, h], start=False, stop=False)
                        mm = pe.matmul(bank[:, 0:M_V], hi, mv_lo[:, k, h, 0:M_V], start=False, stop=(k == J))
                    mm.then_inc(av_done, 1)

            group(U_O + 2, 1, acts, False, bank_wait=lambda b: pe.wait_ge(m_evac, 12 + b + 1), between=lambda: head_rows(0))
            pe.wait_ge(ones_ready, 1)
            head_scores(0)
            for h in range(1, M_HEADS):
                head_rows(h)
                head_scores(h)
                head_values(h - 1)
            head_values(M_HEADS - 1)

            turn_then_moving(TURN_YM, y_nat, U_OUT, acts, 0)
            group(U_OUT + 2, 1, acts, False, hook=lambda: turn_two(TURN_X1))

            def mlp(layer, turn_n, u_up, u_down, next_turn):
                turn_then_still(turn_n, x_sb, u_up, acts, 2)
                group(u_up + 2, 1, acts, True)

                def pair(i):
                    for g2 in range(2):
                        group(i * 4 + (u_up + 2 * g2), g2, acts, True,
                              lambda b: pe.wait_ge(up_evac, i * 8 + (32 * layer + 4 * (g2 - 2) + b + 1)))

                with pe.Fori(1, UPG // 2) as i:
                    pair(i)
                for n in range(2):
                    def down_unit(j, s, first=False, last=False, bank=None, hook=None):
                        pe.wait_ge(down_ready, j * 2 + (DU * layer + KU * n + s + 1))
                        unit(j * 2 + (u_down + KU * n + s), s, 4 * n, tuple(t[:, UC * s:UC * s + UC] for t in acts), False,
                             first, last, bank, hook=hook)

                    down_unit(0, 0, first=True, bank=lambda b: pe.wait_ge(up_evac, 32 * layer + 24 + 4 * n + b + 1))
                    down_unit(0, 1)
                    with pe.Fori(1, KU // 2 - 1) as j:
                        down_unit(j, 0)
                        down_unit(j, 1)
                    down_unit(KU // 2 - 1, 0)
                    down_unit(KU // 2 - 1, 1, last=True, hook=next_turn if n else None)

            mlp(0, TURN_X1, U_UP, U_DOWN, lambda: turn_two(TURN_X2))

            def rope_turn(G):
                for t in range(T):
                    pe.wait_ge(rope_ready, 4 * (G - G_Q2) + t + 1)
                    for h in range(4):
                        mm = pe.transpose(ps[:, 4 * (G % 2) + t, P * h:P * h + P], roped[:, t, P * h:P * h + P], ident[:])
                    mm.then_inc(rope_turned, 1)

            turn_then_moving(TURN_X2, x_sb, U_Q2, acts, 2)
            group(U_Q2 + 2, 1, acts, False, between=lambda: rope_turn(G_Q2))

            def scores(i):
                J, heads = steps[i]
                n = P * (J + 1)
                if i == 0:
                    pe.wait_ge(v_ready, T)
                elif i >= 2:
                    pe.wait_ge(exp_ready, i - 1)
                qs = slice(P * J, P * J + P)
                for a, h in enumerate(heads):
                    for part, (a_, b_) in enumerate(((q_hi, k_hi), (q_hi, k_lo), (q_lo, k_hi))):
                        for m in range(2):
                            row = slice(A_DIM * m, A_DIM * m + A_DIM)
                            pe.matmul(ps[:, 2 * (i % 2) + m, n * a:n * a + n], a_[row, h, qs], b_[row, h, 0:n],
                                      start=(part == 0), stop=False)
                    for m in range(2):
                        mm = pe.matmul(ps[:, 2 * (i % 2) + m, n * a + P * J:n * a + n], ident_r[:], mask_ts[:],
                                       start=False, stop=True)
                mm.then_inc(scores_done, 1)

            def turn_diff(i):
                J, heads = steps[i]
                pe.wait_ge(diff_ready, i + 1)
                if i < 2:
                    pe.wait_ge(v_ready, T + i + 1)
                else:
                    pe.wait_ge(pt_ready, i - 1)
                for k in range(len(heads) * (J + 1)):
                    mm = pe.transpose(ps[:, 4 + i % 2, P * k:P * k + P], pdiff[:, i % 2, P * k:P * k + P], ident[:])
                mm.then_inc(pt_done, 1)

            def values(i):
                J, heads = steps[i]
                pe.wait_ge(pt_ready, i + 1)
                if i == 0:
                    pe.wait_ge(v_ready, 2 * T)
                if heads[0] % 4 == 0 and J < T - 1:
                    pe.wait_ge(o_copied, 2 * (T - 1 - J) - 1 + heads[0] // 4)
                for a, h in enumerate(heads):
                    out_ = ps[:, 6 + h // 4, P * (h % 4):P * (h % 4) + P]
                    hs = slice(P * h, P * h + P)
                    for k in range(J + 1):
                        c = P * (a * (J + 1) + k)
                        mm = three(out_, pt_hi[:, i % 2, c:c + P], pt_lo[:, i % 2, c:c + P], v_hi[:, k, hs], v_lo[:, k, hs],
                                   k == 0, k == J)
                mm.then_inc(o_done, 1)

            def first_scores():
                scores(0)
                scores(1)

            between = [lambda: rope_turn(G_K2 - 1), lambda: rope_turn(G_K2), lambda: rope_turn(G_K2 + 1), first_scores]
            for n in range(4):
                group(U_K2 + 2 * n, n % 2, acts, False,
                      bank_wait=lambda b: pe.wait_ge(qk_ready, 4 * n + b + 1), between=between[n])

            for i in range(len(steps) + 2):
                if 1 <= i <= len(steps):
                    turn_diff(i - 1)
                if i + 2 < len(steps):
                    scores(i + 2)
                if i >= 2:
                    values(i - 2)
            turn_then_moving(TURN_YA, o_nat, U_OUT2, (q_hi, q_lo), 0)
            group(U_OUT2 + 2, 1, (q_hi, q_lo), False, hook=lambda: turn_two(TURN_X3))
            mlp(1, TURN_X3, U_UP2, U_DOWN2, None)


INPUTS = ("x", "positions", "norm_g", "a_w_in", "a_b_gates", "a_g_head", "a_w_out", "kv_norm_g", "w_kv",
          "b_w_q", "b_lam", "b_g_head", "b_w_out", "mlp_w_up", "mlp_w_down")


def kernel(**inputs):
    import concourse.bacc as bacc
    from concourse.bass_utils import run_bass_kernel_spmd

    nc = bacc.Bacc("TRN2", target_bir_lowering=False, num_devices=1)
    arrays = {f"in_{name}": np.ascontiguousarray(inputs[name]) for name in INPUTS}
    freq = 1.0 / (np.float32(10000.0) ** (np.arange(0, A_DIM, 2, dtype=np.float32) / np.float32(A_DIM)))
    arrays["inv_freq"] = freq.astype(np.float32).reshape(1, HALF)
    args = [nc.dram_tensor(n, a.shape, mybir.dt.from_np(a.dtype), kind="ExternalInput").ap() for n, a in arrays.items()]
    out = nc.dram_tensor("out", (1, SEQ, D_MODEL), F32, kind="ExternalOutput").ap()
    trunk(nc, *args, out)
    result = run_bass_kernel_spmd(nc, [arrays], core_ids=[0])
    return result.results[0]["out"]
```
